# Optimizing a Trainium2 kernel written in Bass

```python
import jax, jax.numpy as jnp
from jax import lax
import numpy as np
import math

D_MODEL = 1024
BATCH = 1
SEQ = 512
DEPTH = 2

CTX_LEN = 256
GRID_W = 64
HEAD_DIM = 64
N_HEADS_A = 8
N_KV_A = 2
N_HEADS_B = 8
N_KV_B = 2
WINDOW = 128
BLOCK = 128
D_FF = -(-8 * D_MODEL // (3 * 256)) * 256
ROPE_THETA = 10000.0
NORM_EPS = 1e-6
NEG_INF = -1e30
Q_A = N_HEADS_A * HEAD_DIM
KV_A = N_KV_A * HEAD_DIM
Q_B = N_HEADS_B * HEAD_DIM
KV_B = N_KV_B * HEAD_DIM
IN_SIZES = (Q_A, KV_A, KV_A, Q_B, KV_B, KV_B, D_MODEL, D_MODEL)
IN_COLS = Q_A + 2 * KV_A + Q_B + 2 * KV_B + 2 * D_MODEL


def rms_norm(x, g):
    xf = x.astype(jnp.float32)
    y = xf * lax.rsqrt(jnp.mean(xf * xf, axis=-1, keepdims=True) + NORM_EPS)
    return (y * g.astype(jnp.float32)).astype(x.dtype)

def modulate(h, shift, scale):
    return h * (1 + scale) + shift

def axial_rope_tables(n_tokens):
    rows = n_tokens // GRID_W
    row = jnp.repeat(jnp.arange(rows, dtype=jnp.float32), GRID_W)
    col = jnp.tile(jnp.arange(GRID_W, dtype=jnp.float32), rows)
    axis_dims = HEAD_DIM // 2
    inv = ROPE_THETA ** (-jnp.arange(0, axis_dims, 2, dtype=jnp.float32) / axis_dims)
    ang = jnp.stack([row[:, None] * inv, col[:, None] * inv], axis=1)
    return jnp.cos(ang), jnp.sin(ang)

def apply_rope(x, cos, sin):
    xr = x.astype(jnp.float32).reshape(x.shape[:-1] + (2, 2, HEAD_DIM // 4))
    x1, x2 = xr[..., 0, :], xr[..., 1, :]
    cs, sn = cos[:, None], sin[:, None]
    out = jnp.stack([x1 * cs - x2 * sn, x2 * cs + x1 * sn], axis=-2)
    return out.reshape(x.shape).astype(x.dtype)

def split_in_proj(z):
    pts = np.cumsum(IN_SIZES)[:-1].tolist()
    qa, ka, va, qb, kb, vb, ga, gb = jnp.split(z, pts, axis=-1)
    lead = z.shape[:-1]
    heads = lambda t, n: t.reshape(lead + (n, HEAD_DIM))
    return (heads(qa, N_HEADS_A), heads(ka, N_KV_A), heads(va, N_KV_A),
            heads(qb, N_HEADS_B), heads(kb, N_KV_B), heads(vb, N_KV_B), ga, gb)

def softmax_with_sink(s, sink_hg):
    sk = jnp.broadcast_to(sink_hg.astype(jnp.float32)[:, :, None, None], s.shape[:-1] + (1,))
    p = jax.nn.softmax(jnp.concatenate([s, sk], axis=-1), axis=-1)
    return p[..., :-1]

def window_attention_latent(q, k, v, kc, vc, sink):
    B, S = q.shape[:2]
    C = kc.shape[1]
    nb = S // BLOCK
    G = N_HEADS_A // N_KV_A
    scale = HEAD_DIM ** -0.5
    qb = q.reshape(B, nb, BLOCK, N_KV_A, G, HEAD_DIM)
    pad = ((0, 0), (BLOCK, BLOCK), (0, 0), (0, 0))
    kp = jnp.pad(k, pad).reshape(B, nb + 2, BLOCK, N_KV_A, HEAD_DIM)
    vp = jnp.pad(v, pad).reshape(B, nb + 2, BLOCK, N_KV_A, HEAD_DIM)
    kw = jnp.concatenate([kp[:, :-2], kp[:, 1:-1], kp[:, 2:]], axis=2)
    vw = jnp.concatenate([vp[:, :-2], vp[:, 1:-1], vp[:, 2:]], axis=2)
    s_win = jnp.einsum('bnqhgd,bnkhd->bnhgqk', qb, kw).astype(jnp.float32) * scale
    qpos = jnp.arange(nb)[:, None] * BLOCK + jnp.arange(BLOCK)[None, :]
    kpos = jnp.arange(nb)[:, None] * BLOCK - BLOCK + jnp.arange(3 * BLOCK)[None, :]
    rel = kpos[:, None, :] - qpos[:, :, None]
    valid = (jnp.abs(rel) <= WINDOW) & (kpos[:, None, :] >= 0) & (kpos[:, None, :] < S)
    s_win = jnp.where(valid[None, :, None, None], s_win, NEG_INF)
    s_ctx = jnp.einsum('bnqhgd,bchd->bnhgqc', qb, kc).astype(jnp.float32) * scale
    p = softmax_with_sink(jnp.concatenate([s_win, s_ctx], axis=-1), sink.reshape(N_KV_A, G)).astype(v.dtype)
    out = (jnp.einsum('bnhgqk,bnkhd->bnqhgd', p[..., :3 * BLOCK], vw)
           + jnp.einsum('bnhgqc,bchd->bnqhgd', p[..., 3 * BLOCK:], vc))
    return out.reshape(B, S, Q_A)

def full_attention_latent(q, k, v, kc, vc):
    B, S = q.shape[:2]
    nb = S // BLOCK
    G = N_HEADS_B // N_KV_B
    scale = HEAD_DIM ** -0.5
    kall = jnp.concatenate([k, kc], axis=1)
    vall = jnp.concatenate([v, vc], axis=1)
    qb = q.reshape(B, nb, BLOCK, N_KV_B, G, HEAD_DIM).transpose(1, 0, 2, 3, 4, 5)

    def one_block(qblk):
        s = jnp.einsum('bqhgd,bkhd->bhgqk', qblk, kall).astype(jnp.float32) * scale
        p = jax.nn.softmax(s, axis=-1).astype(vall.dtype)
        return jnp.einsum('bhgqk,bkhd->bqhgd', p, vall)

    out = lax.map(one_block, qb)
    return out.transpose(1, 0, 2, 3, 4, 5).reshape(B, S, Q_B)

def context_attention(q, k, v, n_kv, sink):
    B, C, H, _ = q.shape
    G = H // n_kv
    qg = q.reshape(B, C, n_kv, G, HEAD_DIM)
    s = jnp.einsum('bqhgd,bkhd->bhgqk', qg, k).astype(jnp.float32) * (HEAD_DIM ** -0.5)
    if sink is None:
        p = jax.nn.softmax(s, axis=-1)
    else:
        p = softmax_with_sink(s, sink.reshape(n_kv, G))
    out = jnp.einsum('bhgqk,bkhd->bqhgd', p.astype(v.dtype), v)
    return out.reshape(B, C, H * HEAD_DIM)

def merge_branches(ya, yb, ga, gb, w_pa, w_pb, w_o):
    m = jax.nn.sigmoid(ga) * (ya @ w_pa) + jax.nn.sigmoid(gb) * (yb @ w_pb)
    return m @ w_o

def swiglu(h, w_gate, w_up, w_down):
    return (jax.nn.silu(h @ w_gate) * (h @ w_up)) @ w_down

def first_inputs(seed: int = 0) -> dict:
    key = jax.random.key(seed)
    ks = jax.random.split(key, 20)
    f32 = jnp.float32
    nrm = lambda k, shape, s: jax.random.normal(k, shape, f32) * s
    return {
        "x": nrm(ks[0], (BATCH, SEQ, D_MODEL), 1.0),
        "c": nrm(ks[1], (BATCH, D_MODEL), 1.0),
        "ctx": nrm(ks[2], (BATCH, CTX_LEN, D_MODEL), 1.0),
        "c_ctx": nrm(ks[3], (D_MODEL,), 1.0),
        "w_ada": nrm(ks[4], (DEPTH, D_MODEL, 6 * D_MODEL), 0.5 * D_MODEL ** -0.5),
        "b_ada": nrm(ks[5], (DEPTH, 6 * D_MODEL), 0.01),
        "norm1_g": 1.0 + nrm(ks[6], (DEPTH, D_MODEL), 0.02),
        "norm2_g": 1.0 + nrm(ks[7], (DEPTH, D_MODEL), 0.02),
        "w_in": nrm(ks[8], (DEPTH, D_MODEL, IN_COLS), D_MODEL ** -0.5),
        "q_norm_g": 1.0 + nrm(ks[9], (DEPTH, HEAD_DIM), 0.02),
        "k_norm_g": 1.0 + nrm(ks[10], (DEPTH, HEAD_DIM), 0.02),
        "sink_a": nrm(ks[11], (DEPTH, N_HEADS_A), 0.5),
        "w_proj_a": nrm(ks[12], (DEPTH, Q_A, D_MODEL), Q_A ** -0.5),
        "w_proj_b": nrm(ks[13], (DEPTH, Q_B, D_MODEL), Q_B ** -0.5),
        "w_out": nrm(ks[14], (DEPTH, D_MODEL, D_MODEL), D_MODEL ** -0.5),
        "w_ffn_gate": nrm(ks[15], (DEPTH, D_MODEL, D_FF), D_MODEL ** -0.5),
        "w_ffn_up": nrm(ks[16], (DEPTH, D_MODEL, D_FF), D_MODEL ** -0.5),
        "w_ffn_down": nrm(ks[17], (DEPTH, D_FF, D_MODEL), D_FF ** -0.5),
        "final_norm_g": 1.0 + nrm(ks[18], (D_MODEL,), 0.02),
    }

def first_block(x, c, ctx, c_ctx, w_ada, b_ada, norm1_g, norm2_g, w_in, q_norm_g, k_norm_g, sink_a,
              w_proj_a, w_proj_b, w_out, w_ffn_gate, w_ffn_up, w_ffn_down, final_norm_g):
    cos, sin = axial_rope_tables(x.shape[1])
    silu_c = jax.nn.silu(c)
    silu_cc = jax.nn.silu(c_ctx)
    xc = ctx
    for l in range(DEPTH):
        last = l == DEPTH - 1
        mod = silu_c @ w_ada[l] + b_ada[l]
        mod_c = silu_cc @ w_ada[l] + b_ada[l]
        sh1, sc1, gt1, sh2, sc2, gt2 = jnp.split(mod[:, None, :], 6, axis=-1)
        csh1, csc1, cgt1, csh2, csc2, cgt2 = jnp.split(mod_c, 6, axis=-1)

        h = modulate(rms_norm(x, norm1_g[l]), sh1, sc1)
        hc = modulate(rms_norm(xc, norm1_g[l]), csh1, csc1)
        qa, ka, va, qb, kb, vb, ga, gb = split_in_proj(h @ w_in[l])
        qac, kac, vac, qbc, kbc, vbc, gac, gbc = split_in_proj(hc @ w_in[l])
        qb = rms_norm(qb, q_norm_g[l])
        kb = rms_norm(kb, k_norm_g[l])
        kbc = rms_norm(kbc, k_norm_g[l])
        ya = window_attention_latent(apply_rope(qa, cos, sin), apply_rope(ka, cos, sin), va, kac, vac, sink_a[l])
        yb = full_attention_latent(apply_rope(qb, cos, sin), apply_rope(kb, cos, sin), vb, kbc, vbc)
        x = x + gt1 * merge_branches(ya, yb, ga, gb, w_proj_a[l], w_proj_b[l], w_out[l])

        h2 = modulate(rms_norm(x, norm2_g[l]), sh2, sc2)
        x = x + gt2 * swiglu(h2, w_ffn_gate[l], w_ffn_up[l], w_ffn_down[l])

        if not last:
            qbc = rms_norm(qbc, q_norm_g[l])
            yac = context_attention(qac, kac, vac, N_KV_A, sink_a[l])
            ybc = context_attention(qbc, kbc, vbc, N_KV_B, None)
            xc = xc + cgt1 * merge_branches(yac, ybc, gac, gbc, w_proj_a[l], w_proj_b[l], w_out[l])
            h2c = modulate(rms_norm(xc, norm2_g[l]), csh2, csc2)
            xc = xc + cgt2 * swiglu(h2c, w_ffn_gate[l], w_ffn_up[l], w_ffn_down[l])
    return rms_norm(x, final_norm_g)


DEPTH_2 = 1

N_HEADS = 8
N_KV_GROUPS = 2
GROUP_SIZE = N_HEADS // N_KV_GROUPS
NSA_WIDTH = N_HEADS * HEAD_DIM
KV_WIDTH = N_KV_GROUPS * HEAD_DIM
CMP_STRIDE = 16
CMP_BLOCK = 2 * CMP_STRIDE
CMP_HIDDEN = 256
SEL_BLOCK = 64
SEL_PER_CMP = SEL_BLOCK // CMP_STRIDE
N_SELECT = 16
WINDOW_2 = 512
Q_BLOCK = 128
LRU_WIDTH = 512
LRU_BLOCKS = 8
LRU_BLOCK_DIM = LRU_WIDTH // LRU_BLOCKS
CONV_WIDTH = 4
LRU_C = 8.0
N_BUCKETS = 32
MAX_DISTANCE = 128
N_BRANCHES = 2
EPS = 1e-6
NEG = -1e30
FORCE_SCORE = 1e9
IN_SIZES_2 = (NSA_WIDTH, 6 * KV_WIDTH, NSA_WIDTH, 3 * N_HEADS, LRU_WIDTH, LRU_WIDTH, N_BRANCHES * D_MODEL)
D_IN = NSA_WIDTH + 6 * KV_WIDTH + NSA_WIDTH + 3 * N_HEADS + LRU_WIDTH + LRU_WIDTH + N_BRANCHES * D_MODEL


def rms_norm_2(x, g):
    xf = x.astype(jnp.float32)
    y = xf * lax.rsqrt(jnp.mean(xf * xf, axis=-1, keepdims=True) + EPS)
    return (y * g.astype(jnp.float32)).astype(x.dtype)

def t5_bucket(dist):
    n = jnp.maximum(dist, 0)
    max_exact = N_BUCKETS // 2
    nf = jnp.maximum(n, 1).astype(jnp.float32)
    large = max_exact + (jnp.log(nf / max_exact) / math.log(MAX_DISTANCE / max_exact)
                         * (N_BUCKETS - max_exact)).astype(jnp.int32)
    large = jnp.minimum(large, N_BUCKETS - 1)
    return jnp.where(n < max_exact, n, large)

def masked_softmax(s, mask):
    s = jnp.where(mask, s.astype(jnp.float32), NEG)
    return jax.nn.softmax(s, axis=-1) * mask

def compress_blocks(kv, pe, w1, b1, w2):
    B, S, G, dh = kv.shape
    ch = kv.reshape(B, S // CMP_STRIDE, CMP_STRIDE, G, dh)
    blocks = jnp.concatenate([ch[:, :-1], ch[:, 1:]], axis=2)
    blocks = blocks + pe[None, None, :, None, :]
    nc = blocks.shape[1]
    flat = blocks.transpose(0, 1, 3, 2, 4).reshape(B, nc, G, CMP_BLOCK * dh)
    return jax.nn.silu(flat @ w1 + b1) @ w2

def second_inputs(seed: int = 0) -> dict:
    key = jax.random.key(seed)
    ks = jax.random.split(key, 24)
    nrm = lambda k, shape, s: jax.random.normal(k, shape, jnp.float32) * s
    u = jax.random.uniform(ks[17], (LRU_WIDTH,), jnp.float32, 0.9, 0.999)
    sig = u ** (1.0 / LRU_C)
    lru_lambda = jnp.log(sig) - jnp.log1p(-sig)
    return {
        "x": nrm(ks[0], (BATCH, SEQ, D_MODEL), 1.0),
        "norm_gain": 1.0 + nrm(ks[1], (D_MODEL,), 0.1),
        "w_in": nrm(ks[2], (D_MODEL, D_IN), D_MODEL ** -0.5),
        "q_norm_gain": 1.0 + nrm(ks[3], (HEAD_DIM,), 0.1),
        "k_norm_gain": 1.0 + nrm(ks[4], (3, HEAD_DIM), 0.1),
        "cmp_pe": nrm(ks[5], (2, CMP_BLOCK, HEAD_DIM), 0.5),
        "cmp_w1": nrm(ks[6], (2, CMP_BLOCK * HEAD_DIM, CMP_HIDDEN), (CMP_BLOCK * HEAD_DIM) ** -0.5),
        "cmp_b1": nrm(ks[7], (2, CMP_HIDDEN), 0.02),
        "cmp_w2": nrm(ks[8], (2, CMP_HIDDEN, HEAD_DIM), CMP_HIDDEN ** -0.5),
        "rel_bias": nrm(ks[9], (N_BUCKETS, N_HEADS), 0.5),
        "conv_w": nrm(ks[10], (CONV_WIDTH, LRU_WIDTH), CONV_WIDTH ** -0.5),
        "conv_b": nrm(ks[11], (LRU_WIDTH,), 0.02),
        "lru_wa": nrm(ks[12], (LRU_BLOCKS, LRU_BLOCK_DIM, LRU_BLOCK_DIM), LRU_BLOCK_DIM ** -0.5),
        "lru_ba": nrm(ks[13], (LRU_WIDTH,), 0.02),
        "lru_wx": nrm(ks[14], (LRU_BLOCKS, LRU_BLOCK_DIM, LRU_BLOCK_DIM), LRU_BLOCK_DIM ** -0.5),
        "lru_bx": nrm(ks[15], (LRU_WIDTH,), 0.02),
        "lru_lambda": lru_lambda,
        "w_proj_a": nrm(ks[18], (NSA_WIDTH, D_MODEL), NSA_WIDTH ** -0.5),
        "w_proj_b": nrm(ks[19], (LRU_WIDTH, D_MODEL), LRU_WIDTH ** -0.5),
        "w_out": nrm(ks[20], (D_MODEL, D_MODEL), D_MODEL ** -0.5),
    }

def nsa_mixer(q, k_cmp, v_cmp, k_slc, v_slc, k_win, v_win, br_gate, q_norm_gain, k_norm_gain,
              cmp_pe, cmp_w1, cmp_b1, cmp_w2, rel_bias):
    B, S, _ = q.shape
    G, R, dh = N_KV_GROUPS, GROUP_SIZE, HEAD_DIM
    nsb = S // SEL_BLOCK
    n_sel = min(N_SELECT, nsb)
    scale = dh ** -0.5

    q = (rms_norm_2(q.reshape(B, S, G, R, dh), q_norm_gain) * scale).transpose(0, 2, 3, 1, 4)
    kc = rms_norm_2(compress_blocks(k_cmp, cmp_pe[0], cmp_w1[0], cmp_b1[0], cmp_w2[0]), k_norm_gain[0])
    vc = compress_blocks(v_cmp, cmp_pe[1], cmp_w1[1], cmp_b1[1], cmp_w2[1])
    kc = kc.transpose(0, 2, 1, 3)
    vc = vc.transpose(0, 2, 1, 3)
    nc = kc.shape[2]
    k_blocks = rms_norm_2(k_slc, k_norm_gain[1]).transpose(0, 2, 1, 3).reshape(B, G, nsb, SEL_BLOCK, dh)
    v_blocks = v_slc.transpose(0, 2, 1, 3).reshape(B, G, nsb, SEL_BLOCK, dh)
    pad_w = ((0, 0), (0, 0), (WINDOW_2, 0), (0, 0))
    k_wp = jnp.pad(rms_norm_2(k_win, k_norm_gain[2]).transpose(0, 2, 1, 3), pad_w)
    v_wp = jnp.pad(v_win.transpose(0, 2, 1, 3), pad_w)

    bias_gr = rel_bias.reshape(N_BUCKETS, G, R)
    def shared_bias(dist):
        return rel_bias[t5_bucket(dist)].transpose(2, 0, 1).reshape(G, R, *dist.shape)
    def group_bias(dist):
        b = jax.vmap(lambda tab, bk: tab[bk], in_axes=(1, 1), out_axes=1)(bias_gr, t5_bucket(dist))
        return jnp.moveaxis(b, -1, 2)

    c_end = jnp.arange(nc, dtype=jnp.int32) * CMP_STRIDE + CMP_BLOCK - 1
    blk = jnp.arange(nsb, dtype=jnp.int32)
    bi = jnp.arange(B)[:, None, None, None]
    gi = jnp.arange(G)[None, :, None, None]
    right_pad = SEL_PER_CMP * nsb + SEL_PER_CMP - 1 - nc

    def block_fn(q0):
        qc = lax.dynamic_slice_in_dim(q, q0, Q_BLOCK, axis=3)
        t = q0 + jnp.arange(Q_BLOCK, dtype=jnp.int32)
        dist = t[:, None] - c_end[None, :]
        s = jnp.einsum('bgrqd,bgcd->bgrqc', qc, kc) + shared_bias(dist)
        p_cmp = masked_softmax(s, dist >= 0)
        o_cmp = jnp.einsum('bgrqc,bgcd->bgrqd', p_cmp.astype(vc.dtype), vc)
        imp = jnp.pad(p_cmp.sum(axis=2), ((0, 0), (0, 0), (0, 0), (1, right_pad)))
        imp_blk = (imp[..., :SEL_PER_CMP * nsb].reshape(B, G, Q_BLOCK, nsb, SEL_PER_CMP).sum(-1)
                   + imp[..., SEL_PER_CMP:SEL_PER_CMP * nsb + SEL_PER_CMP:SEL_PER_CMP])
        cur = (t // SEL_BLOCK)[:, None]
        valid = blk[None, :] <= cur
        force = (blk[None, :] == 0) | (blk[None, :] == cur) | (blk[None, :] == cur - 1)
        score = jnp.where(valid, jnp.where(force, FORCE_SCORE, imp_blk), -1.0)
        _, idx = lax.top_k(score, n_sel)
        kb = k_blocks[bi, gi, idx].reshape(B, G, Q_BLOCK, n_sel * SEL_BLOCK, dh)
        vb = v_blocks[bi, gi, idx].reshape(B, G, Q_BLOCK, n_sel * SEL_BLOCK, dh)
        pos = (idx[..., None] * SEL_BLOCK + jnp.arange(SEL_BLOCK, dtype=jnp.int32)).reshape(B, G, Q_BLOCK, -1)
        dist = t[None, None, :, None] - pos
        s = jnp.einsum('bgrqd,bgqkd->bgrqk', qc, kb) + group_bias(dist)
        p = masked_softmax(s, (dist >= 0)[:, :, None])
        o_slc = jnp.einsum('bgrqk,bgqkd->bgrqd', p.astype(vb.dtype), vb)
        kw = lax.dynamic_slice_in_dim(k_wp, q0, WINDOW_2 + Q_BLOCK, axis=2)
        vw = lax.dynamic_slice_in_dim(v_wp, q0, WINDOW_2 + Q_BLOCK, axis=2)
        pos = q0 - WINDOW_2 + jnp.arange(WINDOW_2 + Q_BLOCK, dtype=jnp.int32)
        dist = t[:, None] - pos[None, :]
        mask = (dist >= 0) & (dist < WINDOW_2) & (pos[None, :] >= 0)
        s = jnp.einsum('bgrqd,bgkd->bgrqk', qc, kw) + shared_bias(dist)
        p = masked_softmax(s, mask)
        o_win = jnp.einsum('bgrqk,bgkd->bgrqd', p.astype(vw.dtype), vw)
        return o_cmp, o_slc, o_win

    starts = jnp.arange(0, S, Q_BLOCK, dtype=jnp.int32)
    outs = lax.map(block_fn, starts)
    o = jnp.stack([ob.transpose(1, 0, 4, 2, 3, 5).reshape(B, S, N_HEADS, dh) for ob in outs], axis=2)
    g = jax.nn.sigmoid(br_gate.reshape(B, S, 3, N_HEADS, 1))
    return (g * o).sum(axis=2).reshape(B, S, NSA_WIDTH)

def rglru_mixer(u, conv_w, conv_b, lru_wa, lru_ba, lru_wx, lru_bx, lru_lambda):
    B, S, W = u.shape
    up = jnp.pad(u, ((0, 0), (CONV_WIDTH - 1, 0), (0, 0)))
    uc = conv_b + sum(up[:, k:k + S] * conv_w[k] for k in range(CONV_WIDTH))
    ub = uc.reshape(B, S, LRU_BLOCKS, LRU_BLOCK_DIM)
    r = jax.nn.sigmoid(jnp.einsum('bsnd,nde->bsne', ub, lru_wa).reshape(B, S, W) + lru_ba)
    i = jax.nn.sigmoid(jnp.einsum('bsnd,nde->bsne', ub, lru_wx).reshape(B, S, W) + lru_bx)
    log_a = (-LRU_C * r.astype(jnp.float32)) * jax.nn.softplus(-lru_lambda.astype(jnp.float32))
    a = jnp.exp(log_a)
    b = jnp.sqrt(-jnp.expm1(2.0 * log_a)) * (i * uc).astype(jnp.float32)
    def comb(left, right):
        a1, b1 = left
        a2, b2 = right
        return a1 * a2, a2 * b1 + b2
    _, h = lax.associative_scan(comb, (a, b), axis=1)
    return h.astype(u.dtype)

def second_block(x, norm_gain, w_in, q_norm_gain, k_norm_gain, cmp_pe, cmp_w1, cmp_b1, cmp_w2, rel_bias,
              conv_w, conv_b, lru_wa, lru_ba, lru_wx, lru_bx, lru_lambda, w_proj_a, w_proj_b, w_out):
    B, S, _ = x.shape
    split_idx = np.cumsum(IN_SIZES_2)[:-1].tolist()
    for _layer in range(DEPTH_2):
        h = rms_norm_2(x, norm_gain)
        proj = h @ w_in
        q, kv_all, g_nsa, br_gate, u_lru, g_lru, merge_g = jnp.split(proj, split_idx, axis=-1)
        kv_all = kv_all.reshape(B, S, 6, N_KV_GROUPS, HEAD_DIM)
        y_a = nsa_mixer(q, kv_all[:, :, 0], kv_all[:, :, 1], kv_all[:, :, 2], kv_all[:, :, 3],
                        kv_all[:, :, 4], kv_all[:, :, 5], br_gate, q_norm_gain, k_norm_gain,
                        cmp_pe, cmp_w1, cmp_b1, cmp_w2, rel_bias)
        y_a = (y_a * jax.nn.silu(g_nsa)) @ w_proj_a
        y_b = rglru_mixer(u_lru, conv_w, conv_b, lru_wa, lru_ba, lru_wx, lru_bx, lru_lambda)
        y_b = (y_b * jax.nn.silu(g_lru)) @ w_proj_b
        gate_a, gate_b = jnp.split(merge_g, N_BRANCHES, axis=-1)
        m = jax.nn.sigmoid(gate_a) * y_a + jax.nn.sigmoid(gate_b) * y_b
        x = x + m @ w_out
    return x


def setup_inputs(seed=0):
    out = dict(first_inputs(seed))
    for name, value in second_inputs(seed + 1).items():
        if name != "x":
            out[name + "_2"] = value
    return out


def reference(
    x, c, ctx, c_ctx, w_ada, b_ada, norm1_g, norm2_g, w_in, q_norm_g, k_norm_g, sink_a,
    w_proj_a, w_proj_b, w_out, w_ffn_gate, w_ffn_up, w_ffn_down, final_norm_g, norm_gain_2,
    w_in_2, q_norm_gain_2, k_norm_gain_2, cmp_pe_2, cmp_w1_2, cmp_b1_2, cmp_w2_2, rel_bias_2,
    conv_w_2, conv_b_2, lru_wa_2, lru_ba_2, lru_wx_2, lru_bx_2, lru_lambda_2, w_proj_a_2,
    w_proj_b_2, w_out_2,
):
    x = first_block(
        x, c, ctx, c_ctx, w_ada, b_ada, norm1_g, norm2_g, w_in, q_norm_g, k_norm_g, sink_a,
        w_proj_a, w_proj_b, w_out, w_ffn_gate, w_ffn_up, w_ffn_down, final_norm_g,
    )
    return second_block(
        x, norm_gain_2, w_in_2, q_norm_gain_2, k_norm_gain_2, cmp_pe_2, cmp_w1_2, cmp_b1_2,
        cmp_w2_2, rel_bias_2, conv_w_2, conv_b_2, lru_wa_2, lru_ba_2, lru_wx_2, lru_bx_2,
        lru_lambda_2, w_proj_a_2, w_proj_b_2, w_out_2,
    )


_drawn_inputs = setup_inputs


def setup_inputs(seed=0):
    import zlib

    import numpy as np

    out = dict(_drawn_inputs(seed))
    spreads = {}
    factors = {'b_ada': 4.173,
     'norm1_g': 8.0,
     'norm2_g': 6.306,
     'q_norm_g': 8.0,
     'k_norm_g': 8.0,
     'sink_a': 8.0,
     'final_norm_g': 2.805,
     'q_norm_gain_2': 8.0,
     'k_norm_gain_2': 8.0,
     'cmp_b1_2': 36.214,
     'rel_bias_2': 16.525,
     'lru_ba_2': 64.0,
     'lru_bx_2': 64.0,
     'conv_b_2': 5.108}
    for name, (base, spread) in spreads.items():
        noise = np.random.default_rng([zlib.crc32(name.encode()), seed]).standard_normal(out[name].shape)
        drawn = base * np.exp(spread * noise) if base else spread * noise
        out[name] = __import__('jax').numpy.asarray(drawn.astype(out[name].dtype))
    for name, factor in factors.items():
        out[name] = (out[name] * factor).astype(out[name].dtype)
    return out
```

```python
from contextlib import ExitStack

import numpy as np

import concourse.bass as bass
from concourse import mybir

F32 = mybir.dt.float32
F32R = mybir.dt.float32r
ALU = mybir.AluOpType
ACT = mybir.ActivationFunctionType
AX_X = mybir.AxisListType.X

P = 128
D = 1024
CH = D // P
SEQ, CTX = 512, 256
TOK = SEQ + CTX
LAT = (0, SEQ)
CON = (SEQ, CTX)
HD = 64
PAIRS = 4
D_FF = 2816
EPS = 1e-6
NEG = -1e30
DEPTH = 2
RV_LEN = 1152
B_REL, B_HOT, B_W2, B_B1 = 1408, 2432, 3584, 4608
B_ALL = B_B1 + 512
LRU_C = 8.0
W_LEN = 912
UNIT = 1024

N_ADA, N_QKV, N_GATE, N_MERGE, N_OUT = 48, 12, 16, 8, 8
FF_PARTS = (8, 8, 6)
PER_LAYER = N_ADA + N_QKV + N_GATE + N_MERGE + N_OUT + sum(2 * f + CH for f in FF_PARTS)
N_IN2 = 6 + 4 + 1 + 4 + 4 + 4 + 16
N_CMP = 8
N_UNITS = DEPTH * PER_LAYER + N_IN2 + N_CMP + 1 + N_MERGE + N_OUT

COLS = {}


def _cols(**sizes):
    at = 0
    for name, n in sizes.items():
        COLS[name] = (at, n)
        at += n
    COLS["all"] = (0, at)


_cols(ident=128, ones=128, bones=128, sel=2, eps=1, c=16, b_ada=2 * 96, g1=2 * 16, g2=2 * 16, gf=8,
      qg=2, kg=2, sink=16, ng2=8, qg2=1, kg2=3, pe=32, convw=16, convb=4, ba=4, bx=4, lam=4)


SLOT = {0: 0, 1: 1, 4: 2, 5: 3, 2: 4, 3: 5}


def build_program(nc, ins, out):
    stream, xin, cst, big = ins["stream"], ins["x"], ins["cst"], ins["big"]

    with ExitStack() as ctx:
        def sb(name, shape, dt=F32, stack=ctx):
            return stack.enter_context(nc.sbuf_tensor(name, shape, dt))

        def sem(name):
            return ctx.enter_context(nc.semaphore(name))

        def region(name, nbytes, *views):
            got = {}
            for view in views:
                with ExitStack() as s:
                    for n, shape, dt in view:
                        got[n] = sb(n, shape, dt, s)
            sb(name, [P, nbytes // 4])
            return got

        def dram(name, shape):
            return nc.dram_tensor(name, shape, F32, kind="Internal").ap()

        raw = sb("w_raw", [P, 2, UNIT])
        w_hi = sb("w_hi", [P, 2, UNIT], F32R)
        w_lo = sb("w_lo", [P, 2, UNIT], F32R)
        vec = sb("vec", [P, COLS["all"][1]])
        r_t = region("region_tables", 8 * SEQ, [("cosT", [P, SEQ], F32), ("sinT", [P, SEQ], F32)],
                     [("cmp_raw", [P, 2, SEQ], F32)])
        cosT, sinT = r_t["cosT"], r_t["sinT"]
        band = sb("band", [P, 3 * P], F32R)
        identR = sb("identR", [P, P], F32R)
        mod = sb("mod", [P, 6 * CH, 2])
        aff = sb("aff", [P, 2, CH, 2])
        nsink = sb("nsink", [P, 16])
        small = sb("small", [P, 16])
        cs = sb("cs", [P, 2, 16])
        r_x = region("region_x", 4 * CH * TOK,
                     [("x", [P, CH, TOK], F32)],
                     [("q_hi_now", [P, 2, TOK], F32R), ("q_lo_now", [P, 2, TOK], F32R),
                      ("pc_hi", [P, 2, 2, CTX], F32R), ("pc_lo", [P, 2, 2, CTX], F32R)],
                     [("q2_hi", [P, 2, SEQ], F32R), ("q2_lo", [P, 2, SEQ], F32R), ("bias", [P, 2, 2, W_LEN], F32)])
        r_h = region("region_h", 8 * CH * TOK,
                     [("h_hi", [P, CH, TOK], F32R), ("h_lo", [P, CH, TOK], F32R)],
                     [("p_hi", [P, 2, 6, SEQ], F32R), ("p_lo", [P, 2, 6, SEQ], F32R)],
                     [("rel_cols", [P, 8 * P], F32), ("onehot", [P, RV_LEN], F32), ("rv", [P, 2, RV_LEN], F32)],
                     [("r_hi", [P, 2, 16, P], F32R), ("r_lo", [P, 2, 16, P], F32R)],
                     [("s_hi", [P, 2, 4, SEQ], F32R), ("s_lo", [P, 2, 4, SEQ], F32R),
                      ("sc_hi", [P, 2, SEQ], F32R), ("sc_lo", [P, 2, SEQ], F32R)])
        r_q1 = region("region_q_hi", 4 * CH * TOK, [("q_hi", [P, CH, TOK], F32R)],
                      [("q_hi_half", [P, 4, TOK], F32R), ("br", [P, SEQ], F32), ("br_cols", [P, 4, 32], F32),
                       ("kc_hi", [P, 2, 32], F32R), ("kc_lo", [P, 2, 32], F32R),
                       ("vc_hi", [P, 192], F32R), ("vc_lo", [P, 192], F32R), ("cmp_s", [P, 4, 32], F32),
                       ("cmp_n", [P, 4, 4], F32), ("kcf", [P, 5, 32], F32)])
        r_q2 = region("region_q_lo", 4 * CH * TOK, [("q_lo", [P, CH, TOK], F32R)],
                      [("q_lo_half", [P, 4, TOK], F32R), ("w2", [P, 2, 2, 2, P], F32), ("b1_rows", [P, 2, 256], F32),
                       ("hid", [P, 2, 256], F32), ("hid_t", [P, 2, 2, P], F32)])
        q_hi, q_lo = r_q1["q_hi"], r_q2["q_lo"]
        r_kv = region("region_kv", 4 * (8 * TOK + 4 * 6 * 192),
                      [("k_hi", [P, 4, TOK], F32R), ("k_lo", [P, 4, TOK], F32R),
                       ("v_hi", [P, 2, 6, 192], F32R), ("v_lo", [P, 2, 6, 192], F32R)],
                      [("cl", [P, CH, P], F32R), ("ada_row", [P, 2, 512], F32)],
                      [("sq", [P, 2, SEQ], F32), ("acc", [P, SEQ], F32), ("y0", [P, SEQ], F32),
                       ("nt", [P, SEQ], F32), ("tx", [P, 2, SEQ], F32), ("hf", [P, 2, SEQ], F32)],
                      [("m1", [P, 2, TOK], F32), ("m2", [P, 2, TOK], F32)],
                      [("su", [P, 2, TOK], F32), ("ff", [P, 2, TOK], F32)],
                      [("u", [P, 4, SEQ], F32), ("gl", [P, 4, SEQ], F32), ("uc", [P, SEQ], F32), ("uc_hi", [P, SEQ], F32R),
                       ("uc_lo", [P, SEQ], F32R), ("rg", [P, SEQ], F32), ("ig", [P, SEQ], F32), ("a", [P, SEQ], F32),
                       ("th", [P, SEQ], F32), ("aa", [P, SEQ], F32), ("hh", [P, SEQ], F32), ("sp", [P, 8, 4], F32)])
        r_s = region("region_scratch", 4 * 4 * TOK,
                     [("zt", [P, 2, TOK], F32), ("zq", [P, TOK], F32), ("zy", [P, TOK], F32)],
                     [("sg", [P, 4, TOK], F32)],
                     [("pr", [P, 3, TOK], F32)],
                     [("pr2", [P, 3, SEQ], F32), ("gn", [P, 2, SEQ], F32), ("yf", [P, SEQ], F32)],
                     [("kk", [P, 4, SEQ], F32), ("rf", [P, 2, 16, 31], F32)],
                     [("ga", [P, 2, TOK], F32), ("gb", [P, 2, TOK], F32)])
        x, h_hi, h_lo = r_x["x"], r_h["h_hi"], r_h["h_lo"]
        ps = ctx.enter_context(nc.psum_tensor("ps", [P, 8, 512], F32))
        psf = ps[:, :, :].rearrange("p b n -> p (b n)")
        gates = dram("gates", (2 * CH + 12, P, TOK))
        x_keep = dram("x_keep", (P, CH, TOK))

        def col(name, a=0, n=1):
            at = COLS[name][0] + a
            return vec[:, at:at + n]

        def col_at(name, a):
            return vec[:, bass.ds(COLS[name][0] + a, 1)]

        ident, ones, bones, sel = col("ident", 0, P), col("ones", 0, P), col("bones", 0, P), col("sel", 0, 2)

        raw_loaded = [sem("raw_loaded0"), sem("raw_loaded1")]
        hi_ready, lo_ready, unit_done = sem("hi_ready"), sem("lo_ready"), sem("unit_done")
        const_loaded = sem("const_loaded")

        def split_hi(act, u, i=None, per=0):
            slot = u % 2
            act.wait_ge(raw_loaded[slot], 16 * (u // 2 + 1) if i is None else i * (8 * per) + 16 * (u // 2 + 1))
            if i is not None or u >= 2:
                act.wait_ge(unit_done, u if i is None else i * per + u)
            nc.scalar.activation(w_hi[:, slot, :], raw[:, slot, :], ACT.Copy).then_inc(hi_ready, 1)

        def split_lo(dve, u, i=None, per=0):
            slot = u % 2
            dve.wait_ge(hi_ready, u + 1 if i is None else i * per + (u + 1))
            nc.vector.tensor_tensor(w_lo[:, slot, :], raw[:, slot, :], w_hi[:, slot, :].bitcast(F32),
                                    ALU.subtract).then_inc(lo_ready, 1)

        def unit_at(u, i, per):
            return u if i is None else i * per + u

        def three(out_ap, lh, ll, rh, rl, start, stop):
            nc.tensor.matmul(out_ap, lh, rh, start=start, stop=False)
            nc.tensor.matmul(out_ap, lh, rl, start=False, stop=False)
            return nc.tensor.matmul(out_ap, ll, rh, start=False, stop=stop)

        def linear(slot_bank, u, groups, act_hi, act_lo, chunks, first=0, act_first=0):
            s = u % 2
            for s0, n in groups:
                o = psf[:, slot_bank * 512 + s0:slot_bank * 512 + s0 + n]
                for c in range(chunks):
                    w = slice((first + c) * P, (first + c + 1) * P)
                    mm = three(o, w_hi[:, s, w], w_lo[:, s, w], act_hi[:, act_first + c, s0:s0 + n],
                               act_lo[:, act_first + c, s0:s0 + n], c == 0, c == chunks - 1)
            return mm

        phases = []

        class Signal:

            def __init__(self, s, base):
                self.sem, self.base = s, base

        kept, from_one = {}, []

        def signals(kind, by_dma=False, **totals):
            got = []
            for name, total in totals.items():
                key = kind + "_" + name
                if key not in kept:
                    kept[key] = [sem(key), 0 if by_dma else 1]
                    if not by_dma:
                        from_one.append(kept[key][0])
                got.append(Signal(*kept[key]))
                kept[key][1] += total
            return got

        def phase(done, **engines):
            phases.append((engines, [(s.sem, s.base + v) if isinstance(s, Signal) else (s, v) for s, v in done]))

        def loop(eng, a, b):
            return eng.Fori(a, b)

        cond_ready, c_sig, c_sil, c_hi, c_lo = (sem("cond_ready"), sem("c_sig"), sem("c_sil"), sem("c_hi"), sem("c_lo"))
        cl, ada_row = r_kv["cl"], r_kv["ada_row"]

        def consts_pool(pool):
            pool.dma_start(vec[:, :], cst).then_inc(const_loaded, 16)
            pool.dma_start(cosT[:, :], big[:, 0:512]).then_inc(const_loaded, 16)
            pool.dma_start(sinT[:, :], big[:, 512:1024]).then_inc(const_loaded, 16)
            pool.dma_start(x[:, :, :], xin).then_inc(const_loaded, 16)

        band_f = r_s["zq"]

        def consts_pool2(pool):
            pool.dma_start(band_f[:, 0:3 * P], big[:, 1024:1024 + 3 * P]).then_inc(const_loaded, 16)

        def consts_all_pool(pool):
            consts_pool(pool)
            consts_pool2(pool)

        def consts_act(act):
            act.wait_ge(const_loaded, 80)
            nc.scalar.activation(cs[:, 0, :], col("c", 0, 16), ACT.Sigmoid).then_inc(c_sig, 1)
            split_hi(act, 0)

        def consts_dve(dve):
            dve.wait_ge(const_loaded, 80)
            nc.vector.tensor_copy(band[:, :], band_f[:, 0:3 * P]).then_inc(cond_ready, 1)
            nc.vector.tensor_copy(identR[:, :], ident).then_inc(cond_ready, 1)
            nc.vector.tensor_scalar(nsink[:, :], col("sink", 0, 16), -1.0, None, ALU.mult).then_inc(cond_ready, 1)
            split_lo(dve, 0)
            dve.wait_ge(c_sig, 1)
            nc.vector.tensor_tensor(cs[:, 1, :], cs[:, 0, :], col("c", 0, 16), ALU.mult).then_inc(c_sil, 1)

        phase([(cond_ready, 3), (c_sil, 1), (lo_ready, 1)], pool=consts_all_pool, act=consts_act, dve=consts_dve)

        u0 = 0
        class Chain:

            def __init__(self, s):
                self.s, self.n, self.i, self.per, self.base = s, 0, None, 0, 0

            def link(self, eng, ins):
                ins.then_inc(self.s, 1)
                self.n += 1
                eng.wait_ge(self.s, self.n if self.i is None else self.i * self.per + self.n)

            @property
            def value(self):
                return self.n if self.i is None else self.i * self.per + self.n

            def enter(self, i, per):
                self.i, self.per, self.start = i, per, self.n

            def leave(self, times):
                assert self.n - self.start == self.per, (self.n - self.start, self.per)
                self.n = self.start + self.per * times
                self.i = None

        dve_own, act_own = Chain(sem("dve_own")), Chain(sem("act_own"))

        def ada(layer):
            nonlocal u0
            base = u0
            row_copied, col_summed, col_kept = signals("ada", row_copied=14, col_summed=14, col_kept=14)
            cl_zero, cl_hi_done, cl_done, aff_done = signals("ada", cl_zero=1, cl_hi=1, cl=1, affine=2)
            sil = cs[:, 1, :].rearrange("p (c v) -> p c v", v=2)

            def pe(e):
                e.wait_ge(cl_done.sem, cl_done.base + 1)
                e.sem_inc(row_copied.sem, 2)
                e.sem_inc(col_kept.sem, 2)
                with loop(e, 0, 6) as i:
                    for g in range(2):
                        for j in range(4):
                            u = base + 4 * g + j
                            e.wait_ge(lo_ready, unit_at(u + 1, i, 8))
                            if j == 0:
                                e.wait_ge(row_copied.sem, row_copied.base + i * 2 + g + 1)
                            for cc in range(2):
                                c = 2 * j + cc
                                for w in (w_hi, w_lo):
                                    mm = nc.tensor.matmul(ps[:, g, :], cl[:, c, :], w[:, u % 2, cc * 512:cc * 512 + 512],
                                                          start=(c == 0 and w is w_hi), stop=(c == 7 and w is w_lo))
                            mm.then_inc(unit_done, 1)
                        e.wait_ge(row_copied.sem, row_copied.base + i * 2 + g + 3)
                        e.wait_ge(col_kept.sem, col_kept.base + i * 2 + g + 1)
                        for m in range(4):
                            mm = nc.tensor.matmul(ps[:, 2 + g, 2 * m:2 * m + 2], ada_row[:, g, m * P:(m + 1) * P], sel,
                                                  start=True, stop=True)
                        mm.then_inc(col_summed.sem, 1)

            def act(e):
                e.wait_ge(cl_zero.sem, cl_zero.base + 1)
                nc.scalar.activation(cl[:, :, 0:2], sil, ACT.Copy).then_inc(cl_hi_done.sem, 1)
                e.sem_inc(col_summed.sem, 2)
                with loop(e, 0, 6) as i:
                    for g in range(2):
                        for j in range(4):
                            u = base + 4 * g + j
                            split_hi(e, u + 1, i, 8)
                            if j == 3:
                                e.wait_ge(unit_done, unit_at(u + 2, i, 8))
                                e.wait_ge(col_summed.sem, col_summed.base + i * 2 + g + 1)
                                nc.scalar.activation(ada_row[:, g, :], ps[:, g, :], ACT.Copy).then_inc(row_copied.sem, 1)

            def dve(e):
                nc.vector.memset(cl[:, :, :].bitcast(F32), 0.0).then_inc(cl_zero.sem, 1)
                e.wait_ge(cl_hi_done.sem, cl_hi_done.base + 1)
                nc.vector.tensor_tensor(cl[:, :, 2:4], sil, cl[:, :, 0:2].bitcast(F32), ALU.subtract).then_inc(cl_done.sem, 1)
                bias = col("b_ada", layer * 96, 96).rearrange("p (n v) -> p n v", v=2)
                with loop(e, 0, 6) as i:
                    for g in range(2):
                        for j in range(4):
                            u = base + 4 * g + j
                            split_lo(e, u + 1, i, 8)
                            if j == 3:
                                e.wait_ge(col_summed.sem, col_summed.base + i * 2 + g + 3)
                                n = i * 8 + 4 * g
                                nc.vector.tensor_tensor(mod[:, bass.ds(n, 4), :],
                                                        ps[:, 2 + g, 0:8].rearrange("p (m v) -> p m v", v=2),
                                                        bias[:, bass.ds(n, 4), :], ALU.add).then_inc(col_kept.sem, 1)
                e.wait_ge(col_kept.sem, col_kept.base + 14)
                for k, g in ((0, "g1"), (1, "g2")):
                    gain = col(g, layer * 16, 16).rearrange("p (n v) -> p n v", v=2)
                    at = (3 * k + 1) * CH
                    nc.vector.scalar_tensor_tensor(aff[:, k], mod[:, at:at + CH, :], 1.0, gain, ALU.add,
                                                   ALU.mult).then_inc(aff_done.sem, 1)

            u0 += N_ADA
            phase([(aff_done, 2), (unit_done, 1 + u0), (lo_ready, u0 + 1), (col_summed, 14), (row_copied, 14)],
                  pe=pe, act=act, dve=dve)

        def norm(name, groups, scale_of, shift_of, out_f32=False):
            sq, acc, y0, nt, tx, hf = (r_kv[n] for n in ("sq", "acc", "y0", "nt", "tx", "hf"))
            ng = len(groups)
            squared, summed, stat, rough, scaled, moved, high, low = signals(
                "norm", squared=8 * ng, summed=8 * ng + 2, stat=ng, rough=ng, scaled=8 * ng,
                moved=0 if out_f32 else 8 * ng, high=8 * ng, low=2 if out_f32 else 8 * ng + 2)

            def act(e):
                e.sem_inc(summed.sem, 2)
                for v, (s0, n) in enumerate(groups):
                    with loop(e, 0, 4) as i:
                        for j in range(2):
                            e.wait_ge(summed.sem, summed.base + i * 2 + (v * 8 + j + 1))
                            nc.scalar.activation(sq[:, j, 0:n], x[:, bass.ds(i * 2 + j, 1), s0:s0 + n].rearrange("p a n -> p (a n)"),
                                                 ACT.Square).then_inc(squared.sem, 1)
                    e.wait_ge(stat.sem, stat.base + v + 1)
                    if v:
                        e.wait_ge(scaled.sem, scaled.base + 8 * v)
                    act_own.link(e, nc.scalar.activation(y0[:, 0:n], ps[:, v, 0:n], ACT.Ln, scale=1.0 / D, bias=col("eps")))
                    nc.scalar.activation(y0[:, 0:n], y0[:, 0:n], ACT.Exp, scale=-0.5).then_inc(rough.sem, 1)
                    if v == 0:
                        e.sem_inc(low.sem, 2)
                    with loop(e, 0, 4) as i:
                        for j in range(2):
                            e.wait_ge(scaled.sem, scaled.base + i * 2 + (v * 8 + j + 1))
                            if not out_f32:
                                e.wait_ge(low.sem, low.base + i * 2 + (v * 8 + j + 1))
                                nc.scalar.activation(hf[:, j, 0:n], tx[:, j, 0:n], ACT.Identity,
                                                     scale=scale_of(i * 2 + j, v), bias=shift_of(i * 2 + j, v)).then_inc(moved.sem, 1)
                                e.wait_ge(moved.sem, moved.base + i * 2 + (v * 8 + j + 1))
                                nc.scalar.activation(h_hi[:, bass.ds(i * 2 + j, 1), s0:s0 + n].rearrange("p a n -> p (a n)"),
                                                     hf[:, j, 0:n], ACT.Copy).then_inc(high.sem, 1)
                            else:
                                nc.scalar.activation(x[:, bass.ds(i * 2 + j, 1), s0:s0 + n].rearrange("p a n -> p (a n)"),
                                                     tx[:, j, 0:n], ACT.Identity, scale=scale_of(i * 2 + j, v)).then_inc(high.sem, 1)

            def dve(e):
                for v, (s0, n) in enumerate(groups):
                    e.wait_ge(squared.sem, squared.base + 8 * v + 1)
                    if v:
                        e.wait_ge(stat.sem, stat.base + v)
                    nc.vector.tensor_copy(acc[:, 0:n], sq[:, 0, 0:n]).then_inc(summed.sem, 1)
                    for c in range(1, 8):
                        e.wait_ge(squared.sem, squared.base + 8 * v + c + 1)
                        e.wait_ge(summed.sem, summed.base + 8 * v + c + 2)
                        nc.vector.tensor_tensor(acc[:, 0:n], acc[:, 0:n], sq[:, c % 2, 0:n], ALU.add).then_inc(summed.sem, 1)
                    e.wait_ge(rough.sem, rough.base + v + 1)
                    newton(e, ps[:, v, 0:n], y0[:, 0:n], nt[:, 0:n], D)
                    with loop(e, 0, 4) as i:
                        for j in range(2):
                            nc.vector.tensor_tensor(tx[:, j, 0:n], x[:, bass.ds(i * 2 + j, 1), s0:s0 + n].rearrange("p a n -> p (a n)"),
                                                    y0[:, 0:n], ALU.mult).then_inc(scaled.sem, 1)
                        for j in range(2):
                            e.wait_ge(high.sem, high.base + i * 2 + (v * 8 + j + 1))
                            if not out_f32:
                                nc.vector.tensor_tensor(h_lo[:, bass.ds(i * 2 + j, 1), s0:s0 + n].rearrange("p a n -> p (a n)"),
                                                        hf[:, j, 0:n],
                                                        h_hi[:, bass.ds(i * 2 + j, 1), s0:s0 + n].bitcast(F32).rearrange("p a n -> p (a n)"),
                                                        ALU.subtract).then_inc(low.sem, 1)

            def pe(e):
                for v, (s0, n) in enumerate(groups):
                    e.wait_ge(summed.sem, summed.base + 8 * (v + 1) + 2)
                    nc.tensor.matmul(ps[:, v, 0:n], ones, acc[:, 0:n], start=True, stop=True).then_inc(stat.sem, 1)

            n = len(groups)
            done = [(high, 8 * n), (stat, n), (scaled, 8 * n), (summed, 8 * n + 2)]
            if not out_f32:
                done.append((low, 8 * n + 2))
            phase(done, act=act, dve=dve, pe=pe)

        def newton(e, sums, y, t, width):
            dve_own.link(e, nc.vector.tensor_tensor(t, y, y, ALU.mult))
            dve_own.link(e, nc.vector.scalar_tensor_tensor(t, sums, width * EPS, t, ALU.add, ALU.mult))
            dve_own.link(e, nc.vector.tensor_scalar(t, t, -0.5 / width, 1.5, ALU.mult, ALU.add))
            dve_own.link(e, nc.vector.tensor_tensor(y, y, t, ALU.mult))

        SWAP = [(p + 16) % 32 for p in range(32)]

        def project(tiles):
            nonlocal u0
            base = u0
            zt, zq, zy = r_s["zt"], r_s["zq"], r_s["zy"]
            k_hi, k_lo, v_hi, v_lo = (r_kv[n] for n in ("k_hi", "k_lo", "v_hi", "v_lo"))
            kinds = [t[0:2] for t in tiles]
            width = [t[2] for t in tiles]
            normed = [t[3] is not None for t in tiles]
            n_sq = np.cumsum([0] + [int(b) for b in normed]).tolist()
            n_st = np.cumsum([0] + [int(b or k == "v") for b, (k, _) in zip(normed, kinds)]).tolist()
            n_sh = np.cumsum([0] + [int(k in "qk") for k, _ in kinds]).tolist()
            n_hl = np.cumsum([0] + [int(k != "raw") for k, _ in kinds]).tolist()
            T = len(kinds)
            copied, squared, stat, rough, shaped, high, low, zeroed = signals(
                "qkv", copied=T, squared=n_sq[T], stat=n_st[T], rough=n_sq[T], shaped=n_sh[T], high=n_hl[T], low=n_hl[T], zeroed=10)

            def last_use(t):
                return max([s for s in range(t) if n_st[s + 1] > n_st[s]], default=None)

            def pe(e):
                def linear_tile(t):
                    u = base + t
                    e.wait_ge(lo_ready, u + 1)
                    if t >= 3:
                        e.wait_ge(copied.sem, copied.base + t - 2)
                        if normed[t - 3]:
                            e.wait_ge(squared.sem, squared.base + n_sq[t - 2])
                    gr = [LAT, CON] if width[t] == TOK else [LAT]
                    linear(2 * (t % 3), u, gr, h_hi, h_lo, CH).then_inc(unit_done, 1)

                def second(t):
                    k, j = kinds[t]
                    prev = last_use(t)
                    if k == "v":
                        e.wait_ge(copied.sem, copied.base + t + 1)
                        if prev is not None:
                            e.wait_ge(low.sem, low.base + n_hl[prev + 1])
                        for b in range(width[t] // P):
                            mm = nc.tensor.transpose(psf[:, 3072 + b * P:3072 + (b + 1) * P], zt[:, t % 2, b * P:(b + 1) * P], ident)
                        mm.then_inc(stat.sem, 1)
                    elif normed[t]:
                        e.wait_ge(squared.sem, squared.base + n_sq[t + 1])
                        if prev is not None:
                            e.wait_ge(low.sem, low.base + n_hl[prev + 1])
                        for s0, n in ([LAT, CON] if width[t] == TOK else [LAT]):
                            mm = nc.tensor.matmul(psf[:, 3072 + s0:3072 + s0 + n], bones, zq[:, s0:s0 + n], start=True, stop=True)
                        mm.then_inc(stat.sem, 1)

                for t in range(T + 1):
                    if t < T:
                        linear_tile(t)
                    if t >= 1:
                        second(t - 1)

            def act(e):
                for t in range(T + 1):
                    if t < T:
                        k, j = kinds[t]
                        split_hi(e, base + t + 1)
                        e.wait_ge(unit_done, 1 + base + t + 1)
                        w = width[t]
                        src = psf[:, 1024 * (t % 3):1024 * (t % 3) + w]
                        if k == "raw":
                            nc.scalar.activation(j, src, tiles[t][5]).then_inc(copied.sem, 1)
                        else:
                            if t >= 2:
                                e.wait_ge(low.sem, low.base + n_hl[t - 1])
                            nc.scalar.activation(zt[:, t % 2, 0:w], src, ACT.Copy, scale=tiles[t][5]).then_inc(copied.sem, 1)
                    if t >= 1:
                        second(e, t - 1)
                    if t < T and normed[t]:
                        e.wait_ge(low.sem, low.base + n_hl[t])
                        nc.scalar.activation(zq[:, 0:w], src, ACT.Square).then_inc(squared.sem, 1)

            def second(e, t):
                k, j = kinds[t]
                w = width[t]
                nb = w // P
                if k == "raw":
                    return
                if normed[t]:
                    e.wait_ge(stat.sem, stat.base + n_st[t + 1])
                    act_own.link(e, nc.scalar.activation(zy[:, 0:w], psf[:, 3072:3072 + w], ACT.Ln, scale=1.0 / HD, bias=col("eps")))
                    nc.scalar.activation(zy[:, 0:w], zy[:, 0:w], ACT.Exp, scale=-0.5).then_inc(rough.sem, 1)
                if k == "v":
                    e.wait_ge(stat.sem, stat.base + n_st[t + 1])
                    e.wait_ge(zeroed.sem, zeroed.base + 10)
                    for g in range(2):
                        ins = nc.scalar.activation(v_hi[:, j, 0:nb, 128 * g:128 * g + 64],
                                                   psf[:, 3072:3072 + w].rearrange("p (b n) -> p b n", b=nb)[:, :, 64 * g:64 * g + 64], ACT.Copy)
                        if g == 0:
                            act_own.link(e, ins)
                    ins.then_inc(high.sem, 1)
                    return
                e.wait_ge(shaped.sem, shaped.base + n_sh[t + 1])
                if k == "q":
                    nc.scalar.activation(q_hi[:, j, 0:w], zt[:, t % 2, 0:w], ACT.Copy).then_inc(high.sem, 1)
                else:
                    e.wait_ge(zeroed.sem, zeroed.base + 10)
                    act_own.link(e, nc.scalar.activation(k_hi[0:64, 2 * j, 0:w], zt[0:64, t % 2, 0:w], ACT.Copy))
                    nc.scalar.activation(k_hi[64:128, 2 * j + 1, 0:w], zt[64:128, t % 2, 0:w], ACT.Copy).then_inc(high.sem, 1)

            def dve(e):
                for k_part in (k_hi, k_lo):
                    for j in range(2):
                        nc.vector.memset(k_part[64:128, 2 * j, :].bitcast(F32), 0.0).then_inc(zeroed.sem, 1)
                        nc.vector.memset(k_part[0:64, 2 * j + 1, :].bitcast(F32), 0.0).then_inc(zeroed.sem, 1)
                nc.vector.memset(v_hi[:, :, :, 64:128].bitcast(F32), 0.0).then_inc(zeroed.sem, 1)
                nc.vector.memset(v_lo[:, :, :, 64:128].bitcast(F32), 0.0).then_inc(zeroed.sem, 1)
                for t in range(T + 1):
                    if t < T:
                        split_lo(e, base + t + 1)
                    if t >= 1:
                        shape(e, t - 1)

            def shape(e, t):
                k, j = kinds[t]
                w = width[t]
                z = zt[:, t % 2, :]
                nb = w // P
                if k == "raw":
                    return
                if k == "v":
                    e.wait_ge(high.sem, high.base + n_hl[t + 1])
                    for g in range(2):
                        ins = nc.vector.tensor_tensor(v_lo[:, j, 0:nb, 128 * g:128 * g + 64],
                                                      psf[:, 3072:3072 + w].rearrange("p (b n) -> p b n", b=nb)[:, :, 64 * g:64 * g + 64],
                                                      v_hi[:, j, 0:nb, 128 * g:128 * g + 64].bitcast(F32), ALU.subtract)
                        if g == 0:
                            dve_own.link(e, ins)
                    ins.then_inc(low.sem, 1)
                    return
                e.wait_ge(copied.sem, copied.base + t + 1)
                if normed[t]:
                    e.wait_ge(rough.sem, rough.base + n_sq[t + 1])
                    newton(e, psf[:, 3072:3072 + w], zy[:, 0:w], zq[:, 0:w], HD)
                    ins = nc.vector.scalar_tensor_tensor(z[:, 0:w], z[:, 0:w], tiles[t][3], zy[:, 0:w], ALU.mult, ALU.mult)
                    if tiles[t][4]:
                        dve_own.link(e, ins)
                    else:
                        ins.then_inc(shaped.sem, 1)
                if tiles[t][4]:
                    spin_heads(e, z)
                e.wait_ge(high.sem, high.base + n_hl[t + 1])
                if not tiles[t][4]:
                    e.wait_ge(shaped.sem, shaped.base + n_sh[t + 1])
                if k == "q":
                    nc.vector.tensor_tensor(q_lo[:, j, 0:w], z[:, 0:w], q_hi[:, j, 0:w].bitcast(F32), ALU.subtract).then_inc(low.sem, 1)
                else:
                    dve_own.link(e, nc.vector.tensor_tensor(k_lo[0:64, 2 * j, 0:w], z[0:64, 0:w],
                                                            k_hi[0:64, 2 * j, 0:w].bitcast(F32), ALU.subtract))
                    nc.vector.tensor_tensor(k_lo[64:128, 2 * j + 1, 0:w], z[64:128, 0:w],
                                            k_hi[64:128, 2 * j + 1, 0:w].bitcast(F32), ALU.subtract).then_inc(low.sem, 1)

            def spin_heads(e, z):
                spin = zy[:, 0:SEQ]
                dve_own.link(e, nc.vector.stream_shuffle(spin, z[:, 0:SEQ], SWAP))
                dve_own.link(e, nc.vector.tensor_tensor(spin, spin, sinT[:, :], ALU.mult))
                dve_own.link(e, nc.vector.tensor_tensor(z[:, 0:SEQ], z[:, 0:SEQ], cosT[:, :], ALU.mult))
                nc.vector.tensor_tensor(z[:, 0:SEQ], z[:, 0:SEQ], spin, ALU.add).then_inc(shaped.sem, 1)

            u0 += T
            phase([(high, n_hl[T]), (low, n_hl[T]), (copied, T), (unit_done, 1 + u0), (lo_ready, u0 + 1), (zeroed, 10), (stat, n_st[-1])],
                  pe=pe, act=act, dve=dve)

        def layer_tiles(layer, both):
            w = TOK if both else SEQ
            kg, qg, sc = col("kg", layer), col("qg", layer), HD ** -0.5
            return [("k", 0, TOK, None, True, 1.0), ("v", 0, TOK, None, False, 1.0), ("k", 1, TOK, kg, True, 1.0),
                    ("v", 1, TOK, None, False, 1.0)] + [("q", j, w, qg if j >= 4 else None, True, sc) for j in range(8)]

        def gate_tiles(name, groups, funcs):
            nonlocal u0
            units = 4 * sum(n for _, n in funcs)
            base = u0
            w = sum(n for _, n in groups)
            sg = r_s["sg"]
            done_sig, = signals("gates", sigmoid=units + 4)
            stored = signals("gates", by_dma=True, **{f"stored{j}": 16 + 4 * units for j in range(4)})

            def pe(e):
                e.sem_inc(done_sig.sem, 4)
                with loop(e, 0, units // 4) as i:
                    for j in range(4):
                        u = base + j
                        e.wait_ge(lo_ready, unit_at(u + 1, i, 4))
                        e.wait_ge(done_sig.sem, done_sig.base + i * 4 + j + 1)
                        linear(2 * j, u, groups, h_hi, h_lo, CH).then_inc(unit_done, 1)

            def act(e):
                turn = 0
                for func, turns in funcs:
                    with loop(e, turn, turn + turns) as i:
                        for j in range(4):
                            u = base + j
                            split_hi(e, u + 1, i, 4)
                            e.wait_ge(unit_done, unit_at(u + 2, i, 4))
                            e.wait_ge(stored[j].sem, stored[j].base + i * 16 + 16)
                            nc.scalar.activation(sg[:, j, 0:w], psf[:, 1024 * j:1024 * j + w], func).then_inc(done_sig.sem, 1)
                    turn += turns

            def dve(e):
                with loop(e, 0, units // 4) as i:
                    for j in range(4):
                        split_lo(e, base + j + 1, i, 4)

            def pool(e):
                for j in range(4):
                    e.dma_start(x_keep[:, 2 * j:2 * j + 2, :], x[:, 2 * j:2 * j + 2, :]).then_inc(stored[j].sem, 16)
                with loop(e, 0, units // 4) as i:
                    for j in range(4):
                        e.wait_ge(done_sig.sem, done_sig.base + i * 4 + j + 5)
                        e.dma_start(gates[bass.ds(i * 4 + j, 1), :, 0:w].rearrange("a p n -> p (a n)"), sg[:, j, 0:w]).then_inc(stored[j].sem, 16)

            u0 += units
            phase([(unit_done, 1 + u0), (lo_ready, u0 + 1), (done_sig, units + 4)]
                  + [(s, 16 + 4 * units) for s in stored], pe=pe, act=act, dve=dve, pool=pool)

        def attention(layer, kind, both):
            k_hi, k_lo, v_hi, v_lo = (r_kv[n] for n in ("k_hi", "k_lo", "v_hi", "v_lo"))
            p_hi, p_lo = r_h["p_hi"], r_h["p_lo"]
            qh, ql, pch, pcl = (r_x[n] for n in ("q_hi_now", "q_lo_now", "pc_hi", "pc_lo"))
            pr = r_s["pr"]
            nq = 6 if both else 4
            M = 4 * nq
            q_here = signals("attention", by_dma=True, q_here0=64, q_here1=64)
            (scored, shifted, expd, sunk, scaled, turned, high, low, summed, y_high, y_low) = signals(
                "attention", scored=2 * M, shifted=2 * M, exp=2 * M, sink=0 if kind else 2 * M, scaled=2 * M,
                turned=2 * M, high=2 * M, low=2 * M, summed=8, y_high=4, y_low=4)
            wide = TOK if both else SEQ

            def keys(qt):
                if qt >= 4:
                    return (0, 0)
                return (0, SEQ) if kind else (max(qt - 1, 0) * P, min(qt + 2, 4) * P)

            def span(qt):
                a, b = keys(qt)
                return SEQ - (b - a), TOK

            def blocks(qt):
                a, b = keys(qt)
                return sorted(list(range(a // P, b // P)) + [4, 5], key=SLOT.get)

            def step(n):
                return n // (2 * nq), n // nq, (n // nq) % 2, n % nq

            def pe(e):
                with loop(e, 0, 2) as i:
                    def scores(n):
                        pair, hd, g, qt = step(n)
                        if hd % 2 == 0 and qt == 0:
                            e.wait_ge(q_here[pair].sem, q_here[pair].base + i * 32 + 32)
                        e.wait_ge(expd.sem, expd.base + i * M + max(n - 1, 0))
                        if n == 0:
                            e.wait_ge(shifted.sem, shifted.base + i * M)
                        s = 1024 * (n % 2)
                        kk = 2 * kind + g
                        a, b = keys(qt)
                        lh, ll = qh[:, pair, qt * P:(qt + 1) * P], ql[:, pair, qt * P:(qt + 1) * P]
                        if b > a:
                            o = psf[:, s + SEQ - (b - a):s + SEQ]
                            mm = three(o, lh, ll, k_hi[:, kk, a:b], k_lo[:, kk, a:b], True, kind == 1)
                            if kind == 0:
                                lo = P * (1 if qt == 0 else 0)
                                nc.tensor.matmul(o, identR[:, :], band[:, lo:lo + b - a], start=False, stop=True)
                        o = psf[:, s + SEQ:s + TOK]
                        three(o, lh, ll, k_hi[:, kk, SEQ:TOK], k_lo[:, kk, SEQ:TOK], True, True).then_inc(scored.sem, 1)

                    def turn(n):
                        pair, hd, g, qt = step(n)
                        e.wait_ge(scaled.sem, scaled.base + i * M + n + 1)
                        e.wait_ge(low.sem, low.base + i * M + n)
                        w0 = SEQ - keys(qt)[1]
                        for b, kt in enumerate(blocks(qt)):
                            c = kt * P if kt >= 4 else w0 + kt * P
                            mm = nc.tensor.transpose(psf[:, 2048 + b * P:2048 + (b + 1) * P], pr[:, n % 3, c:c + P], ident)
                        mm.then_inc(turned.sem, 1)

                    def values(hd):
                        g, pair = hd % 2, hd // 2
                        e.wait_ge(low.sem, low.base + i * M + (hd + 1) * nq)
                        if g == 0:
                            e.wait_ge(y_low.sem, y_low.base + i * 2 + pair)
                        buf = hd % 2
                        terms = []
                        for kt in (4, 5, 0, 1, 2, 3):
                            a, b = (0, 4) if (kt >= 4 or kind) else (max(kt - 1, 0), min(kt + 2, 4))
                            for vv, pp in ((v_hi, p_hi), (v_hi, p_lo), (v_lo, p_hi)):
                                terms.append((ps[:, 6, a * P:b * P], vv[:, kind, kt, 64 * g:64 * g + P],
                                              pp[:, buf, SLOT[kt], a * P:b * P]))
                        for m, (o, l, r) in enumerate(terms):
                            mm = nc.tensor.matmul(o, l, r, start=(g == 0 and m == 0), stop=(g == 1 and m == len(terms) - 1))
                        if both:
                            terms = [(vv[:, kind, kt, 64 * g:64 * g + P], pp[:, buf, kt - 4, :]) for kt in (4, 5)
                                     for vv, pp in ((v_hi, pch), (v_hi, pcl), (v_lo, pch))]
                            for m, (l, r) in enumerate(terms):
                                mm = nc.tensor.matmul(ps[:, 7, 0:CTX], l, r, start=(g == 0 and m == 0), stop=(g == 1 and m == 5))
                        mm.then_inc(summed.sem, 1)

                    scores(0)
                    for n in range(M):
                        if n + 1 < M:
                            scores(n + 1)
                        turn(n)
                        if n % nq == 1 and n >= nq:
                            values(n // nq - 1)
                    values(3)

            def act(e):
                with loop(e, 0, 2) as i:

                    def exp(n):
                        pair, hd, g, qt = step(n)
                        e.wait_ge(shifted.sem, shifted.base + i * M + n + 1)
                        e.wait_ge(turned.sem, turned.base + i * M + max(n - 2, 0))
                        a, b = span(qt)
                        s = 1024 * (n % 2)
                        nc.scalar.activation(pr[:, n % 3, a:b], psf[:, s + a:s + b], ACT.Exp, bias=small[:, n % 4:n % 4 + 1],
                                             accum_out=small[:, 4 + n % 4:5 + n % 4]).then_inc(expd.sem, 1)
                        if kind == 0:
                            hcol = layer * 8 + 4 * g + pair
                            nc.scalar.activation(small[:, 8 + n % 4:9 + n % 4], vec[:, bass.ds(i * 2 + (COLS["sink"][0] + hcol), 1)],
                                                 ACT.Exp, bias=small[:, n % 4:n % 4 + 1]).then_inc(sunk.sem, 1)

                    def take(n):
                        pair, hd, g, qt = step(n)
                        e.wait_ge(turned.sem, turned.base + i * M + n + 1)
                        e.wait_ge(summed.sem, summed.base + i * 4 + max(hd - 1, 0))
                        dst_hi, _, src = turned_parts(n)
                        nc.scalar.activation(dst_hi, src, ACT.Copy).then_inc(high.sem, 1)

                    def y(pair):
                        e.wait_ge(summed.sem, summed.base + i * 4 + 2 * pair + 2)
                        nc.scalar.activation(q_hi[:, bass.ds(i * 2 + (4 * kind + pair), 1), 0:wide].rearrange("p a n -> p (a n)"),
                                             psf[:, 3072:3072 + wide], ACT.Copy).then_inc(y_high.sem, 1)

                    for n in range(M):
                        exp(n)
                        if n:
                            take(n - 1)
                        if n % nq == 3 and n // nq == 2:
                            y(0)
                    take(M - 1)
                    y(1)

            def turned_parts(n):
                pair, hd, g, qt = step(n)
                sl = blocks(qt)
                src = psf[:, 2048:2048 + len(sl) * P].rearrange("p (b n) -> p b n", b=len(sl))
                if qt >= 4:
                    at = (slice(None), hd % 2, slice(None), slice((qt - 4) * P, (qt - 3) * P))
                    return pch[at], pcl[at], src
                at = (slice(None), hd % 2, slice(SLOT[sl[0]], SLOT[sl[0]] + len(sl)), slice(qt * P, (qt + 1) * P))
                return p_hi[at], p_lo[at], src

            def n_links():
                c = 0
                for n in range(M):
                    if kind == 0:
                        c += 2
                    c += 1
                return c

            def dve(e):
                with loop(e, 0, 2) as i:
                    dve_own.enter(i, n_links())

                    def shift(n):
                        pair, hd, g, qt = step(n)
                        e.wait_ge(scored.sem, scored.base + i * M + n + 1)
                        a, b = span(qt)
                        s = 1024 * (n % 2)
                        nm = small[:, n % 4:n % 4 + 1]
                        if kind == 1:
                            nc.vector.tensor_reduce(nm, psf[:, s + a:s + b], AX_X, ALU.max, negate=True).then_inc(shifted.sem, 1)
                        else:
                            dve_own.link(e, nc.vector.tensor_reduce(nm, psf[:, s + a:s + b], AX_X, ALU.max, negate=True))
                            hcol = layer * 8 + 4 * g + pair
                            nc.vector.tensor_tensor(nm, nm, nsink[:, bass.ds(i * 2 + hcol, 1)], ALU.min).then_inc(shifted.sem, 1)

                    def scale(n):
                        pair, hd, g, qt = step(n)
                        e.wait_ge(expd.sem, expd.base + i * M + n + 1)
                        a, b = span(qt)
                        rs = small[:, 4 + n % 4:5 + n % 4]
                        if kind == 0:
                            e.wait_ge(sunk.sem, sunk.base + i * M + n + 1)
                            dve_own.link(e, nc.vector.tensor_tensor(rs, rs, small[:, 8 + n % 4:9 + n % 4], ALU.add))
                        rr = small[:, 12 + n % 4:13 + n % 4]
                        dve_own.link(e, nc.vector.reciprocal(rr, rs))
                        nc.vector.tensor_scalar(pr[:, n % 3, a:b], pr[:, n % 3, a:b], rr, None, ALU.mult).then_inc(scaled.sem, 1)

                    def take(n):
                        e.wait_ge(high.sem, high.base + i * M + n + 1)
                        dh, dl, src = turned_parts(n)
                        nc.vector.tensor_tensor(dl, src, dh.bitcast(F32), ALU.subtract).then_inc(low.sem, 1)

                    def y(pair):
                        e.wait_ge(y_high.sem, y_high.base + i * 2 + pair + 1)
                        at = bass.ds(i * 2 + (4 * kind + pair), 1)
                        nc.vector.tensor_tensor(q_lo[:, at, 0:wide].rearrange("p a n -> p (a n)"), psf[:, 3072:3072 + wide],
                                                q_hi[:, at, 0:wide].bitcast(F32).rearrange("p a n -> p (a n)"),
                                                ALU.subtract).then_inc(y_low.sem, 1)

                    shift(0)
                    for n in range(M):
                        if n + 1 < M:
                            shift(n + 1)
                        scale(n)
                        if n:
                            take(n - 1)
                        if n % nq == 3 and n // nq == 2:
                            y(0)
                    take(M - 1)
                    y(1)
                    dve_own.leave(2)

            def pool(e):
                for p in range(PAIRS):
                    if p >= 2:
                        e.wait_ge(scored.sem, scored.base + (p - 1) * 2 * nq)
                    for dst, src in ((qh, q_hi), (ql, q_lo)):
                        e.dma_start(dst[:, p % 2, 0:wide], src[:, 4 * kind + p, 0:wide]).then_inc(q_here[p % 2].sem, 16)

            phase([(y_low, PAIRS), (y_high, PAIRS), (summed, 8), (low, 2 * M), (scaled, 2 * M), (q_here[0], 64), (q_here[1], 64)],
                  pe=pe, act=act, dve=dve, pool=pool)

        def one(t, i, s0, n):
            return t[:, bass.ds(i, 1), s0:s0 + n].rearrange("p a n -> p (a n)")

        def merge(name, groups):
            nonlocal u0
            base = u0
            w = sum(n for _, n in groups)
            ga, gb, m1, m2 = r_s["ga"], r_s["gb"], r_kv["m1"], r_kv["m2"]
            g_here = signals("merge", by_dma=True, gates_here0=128, gates_here1=128)
            gated, mixed, high, low = signals("merge", gated=CH + 2, mixed=CH, high=CH, low=CH)

            def pe(e):
                e.sem_inc(gated.sem, 2)
                with loop(e, 0, 4) as i:
                    for j in range(2):
                        u = base + j
                        e.wait_ge(lo_ready, unit_at(u + 1, i, 2))
                        e.wait_ge(gated.sem, gated.base + i * 2 + j + 1)
                        linear(4 * j, u, groups, q_hi, q_lo, 4)
                        linear(4 * j + 2, u, groups, q_hi, q_lo, 4, first=4, act_first=4).then_inc(unit_done, 1)

            def act(e):
                with loop(e, 0, 4) as i:
                    for j in range(2):
                        split_hi(e, base + j + 1, i, 2)
                        e.wait_ge(mixed.sem, mixed.base + i * 2 + j + 1)
                        nc.scalar.activation(one(h_hi, i * 2 + j, 0, w), m1[:, j, 0:w], ACT.Copy).then_inc(high.sem, 1)

            def dve(e):
                with loop(e, 0, 4) as i:
                    dve_own.enter(i, 2)
                    for j in range(2):
                        u = base + j
                        split_lo(e, u + 1, i, 2)
                        e.wait_ge(unit_done, unit_at(u + 2, i, 2))
                        e.wait_ge(g_here[j].sem, g_here[j].base + i * 32 + 32)
                        b = 2048 * j
                        dve_own.link(e, nc.vector.tensor_tensor(m1[:, j, 0:w], psf[:, b:b + w], ga[:, j, 0:w], ALU.mult))
                        nc.vector.tensor_tensor(m2[:, j, 0:w], psf[:, b + 1024:b + 1024 + w], gb[:, j, 0:w], ALU.mult).then_inc(gated.sem, 1)
                        e.wait_ge(gated.sem, gated.base + i * 2 + j + 3)
                        nc.vector.tensor_tensor(m1[:, j, 0:w], m1[:, j, 0:w], m2[:, j, 0:w], ALU.add).then_inc(mixed.sem, 1)
                        e.wait_ge(high.sem, high.base + i * 2 + j + 1)
                        nc.vector.tensor_tensor(one(h_lo, i * 2 + j, 0, w), m1[:, j, 0:w],
                                                one(h_hi, i * 2 + j, 0, w).bitcast(F32), ALU.subtract).then_inc(low.sem, 1)
                    dve_own.leave(4)

            def pool(e):
                def load(n, j):
                    e.dma_start(ga[:, j, 0:w], gates[n, :, 0:w]).then_inc(g_here[j].sem, 16)
                    e.dma_start(gb[:, j, 0:w], gates[n + CH, :, 0:w]).then_inc(g_here[j].sem, 16)
                for n in range(CH):
                    if n >= 2:
                        e.wait_ge(gated.sem, gated.base + n + 1)
                    load(n, n % 2)

            u0 += N_MERGE
            phase([(unit_done, 1 + u0), (lo_ready, u0 + 1), (high, CH), (low, CH)], pe=pe, act=act, dve=dve, pool=pool)

        def add_to_x(name, groups, act_hi, act_lo, gate, chunks=CH, reload_x=False, plain=False, last=False):
            nonlocal u0
            base = u0
            added, = signals("add", added=CH + 4)
            x_here, = signals("add", by_dma=True, x_here=16 * reload_x)

            def steps(e, body):
                if last:
                    for k in range(2):
                        for j in range(4):
                            body(4 * k + j, None)
                else:
                    with loop(e, 0, 2) as i:
                        for j in range(4):
                            body(j, i)

            def n_at(j, i):
                return j if i is None else i * 4 + j

            def pe(e):
                e.sem_inc(added.sem, 4)
                def body(j, i):
                    e.wait_ge(lo_ready, unit_at(base + j + 1, i, 4))
                    e.wait_ge(added.sem, added.base + n_at(j, i) + 1)
                    linear(2 * (j % 4), base + j, groups, act_hi, act_lo, chunks).then_inc(unit_done, 1)
                steps(e, body)

            def act(e):
                def body(j, i):
                    if not (last and j == 7):
                        split_hi(e, base + j + 1, i, 4)
                steps(e, body)

            def dve(e):
                def body(j, i):
                    if not (last and j == 7):
                        split_lo(e, base + j + 1, i, 4)
                    e.wait_ge(unit_done, unit_at(base + j + 2, i, 4))
                    if reload_x and j % 4 == 0:
                        e.wait_ge(x_here.sem, x_here.base + 16)
                    for v, (s0, n) in enumerate(groups):
                        src = psf[:, 1024 * (j % 4) + s0:1024 * (j % 4) + s0 + n]
                        xc = x[:, j, s0:s0 + n] if i is None else one(x, i * 4 + j, s0, n)
                        if plain:
                            ins = nc.vector.tensor_tensor(xc, src, xc, ALU.add)
                        else:
                            m = mod[:, bass.ds(n_at(j, i) + gate * CH, 1), v]
                            ins = nc.vector.scalar_tensor_tensor(xc, src, m, xc, ALU.mult, ALU.add)
                    ins.then_inc(added.sem, 1)
                steps(e, body)

            def pool(e):
                if reload_x:
                    e.dma_start(x[:, :, :], x_keep).then_inc(x_here.sem, 16)

            u0 += CH
            phase([(unit_done, 1 + u0), (added, CH + 4)] + ([] if last else [(lo_ready, u0 + 1)]), pe=pe, act=act, dve=dve, pool=pool)

        def hidden(name, groups, nf):
            nonlocal u0
            base = u0
            w = sum(n for _, n in groups)
            su, ff = r_kv["su"], r_kv["ff"]
            silud, gated, high, low = signals("hidden", silu=nf, gated=nf + 2, high=nf, low=nf)

            def pe(e):
                e.sem_inc(gated.sem, 2)
                with loop(e, 0, nf // 2) as i:
                    for j in range(4):
                        u = base + j
                        e.wait_ge(lo_ready, unit_at(u + 1, i, 4))
                        if j % 2 == 0:
                            e.wait_ge(gated.sem, gated.base + i * 2 + j // 2 + 1)
                        linear(2 * j, u, groups, h_hi, h_lo, CH).then_inc(unit_done, 1)

            def act(e):
                with loop(e, 0, nf // 2) as i:
                    for j in range(4):
                        u, f = base + j, j // 2
                        split_hi(e, u + 1, i, 4)
                        if j % 2 == 0:
                            e.wait_ge(unit_done, unit_at(u + 2, i, 4))
                            e.wait_ge(gated.sem, gated.base + i * 2 + f + 1)
                            nc.scalar.activation(su[:, f, 0:w], psf[:, 1024 * j:1024 * j + w], ACT.Silu).then_inc(silud.sem, 1)
                        else:
                            e.wait_ge(gated.sem, gated.base + i * 2 + f + 3)
                            nc.scalar.activation(one(q_hi, i * 2 + f, 0, w), ff[:, f, 0:w], ACT.Copy).then_inc(high.sem, 1)

            def dve(e):
                with loop(e, 0, nf // 2) as i:
                    for j in range(4):
                        u, f = base + j, j // 2
                        split_lo(e, u + 1, i, 4)
                        if j % 2:
                            e.wait_ge(unit_done, unit_at(u + 2, i, 4))
                            e.wait_ge(silud.sem, silud.base + i * 2 + f + 1)
                            nc.vector.tensor_tensor(ff[:, f, 0:w], psf[:, 1024 * j:1024 * j + w], su[:, f, 0:w], ALU.mult).then_inc(gated.sem, 1)
                            e.wait_ge(high.sem, high.base + i * 2 + f + 1)
                            nc.vector.tensor_tensor(one(q_lo, i * 2 + f, 0, w), ff[:, f, 0:w],
                                                    one(q_hi, i * 2 + f, 0, w).bitcast(F32), ALU.subtract).then_inc(low.sem, 1)

            u0 += 2 * nf
            phase([(unit_done, 1 + u0), (lo_ready, u0 + 1), (low, nf), (high, nf)], pe=pe, act=act, dve=dve)

        bias_mem = dram("bias_mem", (8, P, RV_LEN + 1))

        def relative_bias():
            rel, hot, rv = r_h["rel_cols"], r_h["onehot"], r_h["rv"]
            here, = signals("bias", by_dma=True, here=32)
            multiplied, copied = signals("bias", multiplied=8, copied=8)
            stored = signals("bias", by_dma=True, stored0=64, stored1=64)

            def pool(e):
                e.dma_start(rel[:, :], big[:, B_REL:B_REL + 8 * P]).then_inc(here.sem, 16)
                e.dma_start(hot[:, :], big[:, B_HOT:B_HOT + RV_LEN]).then_inc(here.sem, 16)
                for h in range(8):
                    e.wait_ge(copied.sem, copied.base + h + 1)
                    e.dma_start(bias_mem[h, :, 0:RV_LEN], rv[:, h % 2, :]).then_inc(stored[h % 2].sem, 16)

            def pe(e):
                e.wait_ge(here.sem, here.base + 32)
                for h in range(8):
                    if h >= 2:
                        e.wait_ge(copied.sem, copied.base + h - 1)
                    for k in range(3):
                        mm = nc.tensor.matmul(ps[:, 3 * (h % 2) + k, 0:384], rel[:, h * P:(h + 1) * P], hot[:, 384 * k:384 * k + 384],
                                              start=True, stop=True)
                    mm.then_inc(multiplied.sem, 1)

            def act(e):
                for h in range(8):
                    e.wait_ge(multiplied.sem, multiplied.base + h + 1)
                    if h >= 2:
                        e.wait_ge(stored[h % 2].sem, stored[h % 2].base + 16 * (h // 2))
                    nc.scalar.activation(rv[:, h % 2, :].rearrange("p (k n) -> p k n", k=3), ps[:, 3 * (h % 2):3 * (h % 2) + 3, 0:384],
                                         ACT.Copy).then_inc(copied.sem, 1)

            phase([(copied, 8), (stored[0], 64), (stored[1], 64)], pe=pe, act=act, pool=pool)

        cmp_raw = r_t["cmp_raw"]
        br, br_cols, kc_hi, kc_lo, vc_hi, vc_lo, cmp_s, cmp_n, kcf = (
            r_q1[n] for n in ("br", "br_cols", "kc_hi", "kc_lo", "vc_hi", "vc_lo", "cmp_s", "cmp_n", "kcf"))

        def compress():
            nonlocal u0
            base = u0
            w2, b1, hid, hid_t = (r_q2[n] for n in ("w2", "b1_rows", "hid", "hid_t"))
            kk, rf, r_hi, r_lo = r_s["kk"], r_s["rf"], r_h["r_hi"], r_h["r_lo"]
            here, = signals("cmp", by_dma=True, here=160)
            (zero, laid, high, low, hidden_, biased, silud, turned, taken, outs, sq_, stat, rough, cols_, kvh, kvl, brt, brc) = signals(
                "cmp", zero=8, laid=8, high=4, low=4, hidden=2, biased=2, silu=2, turned=2, taken=2, outs=2, sq=3,
                stat=2, rough=1, cols=1, kvh=4, kvl=4, br_turned=1, br_cols=1)

            def pool(e):
                e.dma_start(w2[:, :, :, :, :].rearrange("p a b c n -> p (a b c n)"), big[:, B_W2:B_W2 + 8 * P]).then_inc(here.sem, 16)
                e.dma_start(b1[:, :, :].rearrange("p a n -> p (a n)"), big[:, B_B1:B_B1 + 512]).then_inc(here.sem, 16)
                for kind in range(2):
                    for g in range(2):
                        e.dma_start(kk[0:64, 2 * kind + g, :], cmp_raw[64 * g:64 * g + 64, kind, :]).then_inc(here.sem, 16)
                        e.dma_start(kk[64:128, 2 * kind + g, 0:SEQ - 1], cmp_raw[64 * g:64 * g + 64, kind, 1:SEQ]).then_inc(here.sem, 16)

            def dve(e):
                for t in (r_hi[:, :, :, 62:P], r_lo[:, :, :, 62:P], kc_hi[:, :, :], kc_lo[:, :, :], vc_hi[:, :], vc_lo[:, :]):
                    nc.vector.memset(t.bitcast(F32), 0.0).then_inc(zero.sem, 1)
                e.wait_ge(here.sem, here.base + 160)
                for n in range(4):
                    kind, g = n // 2, n % 2
                    if n >= 2:
                        e.wait_ge(low.sem, low.base + n - 1)
                    v = kk[:, n, :].rearrange("p (i c) -> p c i", c=16)
                    for half in range(2):
                        pe_ = col("pe", 16 * kind + 8 * half, 8).unsqueeze(2).to_broadcast([P, 8, 31])
                        nc.vector.tensor_tensor(rf[:, g, 8 * half:8 * half + 8, :], v[:, 0:16:2, half:half + 31], pe_,
                                                ALU.add).then_inc(laid.sem, 1)
                    e.wait_ge(high.sem, high.base + n + 1)
                    e.wait_ge(laid.sem, laid.base + 2 * n + 2)
                    at = (slice(None), kind, slice(None), slice(31 * g, 31 * g + 31))
                    nc.vector.tensor_tensor(r_lo[at], rf[:, g], r_hi[at].bitcast(F32), ALU.subtract).then_inc(low.sem, 1)
                for kind in range(2):
                    for j in range(4):
                        split_lo(e, base + 4 * kind + j + 1)
                    e.wait_ge(unit_done, 1 + base + 4 * kind + 4)
                    nc.vector.tensor_tensor(hid[:, kind], ps[:, kind, 0:256], b1[:, kind], ALU.add).then_inc(biased.sem, 1)
                e.wait_ge(rough.sem, rough.base + 1)
                newton(e, ps[:, 6, 0:31], kcf[:, 2, 0:31], kcf[:, 3, 0:31], HD)
                nc.vector.scalar_tensor_tensor(kcf[:, 1, 0:31], kcf[:, 1, 0:31], col("kg2", 0), kcf[:, 2, 0:31], ALU.mult,
                                               ALU.mult).then_inc(cols_.sem, 1)
                e.wait_ge(kvh.sem, kvh.base + 4)
                for g in range(2):
                    rows = slice(64 * g, 64 * g + 64)
                    nc.vector.tensor_tensor(kc_lo[rows, g, 0:31], kcf[rows, 1, 0:31], kc_hi[rows, g, 0:31].bitcast(F32),
                                            ALU.subtract).then_inc(kvl.sem, 1)
                for g in range(2):
                    nc.vector.tensor_tensor(vc_lo[0:31, P * g:P * g + 64], ps[0:31, 7, 64 * g:64 * g + 64],
                                            vc_hi[0:31, P * g:P * g + 64].bitcast(F32), ALU.subtract).then_inc(kvl.sem, 1)

            def act(e):
                e.wait_ge(zero.sem, zero.base + 6)
                for n in range(4):
                    kind, g = n // 2, n % 2
                    e.wait_ge(laid.sem, laid.base + 2 * n + 2)
                    nc.scalar.activation(r_hi[:, kind, :, 31 * g:31 * g + 31], rf[:, g], ACT.Copy).then_inc(high.sem, 1)
                e.wait_ge(brt.sem, brt.base + 1)
                for qt in range(4):
                    act_own.link(e, nc.scalar.activation(br_cols[:, 3 - qt, :], ps[:, 7, qt * P:qt * P + 32], ACT.Copy))
                nc.scalar.activation(cmp_n[:, 0, :], br_cols[:, 0, 0:4], ACT.Copy).then_inc(brc.sem, 1)
                for kind in range(2):
                    for j in range(4):
                        split_hi(e, base + 4 * kind + j + 1)
                for kind in range(2):
                    e.wait_ge(biased.sem, biased.base + kind + 1)
                    nc.scalar.activation(hid[:, kind], hid[:, kind], ACT.Silu).then_inc(silud.sem, 1)
                for kind in range(2):
                    e.wait_ge(turned.sem, turned.base + kind + 1)
                    nc.scalar.activation(hid_t[:, kind, :, :], ps[:, 2 + kind, 0:256].rearrange("p (a n) -> p a n", a=2),
                                         ACT.Copy).then_inc(taken.sem, 1)
                e.wait_ge(outs.sem, outs.base + 2)
                nc.scalar.activation(kcf[:, 0, 0:31], ps[:, 4, 0:31], ACT.Square).then_inc(sq_.sem, 1)
                nc.scalar.activation(kcf[:, 1, 0:31], ps[:, 4, 0:31], ACT.Copy).then_inc(sq_.sem, 1)
                nc.scalar.activation(kcf[:, 4, 0:31], ps[:, 5, 0:31], ACT.Copy).then_inc(sq_.sem, 1)
                e.wait_ge(stat.sem, stat.base + 2)
                act_own.link(e, nc.scalar.activation(kcf[:, 2, 0:31], ps[:, 6, 0:31], ACT.Ln, scale=1.0 / HD, bias=col("eps")))
                nc.scalar.activation(kcf[:, 2, 0:31], kcf[:, 2, 0:31], ACT.Exp, scale=-0.5).then_inc(rough.sem, 1)
                e.wait_ge(cols_.sem, cols_.base + 1)
                for g in range(2):
                    rows = slice(64 * g, 64 * g + 64)
                    nc.scalar.activation(kc_hi[rows, g, 0:31], kcf[rows, 1, 0:31], ACT.Copy).then_inc(kvh.sem, 1)
                for g in range(2):
                    nc.scalar.activation(vc_hi[0:31, P * g:P * g + 64], ps[0:31, 7, 64 * g:64 * g + 64], ACT.Copy).then_inc(kvh.sem, 1)

            def pe(e):
                for qt in range(4):
                    mm = nc.tensor.transpose(ps[:, 7, qt * P:(qt + 1) * P], br[:, qt * P:(qt + 1) * P], ident)
                mm.then_inc(brt.sem, 1)
                e.wait_ge(zero.sem, zero.base + 6)
                for kind in range(2):
                    e.wait_ge(low.sem, low.base + 2 * kind + 2)
                    for j in range(4):
                        u = base + 4 * kind + j
                        e.wait_ge(lo_ready, u + 1)
                        for k in range(4):
                            m, w = 4 * j + k, slice(256 * k, 256 * k + 256)
                            mm = three(ps[:, kind, 0:256], r_hi[:, kind, m, :], r_lo[:, kind, m, :], w_hi[:, u % 2, w],
                                       w_lo[:, u % 2, w], m == 0, m == 15)
                        mm.then_inc(unit_done, 1)
                for kind in range(2):
                    e.wait_ge(silud.sem, silud.base + kind + 1)
                    for ht in range(2):
                        mm = nc.tensor.transpose(ps[:, 2 + kind, ht * P:(ht + 1) * P], hid[:, kind, ht * P:(ht + 1) * P], ident)
                    mm.then_inc(turned.sem, 1)
                for kind in range(2):
                    e.wait_ge(taken.sem, taken.base + kind + 1)
                    for n in range(4):
                        g, ht = n // 2, n % 2
                        mm = nc.tensor.matmul(ps[:, 4 + kind, 0:31], w2[:, kind, ht, g, :], hid_t[:, kind, ht, 31 * g:31 * g + 31],
                                              start=n == 0, stop=n == 3)
                    mm.then_inc(outs.sem, 1)
                e.wait_ge(sq_.sem, sq_.base + 3)
                nc.tensor.matmul(ps[:, 6, 0:31], bones, kcf[:, 0, 0:31], start=True, stop=True).then_inc(stat.sem, 1)
                e.wait_ge(brc.sem, brc.base + 1)
                nc.tensor.transpose(ps[0:31, 7, 0:P], kcf[:, 4, 0:31], ident).then_inc(stat.sem, 1)

            u0 += N_CMP
            phase([(unit_done, 1 + u0), (lo_ready, u0 + 1), (kvl, 4), (kvh, 4), (cols_, 1), (brc, 1), (low, 4), (zero, 6)],
                  pe=pe, act=act, dve=dve, pool=pool)

        def sparse_attention():
            k_hi, k_lo, v_hi, v_lo = (r_kv[n] for n in ("k_hi", "k_lo", "v_hi", "v_lo"))
            s_hi, s_lo, sc_hi, sc_lo = (r_h[n] for n in ("s_hi", "s_lo", "sc_hi", "sc_lo"))
            qh, ql, bias = r_x["q2_hi"], r_x["q2_lo"], r_x["bias"]
            pr, gn, yf = r_s["pr2"], r_s["gn"], r_s["yf"]
            M, VH = 32, 8
            here = signals("nsa", by_dma=True, here0=5 * 32, here1=5 * 32)
            stored, = signals("nsa", by_dma=True, stored=128)
            (scored, placed, shifted, expd, scaled, turned, high, low, summed, y_ready, y_high, y_low) = signals(
                "nsa", scored=2 * M, placed=2 * M, shifted=2 * M, exp=2 * M, scaled=2 * M, turned=2 * M, high=2 * M, low=2 * M,
                summed=2 * VH, y_ready=4, y_high=4, y_low=4)
            (c_scored, c_shifted, c_exp, c_scaled, c_turned, c_high, c_low) = signals(
                "nsa_cmp", scored=8, shifted=8, exp=8, scaled=8, turned=8, high=8, low=8)

            def step(n):
                return n // 16, (n // 8) % 2, (n // 4) % 2, n % 4, n // 4

            def pe(e):
                with loop(e, 0, 2) as i:
                    def cmp_scores(hd):
                        pair, g = hd // 2, hd % 2
                        if g == 0:
                            e.wait_ge(here[pair].sem, here[pair].base + i * 80 + 80)
                        e.wait_ge(c_shifted.sem, c_shifted.base + i * 4 + hd)
                        for qt in range(4):
                            q = slice(qt * P, (qt + 1) * P)
                            mm = three(ps[:, 4, (3 - qt) * 32:(4 - qt) * 32], qh[:, pair, q], ql[:, pair, q], kc_hi[:, g, :],
                                       kc_lo[:, g, :], True, True)
                        mm.then_inc(c_scored.sem, 1)

                    def cmp_turn(hd):
                        e.wait_ge(c_scaled.sem, c_scaled.base + i * 4 + hd + 1)
                        e.wait_ge(c_low.sem, c_low.base + i * 4 + hd)
                        for qt in range(4):
                            mm = nc.tensor.transpose(ps[0:32, 5, qt * P:(qt + 1) * P], cmp_s[:, 3 - qt, :], ident)
                        mm.then_inc(c_turned.sem, 1)

                    def scores(n):
                        pair, g, b, qt, v = step(n)
                        e.wait_ge(placed.sem, placed.base + i * M + max(n - 1, 0))
                        w = (qt + 1) * P
                        q = slice(qt * P, w)
                        three(ps[:, n % 2, 0:w], qh[:, pair, q], ql[:, pair, q], k_hi[:, 2 * b + g, 0:w], k_lo[:, 2 * b + g, 0:w],
                              True, True).then_inc(scored.sem, 1)

                    def turn(n):
                        pair, g, b, qt, v = step(n)
                        e.wait_ge(scaled.sem, scaled.base + i * M + n + 1)
                        e.wait_ge(low.sem, low.base + i * M + max(n - 1, 0))
                        for kt in range(qt + 1):
                            mm = nc.tensor.transpose(ps[:, 2 + n % 2, kt * P:(kt + 1) * P], pr[:, n % 3, kt * P:(kt + 1) * P], ident)
                        mm.then_inc(turned.sem, 1)

                    def values(v):
                        pair, g, b = v // 4, (v // 2) % 2, v % 2
                        e.wait_ge(low.sem, low.base + i * M + 4 * (v + 1))
                        terms = []
                        if b == 0:
                            e.wait_ge(c_low.sem, c_low.base + i * 4 + v // 2 + 1)
                            if g == 0:
                                e.wait_ge(y_ready.sem, y_ready.base + i * 2 + pair)
                            hb = (v // 2) % 2
                            for vv, pp in ((vc_hi, sc_hi), (vc_hi, sc_lo), (vc_lo, sc_hi)):
                                terms.append((ps[:, 6, :], vv[0:32, 64 * g:64 * g + P], pp[0:32, hb, :]))
                        for kt in range(4):
                            for vv, pp in ((v_hi, s_hi), (v_hi, s_lo), (v_lo, s_hi)):
                                terms.append((ps[:, 6, kt * P:], vv[:, b, kt, 64 * g:64 * g + P], pp[:, v % 2, kt, kt * P:]))
                        for m, (o, l, r) in enumerate(terms):
                            mm = nc.tensor.matmul(o, l, r, start=(v % 4 == 0 and m == 0), stop=(v % 4 == 3 and m == len(terms) - 1))
                        mm.then_inc(summed.sem, 1)

                    cmp_scores(0)
                    scores(0)
                    for n in range(M):
                        if n + 1 < M:
                            if n % 8 == 7:
                                cmp_scores((n + 1) // 8)
                            scores(n + 1)
                        turn(n)
                        if n % 8 == 2:
                            cmp_turn(n // 8)
                        if n % 4 == 1 and n >= 4:
                            values(n // 4 - 1)
                    values(7)

            def act(e):
                with loop(e, 0, 2) as i:
                    def exp(n):
                        w = (step(n)[3] + 1) * P
                        e.wait_ge(shifted.sem, shifted.base + i * M + n + 1)
                        nc.scalar.activation(pr[:, n % 3, 0:w], pr[:, n % 3, 0:w], ACT.Exp, bias=small[:, n % 4:n % 4 + 1],
                                             accum_out=small[:, 4 + n % 4:5 + n % 4]).then_inc(expd.sem, 1)

                    def take(n):
                        pair, g, b, qt, v = step(n)
                        e.wait_ge(turned.sem, turned.base + i * M + n + 1)
                        e.wait_ge(summed.sem, summed.base + i * VH + max(v - 1, 0))
                        nc.scalar.activation(s_hi[:, v % 2, 0:qt + 1, qt * P:(qt + 1) * P],
                                             ps[:, 2 + n % 2, 0:(qt + 1) * P].rearrange("p (b n) -> p b n", b=qt + 1),
                                             ACT.Copy).then_inc(high.sem, 1)

                    def cmp(hd):
                        e.wait_ge(c_shifted.sem, c_shifted.base + i * 4 + hd + 1)
                        nc.scalar.activation(cmp_s[:, :, :], cmp_s[:, :, :], ACT.Exp).then_inc(c_exp.sem, 1)

                    def cmp_take(hd):
                        e.wait_ge(c_turned.sem, c_turned.base + i * 4 + hd + 1)
                        e.wait_ge(summed.sem, summed.base + i * VH + max(2 * hd - 3, 0))
                        nc.scalar.activation(sc_hi[0:32, hd % 2, :], ps[0:32, 5, :], ACT.Copy).then_inc(c_high.sem, 1)

                    def y(pair):
                        e.wait_ge(y_ready.sem, y_ready.base + i * 2 + pair + 1)
                        nc.scalar.activation(qh[:, pair, :], yf[:, :], ACT.Copy).then_inc(y_high.sem, 1)

                    for n in range(M):
                        if n % 8 == 0:
                            cmp(n // 8)
                        exp(n)
                        if n:
                            take(n - 1)
                        if n % 8 == 3:
                            cmp_take(n // 8)
                        if n == 18:
                            y(0)
                    take(M - 1)
                    y(1)

            def dve(e):
                with loop(e, 0, 2) as i:
                    dve_own.enter(i, 4 * 6 + 2 * M)
                    bc = lambda t: t.unsqueeze(2).to_broadcast([P, 4, 32])

                    def shift(n):
                        pair, g, b, qt, v = step(n)
                        w = (qt + 1) * P
                        e.wait_ge(scored.sem, scored.base + i * M + n + 1)
                        e.wait_ge(turned.sem, turned.base + i * M + max(n - 2, 0))
                        nc.vector.tensor_tensor(pr[:, n % 3, 0:w], ps[:, n % 2, 0:w], bias[:, pair, g, 384 - qt * P:SEQ],
                                                ALU.add).then_inc(placed.sem, 1)
                        e.wait_ge(placed.sem, placed.base + i * M + n + 1)
                        nc.vector.tensor_reduce(small[:, n % 4:n % 4 + 1], pr[:, n % 3, 0:w], AX_X, ALU.max, negate=True).then_inc(shifted.sem, 1)

                    def scale(n):
                        pair, g, b, qt, v = step(n)
                        w = (qt + 1) * P
                        e.wait_ge(expd.sem, expd.base + i * M + n + 1)
                        rr = small[:, 12 + n % 4:13 + n % 4]
                        dve_own.link(e, nc.vector.reciprocal(rr, small[:, 4 + n % 4:5 + n % 4]))
                        dve_own.link(e, nc.vector.tensor_tensor(
                            rr, rr, br_cols[:, 3 - qt, bass.ds(i * 2 + (8 * (b + 1) + 4 * g + pair), 1)], ALU.mult))
                        nc.vector.tensor_scalar(pr[:, n % 3, 0:w], pr[:, n % 3, 0:w], rr, None, ALU.mult).then_inc(scaled.sem, 1)

                    def take(n):
                        pair, g, b, qt, v = step(n)
                        e.wait_ge(high.sem, high.base + i * M + n + 1)
                        at = (slice(None), v % 2, slice(0, qt + 1), slice(qt * P, (qt + 1) * P))
                        nc.vector.tensor_tensor(s_lo[at], ps[:, 2 + n % 2, 0:(qt + 1) * P].rearrange("p (b n) -> p b n", b=qt + 1),
                                                s_hi[at].bitcast(F32), ALU.subtract).then_inc(low.sem, 1)

                    def cmp_shift(hd):
                        pair, g = hd // 2, hd % 2
                        wc = bias_of(pair, g)
                        e.wait_ge(c_scored.sem, c_scored.base + i * 4 + hd + 1)
                        e.wait_ge(c_turned.sem, c_turned.base + i * 4 + hd)
                        dve_own.link(e, nc.vector.tensor_tensor(cmp_s[:, :, :], ps[:, 4, 0:P].rearrange("p (r c) -> p r c", r=4), wc, ALU.add))
                        dve_own.link(e, nc.vector.tensor_reduce(cmp_n[:, 0, :], cmp_s[:, :, :], AX_X, ALU.max))
                        nc.vector.tensor_tensor(cmp_s[:, :, :], cmp_s[:, :, :], bc(cmp_n[:, 0, :]), ALU.subtract).then_inc(c_shifted.sem, 1)

                    def cmp_scale(hd):
                        pair, g = hd // 2, hd % 2
                        e.wait_ge(c_exp.sem, c_exp.base + i * 4 + hd + 1)
                        dve_own.link(e, nc.vector.tensor_reduce(cmp_n[:, 1, :], cmp_s[:, :, :], AX_X, ALU.add))
                        dve_own.link(e, nc.vector.reciprocal(cmp_n[:, 2, :], cmp_n[:, 1, :]))
                        dve_own.link(e, nc.vector.tensor_tensor(
                            cmp_n[:, 3, :], cmp_n[:, 2, :],
                            br_cols[:, :, bass.ds(i * 2 + (4 * g + pair), 1)].rearrange("p r a -> p (r a)"), ALU.mult))
                        dve_own.link(e, nc.vector.scalar_tensor_tensor(cmp_s[:, :, :], bias_of(pair, g), NEG / 2, cmp_s[:, :, :],
                                                                       ALU.is_gt, ALU.mult))
                        nc.vector.tensor_tensor(cmp_s[:, :, :], cmp_s[:, :, :], bc(cmp_n[:, 3, :]), ALU.mult).then_inc(c_scaled.sem, 1)

                    def cmp_take(hd):
                        e.wait_ge(c_high.sem, c_high.base + i * 4 + hd + 1)
                        nc.vector.tensor_tensor(sc_lo[0:32, hd % 2, :], ps[0:32, 5, :], sc_hi[0:32, hd % 2, :].bitcast(F32),
                                                ALU.subtract).then_inc(c_low.sem, 1)

                    def y(pair):
                        e.wait_ge(summed.sem, summed.base + i * VH + 4 * pair + 4)
                        e.wait_ge(y_low.sem, y_low.base + i * 2 + pair)
                        nc.vector.tensor_tensor(yf[:, :], ps[:, 6, :], gn[:, pair, :], ALU.mult).then_inc(y_ready.sem, 1)
                        e.wait_ge(y_high.sem, y_high.base + i * 2 + pair + 1)
                        nc.vector.tensor_tensor(ql[:, pair, :], yf[:, :], qh[:, pair, :].bitcast(F32), ALU.subtract).then_inc(y_low.sem, 1)

                    cmp_shift(0)
                    shift(0)
                    for n in range(M):
                        if n % 8 == 0 and n:
                            cmp_shift(n // 8)
                        if n + 1 < M:
                            shift(n + 1)
                        if n % 8 == 1:
                            cmp_scale(n // 8)
                        scale(n)
                        if n:
                            take(n - 1)
                        if n % 8 == 3:
                            cmp_take(n // 8)
                        if n == 18:
                            y(0)
                    take(M - 1)
                    y(1)
                    dve_own.leave(2)

            def bias_of(pair, g):
                at = (pair * 2 + g) * W_LEN + 31
                return bass.AP(bias, at, [[4 * W_LEN, P], [P, 4], [16, 32]])

            def pool(e):
                def store(p):
                    e.wait_ge(y_low.sem, y_low.base + p + 1)
                    for dst, src in ((q_hi, qh), (q_lo, ql)):
                        e.dma_start(dst[:, p, 0:SEQ], src[:, p % 2, :]).then_inc(stored.sem, 16)

                for p in range(PAIRS):
                    s = p % 2
                    if p >= 2:
                        store(p - 2)
                        e.wait_ge(stored.sem, stored.base + 32 * (p - 1))
                    for dst, src in ((qh, q_hi), (ql, q_lo)):
                        e.dma_start(dst[:, s, :], src[:, p, 0:SEQ]).then_inc(here[s].sem, 16)
                    for g in range(2):
                        rows = bias_mem[4 * g + p].rearrange("p l -> (p l)")[P - 1:P - 1 + P * RV_LEN].rearrange("(p l) -> p l", p=P)
                        e.dma_start(bias[:, s, g, :], rows[:, 0:W_LEN]).then_inc(here[s].sem, 16)
                    e.dma_start(gn[:, s, :], gates[16 + p, :, 0:SEQ]).then_inc(here[s].sem, 16)
                store(2)
                store(3)

            phase([(stored, 128), (y_low, 4), (y_high, 4), (summed, 16), (low, 2 * M), (c_low, 8), (here[0], 160), (here[1], 160)],
                  pe=pe, act=act, dve=dve, pool=pool)

        def recurrence():
            nonlocal u0
            base = u0
            u, gl, uc, uc_hi, uc_lo, rg, ig, a, th, aa, hh, sp = (
                r_kv[n] for n in ("u", "gl", "uc", "uc_hi", "uc_lo", "rg", "ig", "a", "th", "aa", "hh", "sp"))
            here, = signals("lru", by_dma=True, here=32)
            sp_e, sp_done, conv, split, split2, blocks_, gated, rt, bb, y_, yh, yl = signals(
                "lru", sp_e=1, sp=1, conv=4, split=4, split2=4, blocks=3, gates=4, root=4, v=4, y=4, yh=4, yl=4)

            def pool(e):
                e.dma_start(u[:, :, :], gates[20:24, :, 0:SEQ].rearrange("c p n -> p c n")).then_inc(here.sem, 16)
                e.dma_start(gl[:, :, :], gates[24:28, :, 0:SEQ].rearrange("c p n -> p c n")).then_inc(here.sem, 16)

            def pe(e):
                e.wait_ge(lo_ready, base + 1)
                s = base % 2
                for c in range(4):
                    e.wait_ge(split2.sem, split2.base + c + 1)
                    if c >= 2:
                        e.wait_ge(gated.sem, gated.base + c - 1)
                    for k in range(2):
                        w = slice((4 * k + c) * P, (4 * k + c + 1) * P)
                        mm = three(ps[:, 2 * (c % 2) + k, :], w_hi[:, s, w], w_lo[:, s, w], uc_hi[:, :], uc_lo[:, :], True, True)
                    mm.then_inc(blocks_.sem if c < 3 else unit_done, 1)

            def act(e):
                az, ex, lam = sp[:, 0, :], sp[:, 1, :], col("lam", 0, 4)
                act_own.link(e, nc.scalar.activation(az, lam, ACT.Abs))
                nc.scalar.activation(ex, az, ACT.Exp, scale=-1.0).then_inc(sp_e.sem, 1)
                split_hi(e, base + 1)
                for c in range(4):
                    e.wait_ge(conv.sem, conv.base + c + 1)
                    if c:
                        e.wait_ge(blocks_.sem, blocks_.base + c)
                    nc.scalar.activation(uc_hi[:, :], uc[:, :], ACT.Copy).then_inc(split.sem, 1)
                    if c < 3:
                        e.wait_ge(blocks_.sem, blocks_.base + c + 1)
                    else:
                        e.wait_ge(unit_done, 1 + base + 1)
                    if c:
                        e.wait_ge(y_.sem, y_.base + c)
                    b = 2 * (c % 2)
                    e.wait_ge(sp_done.sem, sp_done.base + 1)
                    act_own.link(e, nc.scalar.activation(ig[:, :], ps[:, b + 1, :], ACT.Sigmoid, bias=col("bx", c)))
                    act_own.link(e, nc.scalar.activation(rg[:, :], ps[:, b, :], ACT.Sigmoid, bias=col("ba", c)))
                    act_own.link(e, nc.scalar.activation(a[:, :], rg[:, :], ACT.Exp, scale=sp[:, 5, c:c + 1]))
                    act_own.link(e, nc.scalar.activation(aa[:, :], rg[:, :], ACT.Exp, scale=sp[:, 6, c:c + 1]))
                    nc.scalar.activation(th[:, :], rg[:, :], ACT.Tanh, scale=sp[:, 7, c:c + 1]).then_inc(gated.sem, 1)
                    e.wait_ge(rt.sem, rt.base + c + 1)
                    nc.scalar.activation(aa[:, :], aa[:, :], ACT.Sqrt).then_inc(bb.sem, 1)
                    e.wait_ge(y_.sem, y_.base + c + 1)
                    nc.scalar.activation(q_hi[:, 4 + c, 0:SEQ], hh[:, :], ACT.Copy).then_inc(yh.sem, 1)

            def dve(e):
                e.wait_ge(sp_e.sem, sp_e.base + 1)
                T = nc.vector
                own = lambda ins: dve_own.link(e, ins)
                lam, ex, s1, s2, po = col("lam", 0, 4), sp[:, 1, :], sp[:, 2, :], sp[:, 3, :], sp[:, 4, :]
                own(T.tensor_scalar(s2, ex, 2.0, None, ALU.add))
                own(T.reciprocal(s2, s2))
                own(T.tensor_tensor(s1, ex, s2, ALU.mult))
                own(T.tensor_tensor(s2, s1, s1, ALU.mult))
                own(T.tensor_scalar(po, s2, 1.0 / 15, 1.0 / 13, ALU.mult, ALU.add))
                for k in (11, 9, 7, 5, 3, 1):
                    own(T.tensor_tensor(po, po, s2, ALU.mult))
                    own(T.tensor_scalar(po, po, 1.0 / k, None, ALU.add))
                own(T.scalar_tensor_tensor(po, po, 2.0, s1, ALU.mult, ALU.mult))
                own(T.tensor_scalar(s1, lam, -1.0, 0.0, ALU.mult, ALU.max))
                own(T.tensor_tensor(po, po, s1, ALU.add))
                own(T.tensor_scalar(sp[:, 5, :], po, -LRU_C, None, ALU.mult))
                own(T.tensor_scalar(sp[:, 6, :], po, -2 * LRU_C, None, ALU.mult))
                T.tensor_scalar(sp[:, 7, :], po, LRU_C, None, ALU.mult).then_inc(sp_done.sem, 1)
                split_lo(e, base + 1)
                e.wait_ge(here.sem, here.base + 32)
                for c in range(4):
                    if c:
                        e.wait_ge(y_.sem, y_.base + c)
                        e.wait_ge(split2.sem, split2.base + c)
                    cw = lambda k: col("convw", 4 * c + k)
                    own(T.tensor_scalar(uc[:, :], u[:, c, :], cw(3), col("convb", c), ALU.mult, ALU.add))
                    for k in range(3):
                        d = 3 - k
                        ins = T.scalar_tensor_tensor(uc[:, d:], u[:, c, 0:SEQ - d], cw(k), uc[:, d:], ALU.mult, ALU.add)
                        if k < 2:
                            own(ins)
                        else:
                            ins.then_inc(conv.sem, 1)
                    e.wait_ge(split.sem, split.base + c + 1)
                    e.wait_ge(conv.sem, conv.base + c + 1)
                    T.tensor_tensor(uc_lo[:, :], uc[:, :], uc_hi[:, :].bitcast(F32), ALU.subtract).then_inc(split2.sem, 1)
                    e.wait_ge(gated.sem, gated.base + c + 1)
                    own(T.tensor_tensor(ig[:, :], ig[:, :], uc[:, :], ALU.mult))
                    T.scalar_tensor_tensor(aa[:, :], aa[:, :], 1.0, th[:, :], ALU.add, ALU.mult).then_inc(rt.sem, 1)
                    e.wait_ge(bb.sem, bb.base + c + 1)
                    own(T.tensor_tensor(ig[:, :], ig[:, :], aa[:, :], ALU.mult))
                    if c:
                        e.wait_ge(yl.sem, yl.base + c)
                    own(T.tensor_tensor_scan(hh[:, :], a[:, :], ig[:, :], 0.0, ALU.mult, ALU.add))
                    T.tensor_tensor(hh[:, :], hh[:, :], gl[:, c, :], ALU.mult).then_inc(y_.sem, 1)
                    e.wait_ge(yh.sem, yh.base + c + 1)
                    T.tensor_tensor(q_lo[:, 4 + c, 0:SEQ], hh[:, :], q_hi[:, 4 + c, 0:SEQ].bitcast(F32), ALU.subtract).then_inc(yl.sem, 1)

            u0 += 1
            phase([(yl, 4), (yh, 4), (unit_done, 1 + u0), (lo_ready, u0 + 1), (here, 32)], pe=pe, act=act, dve=dve, pool=pool)

        def second_block():
            lat = [LAT]
            sc = HD ** -0.5
            steps = [
                relative_bias,
                lambda: norm("norm_f", lat, lambda c, v: col_at("gf", c), None, out_f32=True),
                lambda: norm("norm_2", lat, lambda c, v: col_at("ng2", c), lambda c, v: 0.0),
                lambda: project([("raw", cmp_raw[:, 0, :], SEQ, None, False, ACT.Copy), ("raw", cmp_raw[:, 1, :], SEQ, None, False, ACT.Copy),
                                 ("k", 0, SEQ, col("kg2", 1), False, 1.0), ("v", 0, SEQ, None, False, 1.0),
                                 ("k", 1, SEQ, col("kg2", 2), False, 1.0), ("v", 1, SEQ, None, False, 1.0)]
                                + [("q", j, SEQ, col("qg2"), False, sc) for j in range(4)]
                                + [("raw", br[:, :], SEQ, None, False, ACT.Sigmoid)]),
                lambda: gate_tiles("gates_2", lat, [(ACT.Sigmoid, 4), (ACT.Silu, 1), (ACT.Copy, 1), (ACT.Silu, 1)]),
                compress, sparse_attention, recurrence,
                lambda: merge("merge_2", lat),
                lambda: add_to_x("out_2", lat, h_hi, h_lo, 0, reload_x=True, plain=True, last=True)]
            for step in steps:
                step()

        for layer in range(DEPTH):
            both = [LAT, CON]
            mine = both if layer == 0 else [LAT]
            steps = [
                lambda: ada(layer),
                lambda: norm(f"norm1_{layer}", both, lambda c, v: aff[:, 0, bass.ds(c, 1), v], lambda c, v: mod[:, bass.ds(c, 1), v]),
                lambda: project(layer_tiles(layer, layer == 0)),
                lambda: gate_tiles(f"gates{layer}", mine, [(ACT.Sigmoid, N_GATE // 4)]),
                lambda: attention(layer, 0, layer == 0),
                lambda: attention(layer, 1, layer == 0),
                lambda: merge(f"merge{layer}", mine),
                lambda: add_to_x(f"out{layer}", mine, h_hi, h_lo, 2, reload_x=True),
                lambda: norm(f"norm2_{layer}", mine, lambda c, v: aff[:, 1, bass.ds(c, 1), v],
                             lambda c, v: mod[:, bass.ds(c + 3 * CH, 1), v])]
            for part, nf in enumerate(FF_PARTS):
                steps += [lambda part=part, nf=nf: hidden(f"hidden{layer}_{part}", mine, nf),
                          lambda part=part, nf=nf: add_to_x(f"down{layer}_{part}", mine, q_hi, q_lo, 5, chunks=nf)]
            for step in steps:
                step()
        second_block()
        assert u0 == N_UNITS

        out_done = sem("out_done")
        block = ctx.enter_context(nc.Block())

        def run(e, name):
            for k, (engines, _) in enumerate(phases):
                if name in engines:
                    for s, v in (phases[k - 1][1] if k else []):
                        if v:
                            e.wait_ge(s, v)
                    engines[name](e)

        @block.sync
        def _(e):
            for s in range(2):
                e.dma_start(raw[:, s, :], stream[s]).then_inc(raw_loaded[s], 16)
            with e.Fori(1, N_UNITS // 2) as i:
                for s in range(2):
                    e.wait_ge(lo_ready, i * 2 + (s - 1))
                    e.dma_start(raw[:, s, :], stream[bass.ds(i * 2 + s, 1)].rearrange("a p n -> p (a n)")).then_inc(raw_loaded[s], 16)
            for s in range(2):
                e.wait_ge(raw_loaded[s], 8 * N_UNITS)

        @block.gpsimd
        def _(e):
            for counter in [unit_done] + from_one:
                e.sem_inc(counter, 1)
            run(e, "pool")
            for s, v in phases[-1][1]:
                e.wait_ge(s, v)
            e.dma_start(out, x[:, :, 0:SEQ]).then_inc(out_done, 16)
            e.wait_ge(out_done, 16)

        @block.scalar
        def _(e):
            run(e, "act")

        @block.vector
        def _(e):
            run(e, "dve")

        @block.tensor
        def _(e):
            run(e, "pe")


PAIR = [[64 * j + r for r in range(64)] + [256 + 64 * j + r for r in range(64)] for j in range(PAIRS)]


def unit_of(w):
    c = w.shape[0] // P
    t = w.reshape(c, P, w.shape[1]).transpose(1, 0, 2).reshape(P, -1)
    if t.shape[1] < UNIT:
        t = np.concatenate([t, np.zeros((P, UNIT - t.shape[1]), np.float32)], axis=1)
    return t


def layer_units(a, l):
    w = a["w_ada"][l]
    for g in range(12):
        for j in range(4):
            yield unit_of(w[256 * j:256 * j + 256, 512 * g:512 * g + 512])
    w = a["w_in"][l]
    for at in (512, 640, 1280, 1408):
        yield unit_of(w[:, at:at + P])
    for at in (0, 768):
        for j in range(PAIRS):
            yield unit_of(w[:, [at + r for r in PAIR[j]]])
    for n in range(16):
        yield unit_of(w[:, 1536 + P * n:1536 + P * n + P])
    rows = sum(PAIR, [])
    for n in range(8):
        c = slice(P * n, P * n + P)
        yield np.concatenate([unit_of(a["w_proj_a"][l][rows][:, c])[:, :512], unit_of(a["w_proj_b"][l][rows][:, c])[:, :512]], axis=1)
    for n in range(8):
        yield unit_of(a["w_out"][l][:, P * n:P * n + P])
    f0 = 0
    for nf in FF_PARTS:
        for f in range(f0, f0 + nf):
            yield unit_of(a["w_ffn_gate"][l][:, P * f:P * f + P])
            yield unit_of(a["w_ffn_up"][l][:, P * f:P * f + P])
        for n in range(8):
            yield unit_of(a["w_ffn_down"][l][P * f0:P * (f0 + nf), P * n:P * n + P])
        f0 += nf


def second_units(a):
    w = a["w_in_2"]
    for at in range(512, 1280, P):
        yield unit_of(w[:, at:at + P])
    for j in range(PAIRS):
        yield unit_of(w[:, PAIR[j]])
    yield unit_of(np.concatenate([w[:, 1792:1816], np.zeros((D, P - 24), np.float32)], axis=1))
    for n in range(16):
        yield unit_of(w[:, 2840 + P * n:2840 + P * n + P])
    for j in range(PAIRS):
        yield unit_of(w[:, [1280 + r for r in PAIR[j]]])
    for at in (1816, 2328):
        for n in range(4):
            yield unit_of(w[:, at + P * n:at + P * n + P])
    for kind in range(2):
        for m in range(4):
            yield unit_of(a["cmp_w1_2"][kind][512 * m:512 * m + 512])
    blocks = np.zeros((8, P, P), np.float32)
    for n in range(8):
        at = slice(64 * (n % 2), 64 * (n % 2) + 64)
        blocks[n // 2, at, at] = a["lru_wa_2"][n]
        blocks[4 + n // 2, at, at] = a["lru_wx_2"][n]
    yield unit_of(blocks.reshape(8 * P, P))
    rows = sum(PAIR, [])
    for n in range(8):
        c = slice(P * n, P * n + P)
        yield np.concatenate([unit_of(a["w_proj_a_2"][rows][:, c])[:, :512], unit_of(a["w_proj_b_2"][:, c])[:, :512]], axis=1)
    for n in range(8):
        yield unit_of(a["w_out_2"][:, P * n:P * n + P])


def columns(v):
    return v.reshape(-1, P).T


def twice(m):
    return np.stack([m, m], axis=2).reshape(P, -1)


def every(v):
    return np.broadcast_to(v.reshape(1, -1), (P, v.size))


def table(a):
    t = np.zeros((P, COLS["all"][1]), np.float32)

    def put(name, v, at=0):
        v = np.asarray(v)
        t[:, COLS[name][0] + at:COLS[name][0] + at + v.shape[1]] = v

    put("ident", np.eye(P, dtype=np.float32))
    put("ones", np.ones((P, P), np.float32))
    b = np.zeros((P, P), np.float32)
    b[:64, :64] = b[64:, 64:] = 1
    put("bones", b)
    s = np.zeros((P, 2), np.float32)
    s[0, 0] = s[1, 1] = s[2, 0] = s[3, 1] = 1
    put("sel", s)
    put("eps", np.full((P, 1), EPS, np.float32))
    put("c", np.stack([columns(a["c"][0]), columns(a["c_ctx"])], axis=2).reshape(P, 16))
    for l in range(DEPTH):
        put("b_ada", twice(columns(a["b_ada"][l])), 96 * l)
        put("g1", twice(columns(a["norm1_g"][l])), 16 * l)
        put("g2", twice(columns(a["norm2_g"][l])), 16 * l)
        put("qg", np.concatenate([a["q_norm_g"][l]] * 2)[:, None], l)
        put("kg", np.concatenate([a["k_norm_g"][l]] * 2)[:, None], l)
        put("sink", every(a["sink_a"][l]), 8 * l)
    put("gf", columns(a["final_norm_g"]))
    put("ng2", columns(a["norm_gain_2"]))
    put("qg2", np.concatenate([a["q_norm_gain_2"]] * 2)[:, None])
    put("kg2", np.concatenate([a["k_norm_gain_2"]] * 2, axis=1).T)
    put("pe", a["cmp_pe_2"].reshape(2, 16, P).transpose(2, 0, 1).reshape(P, 32))
    put("convw", a["conv_w_2"].reshape(4, 4, P).transpose(2, 1, 0).reshape(P, 16))
    put("convb", columns(a["conv_b_2"]))
    put("ba", columns(a["lru_ba_2"]))
    put("bx", columns(a["lru_bx_2"]))
    put("lam", columns(a["lru_lambda_2"]))
    return t


def bucket(n):
    if n < 16:
        return n
    f = np.float32
    return min(16 + int(np.log(f(n) / f(16)) / f(np.log(8.0)) * f(16)), 31)


def constants(a):
    t = np.zeros((P, B_ALL), np.float32)
    tok = np.arange(SEQ)
    pos = np.stack([tok // 64, tok % 64]).astype(np.float32)
    inv = (np.float32(10000.0) ** (-np.arange(0, 32, 2, dtype=np.float32) / np.float32(32))).astype(np.float32)
    for p in range(P):
        d = p % 64
        ang = pos[d // 32] * inv[d % 16]
        t[p, 0:SEQ] = np.cos(ang)
        t[p, SEQ:2 * SEQ] = np.sin(ang) * (-1 if d % 32 < 16 else 1)
    q, k = np.arange(P)[:, None], np.arange(P)[None, :]
    t[:, 2 * SEQ:2 * SEQ + P] = np.where(k < q, NEG, 0)
    t[:, 2 * SEQ + 2 * P:2 * SEQ + 3 * P] = np.where(k > q, NEG, 0)
    t[0:32, B_REL:B_REL + 8 * P] = np.repeat(a["rel_bias_2"], P, axis=1)
    t[32, B_REL:B_REL + 8 * P] = NEG
    for n in range(RV_LEN):
        t[bucket(SEQ - 1 - n) if n < SEQ else 32, B_HOT + n] = 1
    w2 = t[:, B_W2:B_W2 + 8 * P].reshape(P, 2, 2, 2, P)
    for g in range(2):
        w2[:, :, :, g, 64 * g:64 * g + 64] = a["cmp_w2_2"].reshape(2, 2, P, HD).transpose(2, 0, 1, 3)
    t[:, B_W2:B_W2 + 8 * P] = w2.reshape(P, -1)
    t[:, B_B1:] = every(a["cmp_b1_2"])
    return t


def pack(a):
    x = np.concatenate([a["x"][0], a["ctx"][0]], axis=0)
    return {
        "stream": np.stack([u for l in range(DEPTH) for u in layer_units(a, l)] + list(second_units(a))),
        "x": np.ascontiguousarray(x.T.reshape(CH, P, TOK).transpose(1, 0, 2)),
        "cst": table(a),
        "big": constants(a),
    }


def kernel(**inputs):
    import concourse.bacc as bacc
    from concourse.bass_utils import run_bass_kernel_spmd

    nc = bacc.Bacc("TRN2", target_bir_lowering=False, num_devices=1)
    packed = pack({name: np.asarray(v) for name, v in inputs.items()})
    arrays, ins = {}, {}
    for name, v in packed.items():
        v = np.ascontiguousarray(v)
        arrays["in_" + name] = v
        ins[name] = nc.dram_tensor("in_" + name, v.shape, mybir.dt.from_np(v.dtype), kind="ExternalInput").ap()
    out = nc.dram_tensor("out_0", (P, CH, SEQ), F32, kind="ExternalOutput").ap()
    build_program(nc, ins, out)
    result = run_bass_kernel_spmd(nc, [arrays], core_ids=[0])
    got = result.results[0]["out_0"]
    return np.ascontiguousarray(got.transpose(2, 1, 0).reshape(1, SEQ, D))
```

```python
from contextlib import ExitStack

import numpy as np

import concourse.bass as bass
from concourse import mybir

F32 = mybir.dt.float32
F32R = mybir.dt.float32r
ALU = mybir.AluOpType
ACT = mybir.ActivationFunctionType
AX_X = mybir.AxisListType.X

P = 128
D = 1024
CH = D // P
SEQ, CTX = 512, 256
TOK = SEQ + CTX
LAT = (0, SEQ)
CON = (SEQ, CTX)
HD = 64
PAIRS = 4
D_FF = 2816
EPS = 1e-6
NEG = -1e30
DEPTH = 2
RV_LEN = 1152
B_REL, B_HOT, B_W2, B_B1 = 1408, 2432, 3584, 4608
B_ALL = B_B1 + 512
LRU_C = 8.0
W_LEN = 912
UNIT = 1024

N_QKV, N_GATE, N_MERGE, N_OUT = 12, 16, 8, 8
FF_PARTS = (8, 8, 6)
PER_LAYER = N_QKV + N_GATE + N_MERGE + N_OUT + sum(2 * f + CH for f in FF_PARTS)
N_IN2 = 6 + 4 + 1 + 4 + 4 + 4 + 16
N_CMP = 8
N_UNITS = DEPTH * PER_LAYER + N_IN2 + N_CMP + 1 + N_MERGE + N_OUT

COLS = {}


def _cols(**sizes):
    at = 0
    for name, n in sizes.items():
        COLS[name] = (at, n)
        at += n
    COLS["all"] = (0, at)


_cols(ident=128, ones=128, bones=128, sel=2, eps=1, c=16, b_ada=2 * 96, g1=2 * 16, g2=2 * 16, gf=8,
      qg=2, kg=2, sink=16, ng2=8, qg2=1, kg2=3, pe=32, convw=16, convb=4, ba=4, bx=4, lam=4)


def build_program(nc, ins, out):
    stream, ada_w, xin, cst, big = ins["stream"], ins["ada"], ins["x"], ins["cst"], ins["big"]

    with ExitStack() as ctx:
        def sb(name, shape, dt=F32, stack=ctx):
            return stack.enter_context(nc.sbuf_tensor(name, shape, dt))

        def sem(name):
            return ctx.enter_context(nc.semaphore(name))

        def region(name, nbytes, *views):
            got = {}
            for view in views:
                with ExitStack() as s:
                    for n, shape, dt in view:
                        got[n] = sb(n, shape, dt, s)
            sb(name, [P, nbytes // 4])
            return got

        def dram(name, shape):
            return nc.dram_tensor(name, shape, F32, kind="Internal").ap()

        raw = sb("w_raw", [P, 2, UNIT])
        w_hi = sb("w_hi", [P, 2, UNIT], F32R)
        w_lo = sb("w_lo", [P, 2, UNIT], F32R)
        vec = sb("vec", [P, COLS["all"][1]])
        r_t = region("region_tables", 8 * SEQ, [("cosT", [P, SEQ], F32), ("sinT", [P, SEQ], F32)],
                     [("cmp_raw", [P, 2, SEQ], F32)])
        cosT, sinT = r_t["cosT"], r_t["sinT"]
        band = sb("band", [P, 3 * P], F32R)
        identR = sb("identR", [P, P], F32R)
        mod = sb("mod", [P, 6 * CH, 2])
        aff = sb("aff", [P, 2, CH, 2])
        nsink = sb("nsink", [P, 16])
        small = sb("small", [P, 16])
        sink_col = sb("sink_col", [P, 4])
        cs = sb("cs", [P, 2, 16])
        r_x = region("region_x", 4 * CH * TOK,
                     [("x", [P, CH, TOK], F32)],
                     [("q_hi_now", [P, 2, TOK], F32R), ("q_lo_now", [P, 2, TOK], F32R),
                      ("sums", [P, SEQ], F32), ("inv", [P, SEQ], F32), ("y_now", [P, SEQ], F32)],
                     [("q2_hi", [P, 2, SEQ], F32R), ("q2_lo", [P, 2, SEQ], F32R), ("bias", [P, 2, 2, W_LEN], F32)])
        r_h = region("region_h", 8 * CH * TOK,
                     [("h_hi", [P, CH, TOK], F32R), ("h_lo", [P, CH, TOK], F32R)],
                     [("ada_raw", [P, 3, 4 * UNIT], F32)],
                     [(n, [P, 4, SEQ], F32) for n in ("rg", "ig", "a", "th", "aa", "hh")],
                     [("p_hi", [P, 8, SEQ], F32R), ("p_lo", [P, 8, SEQ], F32R), ("max_row", [1, 2, SEQ], F32R),
                      ("sink_row", [1, SEQ], F32), ("sink_row_hi", [1, 2, SEQ], F32R), ("sink_row_lo", [1, 2, SEQ], F32R),
                      ("rows", [1, 192 + P], F32R)],
                                          [("r_hi", [P, 2, 16, P], F32R), ("r_lo", [P, 2, 16, P], F32R)],
                     [("s_hi", [P, 2, 4, SEQ], F32R), ("s_lo", [P, 2, 4, SEQ], F32R),
                      ("sc_hi", [P, 2, SEQ], F32R), ("sc_lo", [P, 2, SEQ], F32R)])
        r_q1 = region("region_q_hi", 4 * CH * TOK, [("q_hi", [P, CH, TOK], F32R)],
                      [("ada_hi", [P, 4, UNIT], F32R)],
                      [("q_hi_half", [P, 4, TOK], F32R), ("br", [P, SEQ], F32), ("br_cols", [P, 4, 32], F32),
                       ("kc_hi", [P, 2, 32], F32R), ("kc_lo", [P, 2, 32], F32R),
                       ("vc_hi", [P, 192], F32R), ("vc_lo", [P, 192], F32R), ("cmp_s", [P, 4, 32], F32),
                       ("cmp_n", [P, 4, 4], F32), ("kcf", [P, 5, 32], F32)])
        r_q2 = region("region_q_lo", 4 * CH * TOK, [("q_lo", [P, CH, TOK], F32R)],
                      [("ada_lo", [P, 4, UNIT], F32R)],
                      [("q_lo_half", [P, 4, TOK], F32R), ("w2", [P, 2, 2, 2, P], F32), ("b1_rows", [P, 2, 256], F32),
                       ("hid", [P, 2, 256], F32), ("hid_t", [P, 2, 2, P], F32)])
        q_hi, q_lo = r_q1["q_hi"], r_q2["q_lo"]
        r_kv = region("region_kv", 4 * (8 * TOK + 4 * 6 * 192),
                      [("k_hi", [P, 4, TOK], F32R), ("k_lo", [P, 4, TOK], F32R),
                       ("v_hi", [P, 2, 6, 192], F32R), ("v_lo", [P, 2, 6, 192], F32R)],
                      [("cl", [P, CH, P], F32R), ("ada_row", [P, 3, 512], F32), ("rel_cols", [P, 8 * P], F32),
                       ("onehot", [P, RV_LEN], F32), ("rv", [P, 2, RV_LEN], F32)],
                      [("sq", [P, 2, TOK], F32), ("acc", [P, TOK], F32), ("y0", [P, TOK], F32),
                       ("tx", [P, 4, TOK], F32), ("hf", [P, 4, TOK], F32)],
                      [("m1", [P, 2, TOK], F32), ("m2", [P, 2, TOK], F32)],
                      [("su", [P, 2, TOK], F32), ("ff", [P, 2, TOK], F32)],
                      [("u", [P, 4, SEQ], F32), ("gl", [P, 4, SEQ], F32), ("uc", [P, 4, SEQ], F32), ("uc_hi", [P, 4, SEQ], F32R),
                       ("uc_lo", [P, 4, SEQ], F32R), ("sp", [P, 8, 4], F32)])
        r_s = region("region_scratch", 4 * 4 * TOK,
                     [("zt", [P, 2, TOK], F32), ("zs", [P, 2, TOK], F32)],
                     [("sg", [P, 4, TOK], F32)],
                     [("pr", [P, 4, SEQ], F32)],
                     [("pr2", [P, 3, SEQ], F32), ("gn", [P, 2, SEQ], F32), ("yf", [P, SEQ], F32)],
                     [("kk", [P, 4, SEQ], F32), ("rf", [P, 2, 16, 31], F32)],
                     [("ga", [P, 2, TOK], F32), ("gb", [P, 2, TOK], F32)])
        x, h_hi, h_lo = r_x["x"], r_h["h_hi"], r_h["h_lo"]
        ps = ctx.enter_context(nc.psum_tensor("ps", [P, 8, 512], F32))
        psf = ps[:, :, :].rearrange("p b n -> p (b n)")
        gates = dram("gates", (2 * CH + 12, P, TOK))
        x_keep = dram("x_keep", (P, CH, TOK))

        def col(name, a=0, n=1):
            at = COLS[name][0] + a
            return vec[:, at:at + n]

        def col_at(name, a):
            return vec[:, bass.ds(COLS[name][0] + a, 1)]

        ident, ones, bones, sel = col("ident", 0, P), col("ones", 0, P), col("bones", 0, P), col("sel", 0, 2)

        raw_loaded = [sem("raw_loaded0"), sem("raw_loaded1")]
        hi_ready, lo_ready, unit_done = sem("hi_ready"), sem("lo_ready"), sem("unit_done")
        const_loaded = sem("const_loaded")

        def split_hi(act, u, i=None, per=0):
            slot = u % 2
            act.wait_ge(raw_loaded[slot], 16 * (u // 2 + 1) if i is None else i * (8 * per) + 16 * (u // 2 + 1))
            if i is not None or u >= 2:
                act.wait_ge(unit_done, u if i is None else i * per + u)
            nc.scalar.activation(w_hi[:, slot, :], raw[:, slot, :], ACT.Copy).then_inc(hi_ready, 1)

        def split_lo(dve, u, i=None, per=0):
            slot = u % 2
            dve.wait_ge(hi_ready, u + 1 if i is None else i * per + (u + 1))
            nc.vector.tensor_tensor(w_lo[:, slot, :], raw[:, slot, :], w_hi[:, slot, :].bitcast(F32),
                                    ALU.subtract).then_inc(lo_ready, 1)

        def unit_at(u, i, per):
            return u if i is None else i * per + u

        def three(out_ap, lh, ll, rh, rl, start, stop):
            nc.tensor.matmul(out_ap, lh, rh, start=start, stop=False)
            nc.tensor.matmul(out_ap, lh, rl, start=False, stop=False)
            return nc.tensor.matmul(out_ap, ll, rh, start=False, stop=stop)

        def linear(slot_bank, u, groups, act_hi, act_lo, chunks, first=0, act_first=0):
            s = u % 2
            for s0, n in groups:
                o = psf[:, slot_bank * 512 + s0:slot_bank * 512 + s0 + n]
                for c in range(chunks):
                    w = slice((first + c) * P, (first + c + 1) * P)
                    mm = three(o, w_hi[:, s, w], w_lo[:, s, w], act_hi[:, act_first + c, s0:s0 + n],
                               act_lo[:, act_first + c, s0:s0 + n], c == 0, c == chunks - 1)
            return mm

        phases = []

        class Signal:

            def __init__(self, s, base):
                self.sem, self.base = s, base

        kept, from_one = {}, []

        def signals(kind, by_dma=False, **totals):
            got = []
            for name, total in totals.items():
                key = kind + "_" + name
                if key not in kept:
                    kept[key] = [sem(key), 0 if by_dma else 1]
                    if not by_dma:
                        from_one.append(kept[key][0])
                got.append(Signal(*kept[key]))
                kept[key][1] += total
            return got

        def phase(done, follows_on=False, **engines):
            phases.append((engines, [(s.sem, s.base + v) if isinstance(s, Signal) else (s, v) for s, v in done], follows_on))

        def loop(eng, a, b):
            return eng.Fori(a, b)

        cond_ready, c_sig, c_sil, c_hi, c_lo = (sem("cond_ready"), sem("c_sig"), sem("c_sil"), sem("c_hi"), sem("c_lo"))

        band_f = r_s["zt"]

        def consts_pool(pool):
            pool.dma_start(vec[:, :], cst).then_inc(const_loaded, 16)
            pool.dma_start(cosT[:, :], big[:, 0:512]).then_inc(const_loaded, 16)
            pool.dma_start(sinT[:, :], big[:, 512:1024]).then_inc(const_loaded, 16)
            pool.dma_start(x[:, :, :], xin).then_inc(const_loaded, 16)

            pool.dma_start(band_f[:, 0, 0:3 * P], big[:, 1024:1024 + 3 * P]).then_inc(const_loaded, 16)

        def consts_act(act):
            act.wait_ge(const_loaded, 80)
            nc.scalar.activation(cs[:, 0, :], col("c", 0, 16), ACT.Sigmoid).then_inc(c_sig, 1)
            split_hi(act, 0)

        def consts_dve(dve):
            dve.wait_ge(const_loaded, 80)
            nc.vector.tensor_copy(band[:, :], band_f[:, 0, 0:3 * P]).then_inc(cond_ready, 1)
            nc.vector.tensor_copy(identR[:, :], ident).then_inc(cond_ready, 1)
            nc.vector.tensor_scalar(nsink[:, :], col("sink", 0, 16), -1.0, None, ALU.mult).then_inc(cond_ready, 1)
            split_lo(dve, 0)
            dve.wait_ge(c_sig, 1)
            nc.vector.tensor_tensor(cs[:, 1, :], cs[:, 0, :], col("c", 0, 16), ALU.mult).then_inc(c_sil, 1)

        phase([(cond_ready, 3), (c_sil, 1), (lo_ready, 1)], pool=consts_pool, act=consts_act, dve=consts_dve)

        u0 = 0
        class Chain:

            def __init__(self, s):
                self.s, self.n, self.i, self.per, self.base = s, 0, None, 0, 0

            def link(self, eng, ins):
                ins.then_inc(self.s, 1)
                self.n += 1
                eng.wait_ge(self.s, self.n if self.i is None else self.i * self.per + self.n)

            @property
            def value(self):
                return self.n if self.i is None else self.i * self.per + self.n

            def enter(self, i, per):
                self.i, self.per, self.start = i, per, self.n

            def leave(self, times):
                assert self.n - self.start == self.per, (self.n - self.start, self.per)
                self.n = self.start + self.per * times
                self.i = None

        dve_own, act_own = Chain(sem("dve_own")), Chain(sem("act_own"))

        bias_mem = dram("bias_mem", (8, P, RV_LEN + 1))

        def relative_bias():
            rel, hot, rv = r_kv["rel_cols"], r_kv["onehot"], r_kv["rv"]
            here, = signals("bias", by_dma=True, here=32)
            multiplied, copied = signals("bias", multiplied=8, copied=8)
            stored = signals("bias", by_dma=True, stored0=64, stored1=64)

            def load(e):
                e.dma_start(rel[:, :], big[:, B_REL:B_REL + 8 * P]).then_inc(here.sem, 16)
                e.dma_start(hot[:, :], big[:, B_HOT:B_HOT + RV_LEN]).then_inc(here.sem, 16)

            def pool(e):
                for h in range(8):
                    e.wait_ge(copied.sem, copied.base + h + 1)
                    e.dma_start(bias_mem[h, :, 0:RV_LEN], rv[:, h % 2, :]).then_inc(stored[h % 2].sem, 16)

            def pe(e):
                e.wait_ge(here.sem, here.base + 32)
                for h in range(8):
                    if h >= 2:
                        e.wait_ge(copied.sem, copied.base + h - 1)
                    for k in range(3):
                        mm = nc.tensor.matmul(ps[:, 2 + 3 * (h % 2) + k, 0:384], rel[:, h * P:(h + 1) * P], hot[:, 384 * k:384 * k + 384],
                                              start=True, stop=True)
                    mm.then_inc(multiplied.sem, 1)

            def act(e):
                for h in range(8):
                    e.wait_ge(multiplied.sem, multiplied.base + h + 1)
                    if h >= 2:
                        e.wait_ge(stored[h % 2].sem, stored[h % 2].base + 16 * (h // 2))
                    nc.scalar.activation(rv[:, h % 2, :].rearrange("p (k n) -> p k n", k=3), ps[:, 2 + 3 * (h % 2):5 + 3 * (h % 2), 0:384],
                                         ACT.Copy).then_inc(copied.sem, 1)

            return dict(pe=pe, act=act, pool=pool, load=load), [(copied, 8), (stored[0], 64), (stored[1], 64)]

        def ada(layer, beside=({}, [])):
            wide, a_hi, a_lo, cl, ada_row = r_h["ada_raw"], r_q1["ada_hi"], r_q2["ada_lo"], r_kv["cl"], r_kv["ada_row"]
            here = signals("ada", by_dma=True, here0=64, here1=64, here2=64)
            high, low, used, row_copied, col_summed, col_kept = signals(
                "ada", high=48, low=48, used=52, row_copied=12, col_summed=12, col_kept=12)
            cl_zero, cl_hi_done, cl_done, aff_done = signals("ada", cl_zero=1, cl_hi=1, cl=1, affine=2)
            sil = cs[:, 1, :].rearrange("p (c v) -> p c v", v=2)

            def pool(e):
                if beside[0]:
                    beside[0]["load"](e)
                for g in range(3):
                    e.dma_start(wide[:, g, :], ada_w[12 * layer + g]).then_inc(here[g].sem, 16)
                if beside[0]:
                    beside[0]["pool"](e)
                with loop(e, 1, 4) as i:
                    for g in range(3):
                        e.wait_ge(low.sem, low.base + i * 12 + (4 * g - 8))
                        e.dma_start(wide[:, g, :], ada_w[bass.ds(i * 3 + (12 * layer + g), 1)].rearrange("a p n -> p (a n)")
                                    ).then_inc(here[g].sem, 16)

            def pe(e):
                if beside[0]:
                    beside[0]["pe"](e)
                e.wait_ge(cl_done.sem, cl_done.base + 1)
                e.sem_inc(used.sem, 4)
                with loop(e, 0, 4) as i:
                    def columns_of(g):
                        e.wait_ge(row_copied.sem, row_copied.base + i * 3 + g + 1)
                        e.wait_ge(col_kept.sem, col_kept.base + i * 3)
                        for m in range(4):
                            mm = nc.tensor.matmul(ps[:, 3 + g, 2 * m:2 * m + 2], ada_row[:, g, m * P:(m + 1) * P], sel,
                                                  start=True, stop=True)
                        mm.then_inc(col_summed.sem, 1)

                    for g in range(3):
                        for q in range(4):
                            e.wait_ge(low.sem, low.base + i * 12 + 4 * g + q + 1)
                            if q == 0:
                                e.wait_ge(row_copied.sem, row_copied.base + i * 3)
                            for cc in range(2):
                                for w in (a_hi, a_lo):
                                    mm = nc.tensor.matmul(ps[:, g, :], cl[:, 2 * q + cc, :], w[:, q, cc * 512:cc * 512 + 512],
                                                          start=(q == 0 and cc == 0 and w is a_hi), stop=(q == 3 and cc == 1 and w is a_lo))
                            mm.then_inc(used.sem, 1)
                            if g and q == 1:
                                columns_of(g - 1)
                    columns_of(2)

            def act(e):
                e.wait_ge(cl_zero.sem, cl_zero.base + 1)
                nc.scalar.activation(cl[:, :, 0:2], sil, ACT.Copy).then_inc(cl_hi_done.sem, 1)
                if beside[0]:
                    beside[0]["act"](e)
                with loop(e, 0, 4) as i:
                    for g in range(3):
                        e.wait_ge(here[g].sem, here[g].base + i * 16 + 16)
                        for q in range(4):
                            e.wait_ge(used.sem, used.base + i * 12 + 4 * g + q + 1)
                            nc.scalar.activation(a_hi[:, q, :], wide[:, g, q * UNIT:(q + 1) * UNIT], ACT.Copy).then_inc(high.sem, 1)

            def dve(e):
                nc.vector.memset(cl[:, :, :].bitcast(F32), 0.0).then_inc(cl_zero.sem, 1)
                e.wait_ge(cl_hi_done.sem, cl_hi_done.base + 1)
                nc.vector.tensor_tensor(cl[:, :, 2:4], sil, cl[:, :, 0:2].bitcast(F32), ALU.subtract).then_inc(cl_done.sem, 1)
                bias = col("b_ada", layer * 96, 96).rearrange("p (n v) -> p n v", v=2)
                with loop(e, 0, 4) as i:
                    def copy_row(g):
                        e.wait_ge(used.sem, used.base + i * 12 + 4 * (g + 1) + 4)
                        e.wait_ge(col_summed.sem, col_summed.base + i * 3)
                        nc.vector.tensor_copy(ada_row[:, g, :], ps[:, g, :]).then_inc(row_copied.sem, 1)

                    def keep(g):
                        e.wait_ge(col_summed.sem, col_summed.base + i * 3 + g + 1)
                        n = i * 12 + 4 * g
                        nc.vector.tensor_tensor(mod[:, bass.ds(n, 4), :], ps[:, 3 + g, 0:8].rearrange("p (m v) -> p m v", v=2),
                                                bias[:, bass.ds(n, 4), :], ALU.add).then_inc(col_kept.sem, 1)

                    for g in range(3):
                        for q in range(4):
                            e.wait_ge(high.sem, high.base + i * 12 + 4 * g + q + 1)
                            nc.vector.tensor_tensor(a_lo[:, q, :], wide[:, g, q * UNIT:(q + 1) * UNIT],
                                                    a_hi[:, q, :].bitcast(F32), ALU.subtract).then_inc(low.sem, 1)
                            if g and q == 0:
                                copy_row(g - 1)
                            if g and q == 2:
                                keep(g - 1)
                    copy_row(2)
                    keep(2)
                e.wait_ge(col_kept.sem, col_kept.base + 12)
                for k, g in ((0, "g1"), (1, "g2")):
                    gain = col(g, layer * 16, 16).rearrange("p (n v) -> p n v", v=2)
                    at = (3 * k + 1) * CH
                    nc.vector.scalar_tensor_tensor(aff[:, k], mod[:, at:at + CH, :], 1.0, gain, ALU.add,
                                                   ALU.mult).then_inc(aff_done.sem, 1)

            phase([(aff_done, 2), (used, 52), (low, 48), (col_summed, 12), (row_copied, 12)] + beside[1], pe=pe, act=act, dve=dve, pool=pool)

        def norm(groups, scale_of, shift_of, out_f32=False):
            sq, acc, y0, tx, hf = (r_kv[n] for n in ("sq", "acc", "y0", "tx", "hf"))
            w = sum(n for _, n in groups)
            ops = len(groups) * (1 if out_f32 else 2)
            squared, summed, stat, rough, scaled, high, low = signals(
                "norm", squared=8, summed=10, stat=1, rough=1, scaled=8, high=8 * ops, low=4 if out_f32 else 12)

            def act(e):
                e.sem_inc(summed.sem, 2)
                with loop(e, 0, 4) as i:
                    for j in range(2):
                        e.wait_ge(summed.sem, summed.base + i * 2 + (j + 1))
                        nc.scalar.activation(sq[:, j, 0:w], one(x, i * 2 + j, 0, w), ACT.Square).then_inc(squared.sem, 1)
                e.wait_ge(stat.sem, stat.base + 1)
                act_own.link(e, nc.scalar.activation(y0[:, 0:w], psf[:, 0:w], ACT.Ln, scale=1.0 / D, bias=col("eps")))
                nc.scalar.activation(y0[:, 0:w], y0[:, 0:w], ACT.Exp, scale=-0.5).then_inc(rough.sem, 1)
                e.sem_inc(low.sem, 4)
                with loop(e, 0, 2) as i:
                    for j in range(4):
                        c = i * 4 + j
                        e.wait_ge(scaled.sem, scaled.base + c + 1)
                        if out_f32:
                            nc.scalar.activation(one(x, c, 0, w), tx[:, j, 0:w], ACT.Identity, scale=scale_of(c, 0)).then_inc(high.sem, 1)
                            continue
                        e.wait_ge(low.sem, low.base + c + 1)
                        for in_full in (True, False):
                            for v, (s0, n) in enumerate(groups):
                                dst = hf[:, j, s0:s0 + n] if in_full else one(h_hi, c, s0, n)
                                nc.scalar.activation(dst, tx[:, j, s0:s0 + n], ACT.Identity, scale=scale_of(c, v),
                                                     bias=shift_of(c, v)).then_inc(high.sem, 1)

            def dve(e):
                e.wait_ge(squared.sem, squared.base + 1)
                nc.vector.tensor_copy(acc[:, 0:w], sq[:, 0, 0:w]).then_inc(summed.sem, 1)
                for c in range(1, 8):
                    e.wait_ge(squared.sem, squared.base + c + 1)
                    e.wait_ge(summed.sem, summed.base + c + 2)
                    nc.vector.tensor_tensor(acc[:, 0:w], acc[:, 0:w], sq[:, c % 2, 0:w], ALU.add).then_inc(summed.sem, 1)
                e.wait_ge(rough.sem, rough.base + 1)
                newton(e, psf[:, 0:w], y0[:, 0:w], D)
                with loop(e, 0, 2) as i:
                    def scale(j):
                        nc.vector.tensor_tensor(tx[:, j, 0:w], one(x, i * 4 + j, 0, w), y0[:, 0:w], ALU.mult).then_inc(scaled.sem, 1)

                    def lower(j):
                        e.wait_ge(high.sem, high.base + i * 4 * ops + (j + 1) * ops)
                        if not out_f32:
                            nc.vector.tensor_tensor(one(h_lo, i * 4 + j, 0, w), hf[:, j, 0:w],
                                                    one(h_hi, i * 4 + j, 0, w).bitcast(F32), ALU.subtract).then_inc(low.sem, 1)

                    scale(0)
                    for j in range(4):
                        if j < 3:
                            scale(j + 1)
                        lower(j)

            def pe(e):
                e.wait_ge(summed.sem, summed.base + 10)
                for s0, n in groups:
                    mm = nc.tensor.matmul(psf[:, s0:s0 + n], ones, acc[:, s0:s0 + n], start=True, stop=True)
                mm.then_inc(stat.sem, 1)

            phase([(high, 8 * ops), (stat, 1), (scaled, 8), (summed, 10), (low, 4 if out_f32 else 12)], act=act, dve=dve, pe=pe)

        def newton(e, sums, y, width):
            dve_own.link(e, nc.vector.scalar_tensor_tensor(sums, sums, width * EPS, y, ALU.add, ALU.mult))
            dve_own.link(e, nc.vector.tensor_tensor(sums, sums, y, ALU.mult))
            dve_own.link(e, nc.vector.tensor_scalar(sums, sums, -0.5 / width, 1.5, ALU.mult, ALU.add))
            dve_own.link(e, nc.vector.tensor_tensor(y, y, sums, ALU.mult))

        SWAP = [(p + 16) % 32 for p in range(32)]

        def project(tiles, between):
            nonlocal u0
            base = u0
            zt, zs = r_s["zt"], r_s["zs"]
            k_hi, k_lo, v_hi, v_lo = (r_kv[n] for n in ("k_hi", "k_lo", "v_hi", "v_lo"))
            kinds = [t[0:2] for t in tiles]
            width = [t[2] for t in tiles]
            normed = [t[3] is not None for t in tiles]
            T = len(kinds)
            before = lambda flags: np.cumsum([0] + [int(f) for f in flags]).tolist()
            n_sq = before(normed)
            n_v = before(k == "v" for k, _ in kinds)
            n_st = before(b or k == "v" for b, (k, _) in zip(normed, kinds))
            n_qk = before(k in "qk" for k, _ in kinds)
            copied, squared, stat, rough, shaped, high, low, v_high, v_low, zeroed = signals(
                "qkv", copied=T, squared=n_sq[T], stat=n_st[T], rough=n_sq[T], shaped=n_qk[T], high=n_qk[T], low=n_qk[T],
                v_high=n_v[T], v_low=n_v[T], zeroed=10)
            at = lambda t: 2048 + 1024 * (n_st[t] % 2)
            groups_of = lambda t: [LAT, CON] if width[t] == TOK else [LAT]

            def pe(e):
                def linear_tile(t):
                    u = base + t
                    e.wait_ge(lo_ready, u + 1)
                    if t >= 2:
                        e.wait_ge(copied.sem, copied.base + t - 1)
                        if normed[t - 2]:
                            e.wait_ge(squared.sem, squared.base + n_sq[t - 1])
                    for v, (s0, n) in enumerate(groups_of(t)):
                        o = psf[:, 1024 * (t % 2) + s0:1024 * (t % 2) + s0 + n]
                        for c in range(CH):
                            w = slice(c * P, c * P + P)
                            mm = three(o, w_hi[:, u % 2, w], w_lo[:, u % 2, w], h_hi[:, c, s0:s0 + n], h_lo[:, c, s0:s0 + n],
                                       c == 0, c == CH - 1)
                            if v == 0 and c == 3 and t:
                                second(t - 1)
                    mm.then_inc(unit_done, 1)

                def second(t):
                    k, j = kinds[t]
                    if k != "v" and not normed[t]:
                        return
                    if k == "v":
                        e.wait_ge(copied.sem, copied.base + t + 1)
                    else:
                        e.wait_ge(squared.sem, squared.base + n_sq[t + 1])
                    if n_st[t] >= 2:
                        prev = [s for s in range(t) if n_st[s + 1] > n_st[s]][-2]
                        if kinds[prev][0] == "v":
                            e.wait_ge(v_low.sem, v_low.base + n_v[prev + 1])
                        else:
                            e.wait_ge(shaped.sem, shaped.base + n_qk[prev + 1])
                    if k == "v":
                        for b in range(width[t] // P):
                            mm = nc.tensor.transpose(psf[:, at(t) + b * P:at(t) + (b + 1) * P], zt[:, t % 2, b * P:(b + 1) * P], ident)
                    else:
                        for s0, n in groups_of(t):
                            mm = nc.tensor.matmul(psf[:, at(t) + s0:at(t) + s0 + n], bones, zs[:, n_qk[t] % 2, s0:s0 + n],
                                                  start=True, stop=True)
                    mm.then_inc(stat.sem, 1)

                for t in range(T):
                    linear_tile(t)
                second(T - 1)

            def act(e):
                def turn_or_norm(t):
                    k, j = kinds[t]
                    w = width[t]
                    if k == "v":
                        e.wait_ge(stat.sem, stat.base + n_st[t + 1])
                        e.wait_ge(zeroed.sem, zeroed.base + 10)
                        for g in range(2):
                            ins = nc.scalar.activation(v_hi[:, j, 0:w // P, 128 * g:128 * g + 64],
                                                       psf[:, at(t):at(t) + w].rearrange("p (b n) -> p b n", n=P)[:, :, 64 * g:64 * g + 64], ACT.Copy)
                            if g == 0:
                                act_own.link(e, ins)
                        ins.then_inc(v_high.sem, 1)
                    elif normed[t]:
                        y = zs[:, n_qk[t] % 2, 0:w]
                        e.wait_ge(stat.sem, stat.base + n_st[t + 1])
                        act_own.link(e, nc.scalar.activation(y, psf[:, at(t):at(t) + w], ACT.Ln, scale=1.0 / HD, bias=col("eps")))
                        nc.scalar.activation(y, y, ACT.Exp, scale=-0.5).then_inc(rough.sem, 1)

                def split(t):
                    k, j = kinds[t]
                    w = width[t]
                    if k not in "qk":
                        return
                    e.wait_ge(shaped.sem, shaped.base + n_qk[t + 1])
                    if k == "q":
                        nc.scalar.activation(q_hi[:, j, 0:w], zt[:, t % 2, 0:w], ACT.Copy).then_inc(high.sem, 1)
                    else:
                        e.wait_ge(zeroed.sem, zeroed.base + 10)
                        act_own.link(e, nc.scalar.activation(k_hi[0:64, 2 * j, 0:w], zt[0:64, t % 2, 0:w], ACT.Copy))
                        nc.scalar.activation(k_hi[64:128, 2 * j + 1, 0:w], zt[64:128, t % 2, 0:w], ACT.Copy).then_inc(high.sem, 1)

                def copy(t):
                    k, j = kinds[t]
                    w = width[t]
                    e.wait_ge(unit_done, 1 + base + t + 1)
                    src = psf[:, 1024 * (t % 2):1024 * (t % 2) + w]
                    if k == "raw":
                        nc.scalar.activation(j, src, tiles[t][5]).then_inc(copied.sem, 1)
                        return
                    if t >= 2 and kinds[t - 2][0] == "v":
                        e.wait_ge(stat.sem, stat.base + n_st[t - 1])
                    elif t >= 2:
                        e.wait_ge(low.sem, low.base + n_qk[t - 1])
                    nc.scalar.activation(zt[:, t % 2, 0:w], src, ACT.Copy, scale=tiles[t][5]).then_inc(copied.sem, 1)
                    if normed[t]:
                        if n_qk[t] >= 2:
                            e.wait_ge(shaped.sem, shaped.base + n_qk[t] - 1)
                        nc.scalar.activation(zs[:, n_qk[t] % 2, 0:w], src, ACT.Square).then_inc(squared.sem, 1)

                for t in range(T + 2):
                    if t < T:
                        split_hi(e, base + t + 1)
                    if 1 <= t <= T:
                        turn_or_norm(t - 1)
                    if t >= 2:
                        split(t - 2)
                    if t < T:
                        copy(t)

            def dve(e):
                for k_part in (k_hi, k_lo):
                    for j in range(2):
                        nc.vector.memset(k_part[64:128, 2 * j, :].bitcast(F32), 0.0).then_inc(zeroed.sem, 1)
                        nc.vector.memset(k_part[0:64, 2 * j + 1, :].bitcast(F32), 0.0).then_inc(zeroed.sem, 1)
                nc.vector.memset(v_hi[:, :, :, 64:128].bitcast(F32), between).then_inc(zeroed.sem, 1)
                nc.vector.memset(v_lo[:, :, :, 64:128].bitcast(F32), 0.0).then_inc(zeroed.sem, 1)
                for t in range(T + 2):
                    if t < T:
                        split_lo(e, base + t + 1)
                    if t >= 2:
                        lower(e, t - 2)
                    if 1 <= t <= T:
                        shape(e, t - 1)

            def lower(e, t):
                k, j = kinds[t]
                w = width[t]
                z = zt[:, t % 2, :]
                if k not in "qk":
                    return
                e.wait_ge(high.sem, high.base + n_qk[t + 1])
                if k == "q":
                    nc.vector.tensor_tensor(q_lo[:, j, 0:w], z[:, 0:w], q_hi[:, j, 0:w].bitcast(F32), ALU.subtract).then_inc(low.sem, 1)
                else:
                    dve_own.link(e, nc.vector.tensor_tensor(k_lo[0:64, 2 * j, 0:w], z[0:64, 0:w],
                                                            k_hi[0:64, 2 * j, 0:w].bitcast(F32), ALU.subtract))
                    nc.vector.tensor_tensor(k_lo[64:128, 2 * j + 1, 0:w], z[64:128, 0:w],
                                            k_hi[64:128, 2 * j + 1, 0:w].bitcast(F32), ALU.subtract).then_inc(low.sem, 1)

            def shape(e, t):
                k, j = kinds[t]
                w = width[t]
                z = zt[:, t % 2, :]
                if k == "raw":
                    return
                if k == "v":
                    e.wait_ge(v_high.sem, v_high.base + n_v[t + 1])
                    for g in range(2):
                        ins = nc.vector.tensor_tensor(v_lo[:, j, 0:w // P, 128 * g:128 * g + 64],
                                                      psf[:, at(t):at(t) + w].rearrange("p (b n) -> p b n", n=P)[:, :, 64 * g:64 * g + 64],
                                                      v_hi[:, j, 0:w // P, 128 * g:128 * g + 64].bitcast(F32), ALU.subtract)
                        if g == 0:
                            dve_own.link(e, ins)
                    ins.then_inc(v_low.sem, 1)
                    return
                y = zs[:, n_qk[t] % 2, :]
                e.wait_ge(copied.sem, copied.base + t + 1)
                if normed[t]:
                    e.wait_ge(rough.sem, rough.base + n_sq[t + 1])
                    newton(e, psf[:, at(t):at(t) + w], y[:, 0:w], HD)
                    ins = nc.vector.scalar_tensor_tensor(z[:, 0:w], z[:, 0:w], tiles[t][3], y[:, 0:w], ALU.mult, ALU.mult)
                    if tiles[t][4]:
                        dve_own.link(e, ins)
                    else:
                        ins.then_inc(shaped.sem, 1)
                if tiles[t][4]:
                    spin_heads(e, z, y[:, 0:SEQ])

            def spin_heads(e, z, spin):
                dve_own.link(e, nc.vector.stream_shuffle(spin, z[:, 0:SEQ], SWAP))
                dve_own.link(e, nc.vector.tensor_tensor(spin, spin, sinT[:, :], ALU.mult))
                dve_own.link(e, nc.vector.tensor_tensor(z[:, 0:SEQ], z[:, 0:SEQ], cosT[:, :], ALU.mult))
                nc.vector.tensor_tensor(z[:, 0:SEQ], z[:, 0:SEQ], spin, ALU.add).then_inc(shaped.sem, 1)

            u0 += T
            phase([(high, n_qk[T]), (low, n_qk[T]), (v_high, n_v[T]), (v_low, n_v[T]), (copied, T), (unit_done, 1 + u0), (lo_ready, u0 + 1), (zeroed, 10), (stat, n_st[-1])],
                  pe=pe, act=act, dve=dve)

        def layer_tiles(layer, both):
            w = TOK if both else SEQ
            kg, qg, sc = col("kg", layer), col("qg", layer), HD ** -0.5
            return [("k", 0, TOK, None, True, 1.0), ("v", 0, TOK, None, False, 1.0), ("k", 1, TOK, kg, True, 1.0),
                    ("v", 1, TOK, None, False, 1.0)] + [("q", j, w, qg if j >= 4 else None, True, sc) for j in range(8)]

        def gate_tiles(name, groups, funcs):
            nonlocal u0
            units = 4 * sum(n for _, n in funcs)
            base = u0
            w = sum(n for _, n in groups)
            sg = r_s["sg"]
            done_sig, = signals("gates", sigmoid=units + 4)
            stored = signals("gates", by_dma=True, **{f"stored{j}": 16 + 4 * units for j in range(4)})

            def pe(e):
                e.sem_inc(done_sig.sem, 4)
                with loop(e, 0, units // 4) as i:
                    for j in range(4):
                        u = base + j
                        e.wait_ge(lo_ready, unit_at(u + 1, i, 4))
                        e.wait_ge(done_sig.sem, done_sig.base + i * 4 + j + 1)
                        linear(2 * j, u, groups, h_hi, h_lo, CH).then_inc(unit_done, 1)

            def act(e):
                turn = 0
                for func, turns in funcs:
                    with loop(e, turn, turn + turns) as i:
                        for j in range(4):
                            u = base + j
                            split_hi(e, u + 1, i, 4)
                            e.wait_ge(unit_done, unit_at(u + 2, i, 4))
                            e.wait_ge(stored[j].sem, stored[j].base + i * 16 + 16)
                            nc.scalar.activation(sg[:, j, 0:w], psf[:, 1024 * j:1024 * j + w], func).then_inc(done_sig.sem, 1)
                    turn += turns

            def dve(e):
                with loop(e, 0, units // 4) as i:
                    for j in range(4):
                        split_lo(e, base + j + 1, i, 4)

            def pool(e):
                for j in range(4):
                    e.dma_start(x_keep[:, 2 * j:2 * j + 2, :], x[:, 2 * j:2 * j + 2, :]).then_inc(stored[j].sem, 16)
                with loop(e, 0, units // 4) as i:
                    for j in range(4):
                        e.wait_ge(done_sig.sem, done_sig.base + i * 4 + j + 5)
                        e.dma_start(gates[bass.ds(i * 4 + j, 1), :, 0:w].rearrange("a p n -> p (a n)"), sg[:, j, 0:w]).then_inc(stored[j].sem, 16)

            u0 += units
            phase([(unit_done, 1 + u0), (lo_ready, u0 + 1), (done_sig, units + 4)]
                  + [(s, 16 + 4 * units) for s in stored], pe=pe, act=act, dve=dve, pool=pool)

        def attention(layer, kind, both):
            k_hi, k_lo, v_hi, v_lo = (r_kv[n] for n in ("k_hi", "k_lo", "v_hi", "v_lo"))
            p_hi, p_lo, max_row, sink_row, sink_hi, sink_lo, rows = (
                r_h[n] for n in ("p_hi", "p_lo", "max_row", "sink_row", "sink_row_hi", "sink_row_lo", "rows"))
            qh, ql, sums, inv, yf = (r_x[n] for n in ("q_hi_now", "q_lo_now", "sums", "inv", "y_now"))
            pr = r_s["pr"]
            neg_max = small[:, 0:16].rearrange("p (a b) -> p a b", a=4)
            wide = TOK if both else SEQ
            items = [(pair, g, ctx_q) for pair in range(2) for ctx_q in range(1 + both) for g in range(2)]
            NI, NU = len(items), len(items) // 2
            LAG = 3

            def window(kt, ctx_q):
                if ctx_q:
                    return 0, 2
                return (0, 4) if kt >= 4 or kind else (max(kt - 1, 0), min(kt + 2, 4))

            steps = [(n, kt) for n, (_, _, ctx_q) in enumerate(items) for kt in ((4, 5) if ctx_q else (4, 5, 0, 1, 2, 3))]
            tiles = [(n, qt) for n, (_, _, ctx_q) in enumerate(items) for qt in range(2 if ctx_q else 4)]
            ST, MT = len(steps), len(tiles)
            items.append((2, 0, 0))
            tiles += [(NI, qt) for qt in range(4)]
            end = [max(t for t in range(ST) if steps[t][0] == n) + 1 for n in range(NI)]
            tiles_end = [max(m for m in range(MT + 4) if tiles[m][0] == n) + 1 for n in range(NI + 1)]
            tiles_of = lambda n: [m for m in range(MT + 4) if tiles[m][0] == n]

            row_at = [end[n] - (1 if items[n][2] else 2) for n in range(NI)]

            beside = [-1] * (MT + 4)
            for m in reversed(range(4, MT + 4)):
                n = tiles[m][0]
                latest = row_at[n - 1] - (0 if m + 1 == tiles_end[n] and items[n - 1][2] else 1)
                beside[m] = min(latest, beside[m + 1] - 1 if m + 1 < MT + 4 else latest)
            tiles_at = lambda t: [m for m in range(4, MT + 4) if beside[m] == t or (t == 0 and beside[m] < 0)]

            q_here = signals("attention", by_dma=True, q_here0=64, q_here1=64)
            (ones_set, scored, maxed, floored, row_turned, row_copied, made, exped, high, low, valued, sunk, sink_high, sink_low,
             y_taken, y_ready, y_high, y_low) = signals(
                "attention", ones_set=0 if kind else 3, scored=2 * MT + 4, maxed=2 * MT + 4, floored=0 if kind else 4 * NI + 2,
                row_turned=2 * NI + 1, row_copied=2 * NI + 1, made=2 * ST, exp=2 * ST, high=2 * ST, low=2 * ST, valued=2 * ST,
                sunk=0 if kind else 2 * NI + 1, sink_high=0 if kind else 2 * NI + 1, sink_low=0 if kind else 2 * NI,
                y_taken=8 * NU, y_ready=2 * NU, y_high=2 * NU, y_low=2 * NU)

            def pieces(u):
                return 2 if items[2 * u][2] else 4

            def keys(qt, ctx_q):
                if ctx_q:
                    return (0, 0)
                return (0, SEQ) if kind else (max(qt - 1, 0) * P, min(qt + 2, 4) * P)

            def pe(e):
                def functions(i):
                    def tile_scores(m):
                        n, qt = tiles[m]
                        pair, g, ctx_q = items[n]
                        if g == 0 and ctx_q == 0 and qt == 0:
                            if pair == 1:
                                e.wait_ge(q_here[1].sem, q_here[1].base + i * 32 + 32)
                            else:
                                e.wait_ge(q_here[0].sem, q_here[0].base + (64 if pair else 32))
                        pair %= 2
                        e.wait_ge(maxed.sem, maxed.base + i * MT + m)
                        kk = 2 * kind + g
                        a, b = keys(qt, ctx_q)
                        at = (4 * ctx_q + qt) * P
                        lh = qh[:, pair, at:at + P]
                        if b > a:
                            o = psf[:, SEQ - (b - a):SEQ]
                            nc.tensor.matmul(o, lh, k_hi[:, kk, a:b], start=True, stop=kind == 1)
                            if kind == 0:
                                lo = P * (1 if qt == 0 else 0)
                                nc.tensor.matmul(o, identR[:, :], band[:, lo:lo + b - a], start=False, stop=True)
                        nc.tensor.matmul(psf[:, SEQ:TOK], lh, k_hi[:, kk, SEQ:TOK], start=True, stop=True).then_inc(scored.sem, 1)

                    def turn_row(n):
                        e.wait_ge(maxed.sem, maxed.base + i * MT + tiles_end[n])
                        if kind == 0:
                            e.wait_ge(floored.sem, floored.base + i * 2 * NI + 2 * n + 2)
                        e.wait_ge(row_copied.sem, row_copied.base + i * NI + n)
                        for j in range(len(tiles_of(n))):
                            mm = nc.tensor.matmul(ps[0:1, 5, j * P:(j + 1) * P], neg_max[:, n % 4, j:j + 1], ident, start=True, stop=True)
                        mm.then_inc(row_turned.sem, 1)

                    def make(t):
                        n, kt = steps[t]
                        pair, g, ctx_q = items[n]
                        a, b = window(kt, ctx_q)
                        e.wait_ge(exped.sem, exped.base + i * ST + max(t - 2, 0))
                        o = ps[:, 2 + t % 3, 0:(b - a) * P]
                        q = slice((4 * ctx_q + a) * P, (4 * ctx_q + b) * P)
                        k = slice(kt * P, kt * P + P)
                        kk = 2 * kind + g
                        three(o, k_hi[:, kk, k], k_lo[:, kk, k], qh[:, pair, q], ql[:, pair, q], True, False)
                        if kind == 0 and kt < 4:
                            lo = P * (1 if kt == 0 else 0)
                            nc.tensor.matmul(o, identR[:, :], band[:, lo:lo + (b - a) * P], start=False, stop=False)
                        e.wait_ge(row_copied.sem, row_copied.base + i * NI + n + 1)
                        nc.tensor.matmul(o, rows[:, 192:192 + P], max_row[:, n % 2, a * P:b * P], start=False,
                                         stop=True).then_inc(made.sem, 1)

                    def values(t):
                        n, kt = steps[t]
                        pair, g, ctx_q = items[n]
                        a, b = window(kt, ctx_q)
                        first = kt == 4
                        e.wait_ge(low.sem, low.base + i * ST + t + 1)
                        if first:
                            e.wait_ge(y_taken.sem, y_taken.base + i * 4 * NU + 4 * (n // 2))
                        o = ps[:, 6 + g, a * P:b * P]
                        last = t + 1 == end[n]
                        at = (slice(None), t % 8, slice(0, (b - a) * P))
                        w = slice(64 * g, 64 * g + P)
                        mm = None
                        for v_part, p_part in ((v_hi, p_hi), (v_hi, p_lo), (v_lo, p_hi)):
                            mm = nc.tensor.matmul(o, v_part[:, kind, kt, w], p_part[at], start=first and mm is None,
                                                  stop=last and kind == 1 and v_part is v_lo)
                        if last and kind == 0:
                            e.wait_ge(sink_low.sem, sink_low.base + i * NI + n + 1)
                            q = slice(0, 2 * P if ctx_q else SEQ)
                            for part in (sink_hi, sink_lo):
                                mm = nc.tensor.matmul(ps[:, 6 + g, q], rows[:, w], part[:, n % 2, q], start=False, stop=part is sink_lo)
                        mm.then_inc(valued.sem, 1)

                    return tile_scores, turn_row, make, values

                if kind == 0:
                    e.wait_ge(ones_set.sem, ones_set.base + 3)
                tile_scores, turn_row, _, _ = functions(0)
                for m in range(4):
                    tile_scores(m)
                turn_row(0)
                with loop(e, 0, 2) as i:
                    tile_scores, turn_row, make, values = functions(i)
                    for t in range(ST + LAG):
                        if t < ST:
                            make(t)
                            for m in tiles_at(t):
                                tile_scores(m)
                        if t >= LAG:
                            values(t - LAG)
                        if t in row_at:
                            turn_row(steps[t][0] + 1)

            def act(e):
                def functions(i):
                    def copy_row(n):
                        q = slice(0, P * len(tiles_of(n)))
                        pair, g, ctx_q = items[n]
                        e.wait_ge(row_turned.sem, row_turned.base + i * NI + n + 1)
                        nc.scalar.activation(max_row[:, n % 2, q], ps[0:1, 5, q], ACT.Copy).then_inc(row_copied.sem, 1)
                        if kind == 0:
                            e.wait_ge(row_copied.sem, row_copied.base + i * NI + n + 1)
                            e.wait_ge(sink_low.sem, sink_low.base + i * NI + n)
                            nc.scalar.activation(sink_row[:, q], max_row[:, n % 2, q].bitcast(F32), ACT.Exp,
                                                 bias=sink_col[0:1, n % 4:n % 4 + 1]).then_inc(sunk.sem, 1)
                            e.wait_ge(sunk.sem, sunk.base + i * NI + n + 1)
                            if n >= 2:
                                e.wait_ge(valued.sem, valued.base + i * ST + end[n - 2])
                            nc.scalar.activation(sink_hi[:, n % 2, q], sink_row[:, q], ACT.Copy).then_inc(sink_high.sem, 1)

                    def exp(t):
                        n, kt = steps[t]
                        a, b = window(kt, items[n][2])
                        w = (b - a) * P
                        e.wait_ge(made.sem, made.base + i * ST + t + 1)
                        e.wait_ge(low.sem, low.base + i * ST + max(t - 3, 0))
                        nc.scalar.activation(pr[:, t % 4, 0:w], ps[:, 2 + t % 3, 0:w], ACT.Exp).then_inc(exped.sem, 1)
                        e.wait_ge(exped.sem, exped.base + i * ST + t + 1)
                        e.wait_ge(valued.sem, valued.base + i * ST + max(t - 7, 0))
                        nc.scalar.activation(p_hi[:, t % 8, 0:w], pr[:, t % 4, 0:w], ACT.Copy).then_inc(high.sem, 1)

                    def take(u):
                        w = 2 * P if items[2 * u][2] else SEQ
                        e.wait_ge(valued.sem, valued.base + i * ST + end[2 * u + 1])
                        e.wait_ge(y_low.sem, y_low.base + i * NU + u)
                        up, dn = slice(0, 64), slice(64, P)
                        for dst, rows_, bank, src in ((sums, up, 6, dn), (sums, dn, 7, up), (yf, up, 6, up), (yf, dn, 7, dn)):
                            nc.scalar.activation(dst[rows_, 0:w], ps[src, bank, 0:w], ACT.Copy).then_inc(y_taken.sem, 1)

                    def y(u):
                        pair, _, ctx_q = items[2 * u]
                        s0, w = CON if ctx_q else LAT
                        e.wait_ge(y_ready.sem, y_ready.base + i * NU + u + 1)
                        nc.scalar.activation(one(q_hi, i * 2 + (4 * kind + pair), s0, w), yf[:, 0:w], ACT.Copy).then_inc(y_high.sem, 1)

                    return copy_row, exp, take, y

                functions(0)[0](0)
                with loop(e, 0, 2) as i:
                    copy_row, exp, take, y = functions(i)
                    for t in range(ST + LAG + 3):
                        if t < ST:
                            exp(t)
                        for u in range(NU):
                            since = t - (end[2 * u + 1] - 1 + LAG)
                            if since == 0:
                                take(u)
                            if since == pieces(u) - 1:
                                y(u)
                        if t in row_at:
                            copy_row(steps[t][0] + 1)

            def dve(e):
                if kind == 0:
                    nc.vector.memset(rows[:, 0:192].bitcast(F32), 0.0).then_inc(ones_set.sem, 1)
                    e.wait_ge(ones_set.sem, ones_set.base + 1)
                    nc.vector.memset(rows[:, 64:P].bitcast(F32), 1.0).then_inc(ones_set.sem, 1)
                    nc.vector.memset(rows[:, 192:192 + P].bitcast(F32), 1.0).then_inc(ones_set.sem, 1)

                def functions(i):
                    def tile_max(m):
                        n, qt = tiles[m]
                        pair, g, ctx_q = items[n]
                        e.wait_ge(scored.sem, scored.base + i * MT + m + 1)
                        a, b = keys(qt, ctx_q)
                        if n >= 4 and qt == 0:
                            e.wait_ge(row_turned.sem, row_turned.base + i * NI + n - 3)
                        nc.vector.tensor_reduce(neg_max[:, n % 4, qt:qt + 1], psf[:, SEQ - (b - a):TOK], AX_X, ALU.max,
                                                negate=True).then_inc(maxed.sem, 1)
                        if kind == 0 and m + 1 == tiles_end[n]:
                            e.wait_ge(maxed.sem, maxed.base + i * MT + m + 1)
                            cols = neg_max[:, n % 4, 0:len(tiles_of(n))]
                            hcol = layer * 8 + 4 * g + pair
                            nc.vector.tensor_scalar(sink_col[:, n % 4:n % 4 + 1], ones[:, 0:1], col_at("sink", i * 2 + hcol), None,
                                                    ALU.mult).then_inc(floored.sem, 1)
                            nc.vector.tensor_scalar(cols, cols, nsink[:, bass.ds(i * 2 + hcol, 1)], None, ALU.min).then_inc(floored.sem, 1)

                    def lower(t):
                        n, kt = steps[t]
                        a, b = window(kt, items[n][2])
                        w = (b - a) * P
                        e.wait_ge(high.sem, high.base + i * ST + t + 1)
                        nc.vector.tensor_tensor(p_lo[:, t % 8, 0:w], pr[:, t % 4, 0:w], p_hi[:, t % 8, 0:w].bitcast(F32),
                                                ALU.subtract).then_inc(low.sem, 1)
                        if kind == 0 and (t == 0 or steps[t - 1][0] != n):
                            q = slice(0, P * len(tiles_of(n)))
                            e.wait_ge(sink_high.sem, sink_high.base + i * NI + n + 1)
                            nc.vector.tensor_tensor(sink_lo[:, n % 2, q], sink_row[:, q], sink_hi[:, n % 2, q].bitcast(F32),
                                                    ALU.subtract).then_inc(sink_low.sem, 1)

                    def divide(u, piece):
                        if piece == 0:
                            e.wait_ge(y_taken.sem, y_taken.base + i * 4 * NU + 4 * (u + 1))
                        at = slice(piece * P, piece * P + P)
                        dve_own.link(e, nc.vector.reciprocal(inv[:, at], sums[:, at]))
                        if piece + 1 == pieces(u):
                            w = P * pieces(u)
                            nc.vector.tensor_tensor(yf[:, 0:w], yf[:, 0:w], inv[:, 0:w], ALU.mult).then_inc(y_ready.sem, 1)

                    def y(u):
                        pair, _, ctx_q = items[2 * u]
                        s0, w = CON if ctx_q else LAT
                        e.wait_ge(y_high.sem, y_high.base + i * NU + u + 1)
                        nc.vector.tensor_tensor(one(q_lo, i * 2 + (4 * kind + pair), s0, w), yf[:, 0:w],
                                                one(q_hi, i * 2 + (4 * kind + pair), s0, w).bitcast(F32), ALU.subtract).then_inc(y_low.sem, 1)

                    return tile_max, lower, divide, y

                for m in range(4):
                    functions(0)[0](m)
                with loop(e, 0, 2) as i:
                    dve_own.enter(i, sum(pieces(u) for u in range(NU)))
                    tile_max, lower, divide, y = functions(i)
                    for t in range(ST + LAG + 4 - both):
                        if t < ST:
                            for m in tiles_at(t):
                                tile_max(m)
                            lower(t)
                        for u in range(NU):
                            since = t - (end[2 * u + 1] - 1 + LAG)
                            if 0 <= since < pieces(u):
                                divide(u, since)
                            if since == pieces(u) - both:
                                y(u)
                    dve_own.leave(2)

            def pool(e):
                e.wait_ge(made.sem, made.base)
                e.wait_ge(scored.sem, scored.base)
                for p in range(PAIRS):
                    if p >= 2:
                        e.wait_ge(made.sem, made.base + (p - 1) * (ST // 2))
                    for dst, src in ((qh, q_hi), (ql, q_lo)):
                        e.dma_start(dst[:, p % 2, 0:wide], src[:, 4 * kind + p, 0:wide]).then_inc(q_here[p % 2].sem, 16)

            phase([(y_low, 2 * NU), (y_high, 2 * NU), (valued, 2 * ST), (low, 2 * ST), (maxed, 2 * MT + 4), (row_copied, 2 * NI + 1), (sunk, 0 if kind else 2 * NI + 1), (sink_high, 0 if kind else 2 * NI + 1), (q_here[0], 64), (q_here[1], 64)],
                  pe=pe, act=act, dve=dve, pool=pool, follows_on=kind == 1)

        def one(t, i, s0, n):
            return t[:, bass.ds(i, 1), s0:s0 + n].rearrange("p a n -> p (a n)")

        def merge(name, groups):
            nonlocal u0
            base = u0
            w = sum(n for _, n in groups)
            ga, gb, m1, m2 = r_s["ga"], r_s["gb"], r_kv["m1"], r_kv["m2"]
            g_here = signals("merge", by_dma=True, gates_here0=128, gates_here1=128)
            gated, mixed, high, low = signals("merge", gated=CH + 2, mixed=CH, high=CH, low=CH)

            def pe(e):
                e.sem_inc(gated.sem, 2)
                with loop(e, 0, 4) as i:
                    for j in range(2):
                        u = base + j
                        e.wait_ge(lo_ready, unit_at(u + 1, i, 2))
                        e.wait_ge(gated.sem, gated.base + i * 2 + j + 1)
                        linear(4 * j, u, groups, q_hi, q_lo, 4)
                        linear(4 * j + 2, u, groups, q_hi, q_lo, 4, first=4, act_first=4).then_inc(unit_done, 1)

            def act(e):
                with loop(e, 0, 4) as i:
                    for j in range(2):
                        split_hi(e, base + j + 1, i, 2)
                        e.wait_ge(mixed.sem, mixed.base + i * 2 + j + 1)
                        nc.scalar.activation(one(h_hi, i * 2 + j, 0, w), m1[:, j, 0:w], ACT.Copy).then_inc(high.sem, 1)

            def dve(e):
                with loop(e, 0, 4) as i:
                    dve_own.enter(i, 2)
                    for j in range(2):
                        u = base + j
                        split_lo(e, u + 1, i, 2)
                        e.wait_ge(unit_done, unit_at(u + 2, i, 2))
                        e.wait_ge(g_here[j].sem, g_here[j].base + i * 32 + 32)
                        b = 2048 * j
                        dve_own.link(e, nc.vector.tensor_tensor(m1[:, j, 0:w], psf[:, b:b + w], ga[:, j, 0:w], ALU.mult))
                        nc.vector.tensor_tensor(m2[:, j, 0:w], psf[:, b + 1024:b + 1024 + w], gb[:, j, 0:w], ALU.mult).then_inc(gated.sem, 1)
                        e.wait_ge(gated.sem, gated.base + i * 2 + j + 3)
                        nc.vector.tensor_tensor(m1[:, j, 0:w], m1[:, j, 0:w], m2[:, j, 0:w], ALU.add).then_inc(mixed.sem, 1)
                        e.wait_ge(high.sem, high.base + i * 2 + j + 1)
                        nc.vector.tensor_tensor(one(h_lo, i * 2 + j, 0, w), m1[:, j, 0:w],
                                                one(h_hi, i * 2 + j, 0, w).bitcast(F32), ALU.subtract).then_inc(low.sem, 1)
                    dve_own.leave(4)

            def pool(e):
                def load(n, j):
                    e.dma_start(ga[:, j, 0:w], gates[n, :, 0:w]).then_inc(g_here[j].sem, 16)
                    e.dma_start(gb[:, j, 0:w], gates[n + CH, :, 0:w]).then_inc(g_here[j].sem, 16)
                for n in range(CH):
                    if n >= 2:
                        e.wait_ge(gated.sem, gated.base + n + 1)
                    load(n, n % 2)

            u0 += N_MERGE
            phase([(unit_done, 1 + u0), (lo_ready, u0 + 1), (high, CH), (low, CH)], pe=pe, act=act, dve=dve, pool=pool)

        def add_to_x(name, groups, act_hi, act_lo, gate, chunks=CH, reload_x=False, plain=False, last=False):
            nonlocal u0
            base = u0
            added, = signals("add", added=CH + 4)
            x_here, = signals("add", by_dma=True, x_here=16 * reload_x)

            def steps(e, body):
                if last:
                    for k in range(2):
                        for j in range(4):
                            body(4 * k + j, None)
                else:
                    with loop(e, 0, 2) as i:
                        for j in range(4):
                            body(j, i)

            def n_at(j, i):
                return j if i is None else i * 4 + j

            def pe(e):
                e.sem_inc(added.sem, 4)
                def body(j, i):
                    e.wait_ge(lo_ready, unit_at(base + j + 1, i, 4))
                    e.wait_ge(added.sem, added.base + n_at(j, i) + 1)
                    linear(2 * (j % 4), base + j, groups, act_hi, act_lo, chunks).then_inc(unit_done, 1)
                steps(e, body)

            def act(e):
                def body(j, i):
                    if not (last and j == 7):
                        split_hi(e, base + j + 1, i, 4)
                steps(e, body)

            def dve(e):
                def body(j, i):
                    if not (last and j == 7):
                        split_lo(e, base + j + 1, i, 4)
                    e.wait_ge(unit_done, unit_at(base + j + 2, i, 4))
                    if reload_x and j % 4 == 0:
                        e.wait_ge(x_here.sem, x_here.base + 16)
                    for v, (s0, n) in enumerate(groups):
                        src = psf[:, 1024 * (j % 4) + s0:1024 * (j % 4) + s0 + n]
                        xc = x[:, j, s0:s0 + n] if i is None else one(x, i * 4 + j, s0, n)
                        if plain:
                            ins = nc.vector.tensor_tensor(xc, src, xc, ALU.add)
                        else:
                            m = mod[:, bass.ds(n_at(j, i) + gate * CH, 1), v]
                            ins = nc.vector.scalar_tensor_tensor(xc, src, m, xc, ALU.mult, ALU.add)
                    ins.then_inc(added.sem, 1)
                steps(e, body)

            def pool(e):
                if reload_x:
                    e.dma_start(x[:, :, :], x_keep).then_inc(x_here.sem, 16)

            u0 += CH
            phase([(unit_done, 1 + u0), (added, CH + 4)] + ([] if last else [(lo_ready, u0 + 1)]), pe=pe, act=act, dve=dve, pool=pool)

        def hidden(name, groups, nf):
            nonlocal u0
            base = u0
            w = sum(n for _, n in groups)
            su, ff = r_kv["su"], r_kv["ff"]
            silud, gated, high, low = signals("hidden", silu=nf, gated=nf + 2, high=nf, low=nf)

            def pe(e):
                e.sem_inc(gated.sem, 2)
                with loop(e, 0, nf // 2) as i:
                    for j in range(4):
                        u = base + j
                        e.wait_ge(lo_ready, unit_at(u + 1, i, 4))
                        if j % 2 == 0:
                            e.wait_ge(gated.sem, gated.base + i * 2 + j // 2 + 1)
                        linear(2 * j, u, groups, h_hi, h_lo, CH).then_inc(unit_done, 1)

            def act(e):
                with loop(e, 0, nf // 2) as i:
                    for j in range(4):
                        u, f = base + j, j // 2
                        split_hi(e, u + 1, i, 4)
                        if j % 2 == 0:
                            e.wait_ge(unit_done, unit_at(u + 2, i, 4))
                            e.wait_ge(gated.sem, gated.base + i * 2 + f + 1)
                            nc.scalar.activation(su[:, f, 0:w], psf[:, 1024 * j:1024 * j + w], ACT.Silu).then_inc(silud.sem, 1)
                        else:
                            e.wait_ge(gated.sem, gated.base + i * 2 + f + 3)
                            nc.scalar.activation(one(q_hi, i * 2 + f, 0, w), ff[:, f, 0:w], ACT.Copy).then_inc(high.sem, 1)

            def dve(e):
                with loop(e, 0, nf // 2) as i:
                    for j in range(4):
                        u, f = base + j, j // 2
                        split_lo(e, u + 1, i, 4)
                        if j % 2:
                            e.wait_ge(unit_done, unit_at(u + 2, i, 4))
                            e.wait_ge(silud.sem, silud.base + i * 2 + f + 1)
                            nc.vector.tensor_tensor(ff[:, f, 0:w], psf[:, 1024 * j:1024 * j + w], su[:, f, 0:w], ALU.mult).then_inc(gated.sem, 1)
                            e.wait_ge(high.sem, high.base + i * 2 + f + 1)
                            nc.vector.tensor_tensor(one(q_lo, i * 2 + f, 0, w), ff[:, f, 0:w],
                                                    one(q_hi, i * 2 + f, 0, w).bitcast(F32), ALU.subtract).then_inc(low.sem, 1)

            u0 += 2 * nf
            phase([(unit_done, 1 + u0), (lo_ready, u0 + 1), (low, nf), (high, nf)], pe=pe, act=act, dve=dve)

        cmp_raw = r_t["cmp_raw"]
        br, br_cols, kc_hi, kc_lo, vc_hi, vc_lo, cmp_s, cmp_n, kcf = (
            r_q1[n] for n in ("br", "br_cols", "kc_hi", "kc_lo", "vc_hi", "vc_lo", "cmp_s", "cmp_n", "kcf"))

        def compress():
            nonlocal u0
            base = u0
            w2, b1, hid, hid_t = (r_q2[n] for n in ("w2", "b1_rows", "hid", "hid_t"))
            kk, rf, r_hi, r_lo = r_s["kk"], r_s["rf"], r_h["r_hi"], r_h["r_lo"]
            here, = signals("cmp", by_dma=True, here=160)
            (zero, laid, high, low, hidden_, biased, silud, turned, taken, outs, sq_, stat, rough, cols_, kvh, kvl, brt, brc) = signals(
                "cmp", zero=8, laid=8, high=4, low=4, hidden=2, biased=2, silu=2, turned=2, taken=2, outs=2, sq=3,
                stat=2, rough=1, cols=1, kvh=4, kvl=4, br_turned=1, br_cols=1)

            def pool(e):
                e.dma_start(w2[:, :, :, :, :].rearrange("p a b c n -> p (a b c n)"), big[:, B_W2:B_W2 + 8 * P]).then_inc(here.sem, 16)
                e.dma_start(b1[:, :, :].rearrange("p a n -> p (a n)"), big[:, B_B1:B_B1 + 512]).then_inc(here.sem, 16)
                for kind in range(2):
                    for g in range(2):
                        e.dma_start(kk[0:64, 2 * kind + g, :], cmp_raw[64 * g:64 * g + 64, kind, :]).then_inc(here.sem, 16)
                        e.dma_start(kk[64:128, 2 * kind + g, 0:SEQ - 1], cmp_raw[64 * g:64 * g + 64, kind, 1:SEQ]).then_inc(here.sem, 16)

            def dve(e):
                for t in (r_hi[:, :, :, 62:P], r_lo[:, :, :, 62:P], kc_hi[:, :, :], kc_lo[:, :, :], vc_hi[:, :], vc_lo[:, :]):
                    nc.vector.memset(t.bitcast(F32), 0.0).then_inc(zero.sem, 1)
                e.wait_ge(here.sem, here.base + 160)
                for n in range(4):
                    kind, g = n // 2, n % 2
                    if n >= 2:
                        e.wait_ge(low.sem, low.base + n - 1)
                    v = kk[:, n, :].rearrange("p (i c) -> p c i", c=16)
                    for half in range(2):
                        pe_ = col("pe", 16 * kind + 8 * half, 8).unsqueeze(2).to_broadcast([P, 8, 31])
                        nc.vector.tensor_tensor(rf[:, g, 8 * half:8 * half + 8, :], v[:, 0:16:2, half:half + 31], pe_,
                                                ALU.add).then_inc(laid.sem, 1)
                    e.wait_ge(high.sem, high.base + n + 1)
                    e.wait_ge(laid.sem, laid.base + 2 * n + 2)
                    at = (slice(None), kind, slice(None), slice(31 * g, 31 * g + 31))
                    nc.vector.tensor_tensor(r_lo[at], rf[:, g], r_hi[at].bitcast(F32), ALU.subtract).then_inc(low.sem, 1)
                for kind in range(2):
                    for j in range(4):
                        split_lo(e, base + 4 * kind + j + 1)
                    e.wait_ge(unit_done, 1 + base + 4 * kind + 4)
                    nc.vector.tensor_tensor(hid[:, kind], ps[:, kind, 0:256], b1[:, kind], ALU.add).then_inc(biased.sem, 1)
                e.wait_ge(rough.sem, rough.base + 1)
                newton(e, ps[:, 6, 0:31], kcf[:, 2, 0:31], HD)
                nc.vector.scalar_tensor_tensor(kcf[:, 1, 0:31], kcf[:, 1, 0:31], col("kg2", 0), kcf[:, 2, 0:31], ALU.mult,
                                               ALU.mult).then_inc(cols_.sem, 1)
                e.wait_ge(kvh.sem, kvh.base + 4)
                for g in range(2):
                    rows = slice(64 * g, 64 * g + 64)
                    nc.vector.tensor_tensor(kc_lo[rows, g, 0:31], kcf[rows, 1, 0:31], kc_hi[rows, g, 0:31].bitcast(F32),
                                            ALU.subtract).then_inc(kvl.sem, 1)
                for g in range(2):
                    nc.vector.tensor_tensor(vc_lo[0:31, P * g:P * g + 64], ps[0:31, 7, 64 * g:64 * g + 64],
                                            vc_hi[0:31, P * g:P * g + 64].bitcast(F32), ALU.subtract).then_inc(kvl.sem, 1)

            def act(e):
                e.wait_ge(zero.sem, zero.base + 6)
                for n in range(4):
                    kind, g = n // 2, n % 2
                    e.wait_ge(laid.sem, laid.base + 2 * n + 2)
                    nc.scalar.activation(r_hi[:, kind, :, 31 * g:31 * g + 31], rf[:, g], ACT.Copy).then_inc(high.sem, 1)
                e.wait_ge(brt.sem, brt.base + 1)
                for qt in range(4):
                    act_own.link(e, nc.scalar.activation(br_cols[:, 3 - qt, :], ps[:, 7, qt * P:qt * P + 32], ACT.Copy))
                nc.scalar.activation(cmp_n[:, 0, :], br_cols[:, 0, 0:4], ACT.Copy).then_inc(brc.sem, 1)
                for kind in range(2):
                    for j in range(4):
                        split_hi(e, base + 4 * kind + j + 1)
                for kind in range(2):
                    e.wait_ge(biased.sem, biased.base + kind + 1)
                    nc.scalar.activation(hid[:, kind], hid[:, kind], ACT.Silu).then_inc(silud.sem, 1)
                for kind in range(2):
                    e.wait_ge(turned.sem, turned.base + kind + 1)
                    nc.scalar.activation(hid_t[:, kind, :, :], ps[:, 2 + kind, 0:256].rearrange("p (a n) -> p a n", a=2),
                                         ACT.Copy).then_inc(taken.sem, 1)
                e.wait_ge(outs.sem, outs.base + 2)
                nc.scalar.activation(kcf[:, 0, 0:31], ps[:, 4, 0:31], ACT.Square).then_inc(sq_.sem, 1)
                nc.scalar.activation(kcf[:, 1, 0:31], ps[:, 4, 0:31], ACT.Copy).then_inc(sq_.sem, 1)
                nc.scalar.activation(kcf[:, 4, 0:31], ps[:, 5, 0:31], ACT.Copy).then_inc(sq_.sem, 1)
                e.wait_ge(stat.sem, stat.base + 2)
                act_own.link(e, nc.scalar.activation(kcf[:, 2, 0:31], ps[:, 6, 0:31], ACT.Ln, scale=1.0 / HD, bias=col("eps")))
                nc.scalar.activation(kcf[:, 2, 0:31], kcf[:, 2, 0:31], ACT.Exp, scale=-0.5).then_inc(rough.sem, 1)
                e.wait_ge(cols_.sem, cols_.base + 1)
                for g in range(2):
                    rows = slice(64 * g, 64 * g + 64)
                    nc.scalar.activation(kc_hi[rows, g, 0:31], kcf[rows, 1, 0:31], ACT.Copy).then_inc(kvh.sem, 1)
                for g in range(2):
                    nc.scalar.activation(vc_hi[0:31, P * g:P * g + 64], ps[0:31, 7, 64 * g:64 * g + 64], ACT.Copy).then_inc(kvh.sem, 1)

            def pe(e):
                for qt in range(4):
                    mm = nc.tensor.transpose(ps[:, 7, qt * P:(qt + 1) * P], br[:, qt * P:(qt + 1) * P], ident)
                mm.then_inc(brt.sem, 1)
                e.wait_ge(zero.sem, zero.base + 6)
                for kind in range(2):
                    e.wait_ge(low.sem, low.base + 2 * kind + 2)
                    for j in range(4):
                        u = base + 4 * kind + j
                        e.wait_ge(lo_ready, u + 1)
                        for k in range(4):
                            m, w = 4 * j + k, slice(256 * k, 256 * k + 256)
                            mm = three(ps[:, kind, 0:256], r_hi[:, kind, m, :], r_lo[:, kind, m, :], w_hi[:, u % 2, w],
                                       w_lo[:, u % 2, w], m == 0, m == 15)
                        mm.then_inc(unit_done, 1)
                for kind in range(2):
                    e.wait_ge(silud.sem, silud.base + kind + 1)
                    for ht in range(2):
                        mm = nc.tensor.transpose(ps[:, 2 + kind, ht * P:(ht + 1) * P], hid[:, kind, ht * P:(ht + 1) * P], ident)
                    mm.then_inc(turned.sem, 1)
                for kind in range(2):
                    e.wait_ge(taken.sem, taken.base + kind + 1)
                    for n in range(4):
                        g, ht = n // 2, n % 2
                        mm = nc.tensor.matmul(ps[:, 4 + kind, 0:31], w2[:, kind, ht, g, :], hid_t[:, kind, ht, 31 * g:31 * g + 31],
                                              start=n == 0, stop=n == 3)
                    mm.then_inc(outs.sem, 1)
                e.wait_ge(sq_.sem, sq_.base + 3)
                nc.tensor.matmul(ps[:, 6, 0:31], bones, kcf[:, 0, 0:31], start=True, stop=True).then_inc(stat.sem, 1)
                e.wait_ge(brc.sem, brc.base + 1)
                nc.tensor.transpose(ps[0:31, 7, 0:P], kcf[:, 4, 0:31], ident).then_inc(stat.sem, 1)

            u0 += N_CMP
            phase([(unit_done, 1 + u0), (lo_ready, u0 + 1), (kvl, 4), (kvh, 4), (cols_, 1), (brc, 1), (low, 4), (zero, 6)],
                  pe=pe, act=act, dve=dve, pool=pool)

        def sparse_attention():
            k_hi, k_lo, v_hi, v_lo = (r_kv[n] for n in ("k_hi", "k_lo", "v_hi", "v_lo"))
            s_hi, s_lo, sc_hi, sc_lo = (r_h[n] for n in ("s_hi", "s_lo", "sc_hi", "sc_lo"))
            qh, ql, bias = r_x["q2_hi"], r_x["q2_lo"], r_x["bias"]
            pr, gn, yf = r_s["pr2"], r_s["gn"], r_s["yf"]
            M, VH = 32, 8
            here = signals("nsa", by_dma=True, here0=5 * 32, here1=5 * 32)
            stored, = signals("nsa", by_dma=True, stored=128)
            (scored, placed, shifted, expd, scaled, turned, high, low, summed, y_ready, y_high, y_low) = signals(
                "nsa", scored=2 * M, placed=2 * M, shifted=2 * M, exp=2 * M, scaled=2 * M, turned=2 * M, high=2 * M, low=2 * M,
                summed=2 * VH, y_ready=4, y_high=4, y_low=4)
            (c_scored, c_shifted, c_exp, c_scaled, c_turned, c_high, c_low) = signals(
                "nsa_cmp", scored=8, shifted=8, exp=8, scaled=8, turned=8, high=8, low=8)

            def step(n):
                return n // 16, (n // 8) % 2, (n // 4) % 2, n % 4, n // 4

            def pe(e):
                with loop(e, 0, 2) as i:
                    def cmp_scores(hd):
                        pair, g = hd // 2, hd % 2
                        if g == 0:
                            e.wait_ge(here[pair].sem, here[pair].base + i * 80 + 80)
                        e.wait_ge(c_shifted.sem, c_shifted.base + i * 4 + hd)
                        for qt in range(4):
                            q = slice(qt * P, (qt + 1) * P)
                            mm = three(ps[:, 4, (3 - qt) * 32:(4 - qt) * 32], qh[:, pair, q], ql[:, pair, q], kc_hi[:, g, :],
                                       kc_lo[:, g, :], True, True)
                        mm.then_inc(c_scored.sem, 1)

                    def cmp_turn(hd):
                        e.wait_ge(c_scaled.sem, c_scaled.base + i * 4 + hd + 1)
                        e.wait_ge(c_low.sem, c_low.base + i * 4 + hd)
                        for qt in range(4):
                            mm = nc.tensor.transpose(ps[0:32, 5, qt * P:(qt + 1) * P], cmp_s[:, 3 - qt, :], ident)
                        mm.then_inc(c_turned.sem, 1)

                    def scores(n):
                        pair, g, b, qt, v = step(n)
                        e.wait_ge(placed.sem, placed.base + i * M + max(n - 1, 0))
                        w = (qt + 1) * P
                        q = slice(qt * P, w)
                        three(ps[:, n % 2, 0:w], qh[:, pair, q], ql[:, pair, q], k_hi[:, 2 * b + g, 0:w], k_lo[:, 2 * b + g, 0:w],
                              True, True).then_inc(scored.sem, 1)

                    def turn(n):
                        pair, g, b, qt, v = step(n)
                        e.wait_ge(scaled.sem, scaled.base + i * M + n + 1)
                        e.wait_ge(low.sem, low.base + i * M + max(n - 1, 0))
                        for kt in range(qt + 1):
                            mm = nc.tensor.transpose(ps[:, 2 + n % 2, kt * P:(kt + 1) * P], pr[:, n % 3, kt * P:(kt + 1) * P], ident)
                        mm.then_inc(turned.sem, 1)

                    def values(v):
                        pair, g, b = v // 4, (v // 2) % 2, v % 2
                        e.wait_ge(low.sem, low.base + i * M + 4 * (v + 1))
                        terms = []
                        if b == 0:
                            e.wait_ge(c_low.sem, c_low.base + i * 4 + v // 2 + 1)
                            if g == 0:
                                e.wait_ge(y_ready.sem, y_ready.base + i * 2 + pair)
                            hb = (v // 2) % 2
                            for vv, pp in ((vc_hi, sc_hi), (vc_hi, sc_lo), (vc_lo, sc_hi)):
                                terms.append((ps[:, 6, :], vv[0:32, 64 * g:64 * g + P], pp[0:32, hb, :]))
                        for kt in range(4):
                            for vv, pp in ((v_hi, s_hi), (v_hi, s_lo), (v_lo, s_hi)):
                                terms.append((ps[:, 6, kt * P:], vv[:, b, kt, 64 * g:64 * g + P], pp[:, v % 2, kt, kt * P:]))
                        for m, (o, l, r) in enumerate(terms):
                            mm = nc.tensor.matmul(o, l, r, start=(v % 4 == 0 and m == 0), stop=(v % 4 == 3 and m == len(terms) - 1))
                        mm.then_inc(summed.sem, 1)

                    cmp_scores(0)
                    scores(0)
                    scores(1)
                    for n in range(M):
                        if n + 2 < M:
                            if n % 8 == 6:
                                cmp_scores((n + 2) // 8)
                            scores(n + 2)
                        turn(n)
                        if n % 8 == 2:
                            cmp_turn(n // 8)
                        if n % 4 == 1 and n >= 4:
                            values(n // 4 - 1)
                    values(7)

            def act(e):
                with loop(e, 0, 2) as i:
                    def exp(n):
                        w = (step(n)[3] + 1) * P
                        e.wait_ge(shifted.sem, shifted.base + i * M + n + 1)
                        nc.scalar.activation(pr[:, n % 3, 0:w], pr[:, n % 3, 0:w], ACT.Exp, bias=small[:, n % 4:n % 4 + 1],
                                             accum_out=small[:, 4 + n % 4:5 + n % 4]).then_inc(expd.sem, 1)

                    def take(n):
                        pair, g, b, qt, v = step(n)
                        e.wait_ge(turned.sem, turned.base + i * M + n + 1)
                        e.wait_ge(summed.sem, summed.base + i * VH + max(v - 1, 0))
                        nc.scalar.activation(s_hi[:, v % 2, 0:qt + 1, qt * P:(qt + 1) * P],
                                             ps[:, 2 + n % 2, 0:(qt + 1) * P].rearrange("p (b n) -> p b n", b=qt + 1),
                                             ACT.Copy).then_inc(high.sem, 1)

                    def cmp(hd):
                        e.wait_ge(c_shifted.sem, c_shifted.base + i * 4 + hd + 1)
                        nc.scalar.activation(cmp_s[:, :, :], cmp_s[:, :, :], ACT.Exp).then_inc(c_exp.sem, 1)

                    def cmp_take(hd):
                        e.wait_ge(c_turned.sem, c_turned.base + i * 4 + hd + 1)
                        e.wait_ge(summed.sem, summed.base + i * VH + max(2 * hd - 3, 0))
                        nc.scalar.activation(sc_hi[0:32, hd % 2, :], ps[0:32, 5, :], ACT.Copy).then_inc(c_high.sem, 1)

                    def y(pair):
                        e.wait_ge(y_ready.sem, y_ready.base + i * 2 + pair + 1)
                        nc.scalar.activation(qh[:, pair, :], yf[:, :], ACT.Copy).then_inc(y_high.sem, 1)

                    for n in range(M):
                        if n % 8 == 0:
                            cmp(n // 8)
                        if n == 0:
                            exp(0)
                        if n + 1 < M:
                            exp(n + 1)
                        if n:
                            take(n - 1)
                        if n % 8 == 3:
                            cmp_take(n // 8)
                        if n == 18:
                            y(0)
                    take(M - 1)
                    y(1)

            def dve(e):
                with loop(e, 0, 2) as i:
                    dve_own.enter(i, 4 * 6 + 2 * M)
                    bc = lambda t: t.unsqueeze(2).to_broadcast([P, 4, 32])

                    def shift(n):
                        pair, g, b, qt, v = step(n)
                        w = (qt + 1) * P
                        e.wait_ge(scored.sem, scored.base + i * M + n + 1)
                        e.wait_ge(turned.sem, turned.base + i * M + max(n - 2, 0))
                        nc.vector.tensor_tensor(pr[:, n % 3, 0:w], ps[:, n % 2, 0:w], bias[:, pair, g, 384 - qt * P:SEQ],
                                                ALU.add).then_inc(placed.sem, 1)
                        e.wait_ge(placed.sem, placed.base + i * M + n + 1)
                        nc.vector.tensor_reduce(small[:, n % 4:n % 4 + 1], pr[:, n % 3, 0:w], AX_X, ALU.max, negate=True).then_inc(shifted.sem, 1)

                    def scale(n):
                        pair, g, b, qt, v = step(n)
                        w = (qt + 1) * P
                        e.wait_ge(expd.sem, expd.base + i * M + n + 1)
                        rr = small[:, 12 + n % 4:13 + n % 4]
                        dve_own.link(e, nc.vector.reciprocal(rr, small[:, 4 + n % 4:5 + n % 4]))
                        dve_own.link(e, nc.vector.tensor_tensor(
                            rr, rr, br_cols[:, 3 - qt, bass.ds(i * 2 + (8 * (b + 1) + 4 * g + pair), 1)], ALU.mult))
                        nc.vector.tensor_scalar(pr[:, n % 3, 0:w], pr[:, n % 3, 0:w], rr, None, ALU.mult).then_inc(scaled.sem, 1)

                    def take(n):
                        pair, g, b, qt, v = step(n)
                        e.wait_ge(high.sem, high.base + i * M + n + 1)
                        at = (slice(None), v % 2, slice(0, qt + 1), slice(qt * P, (qt + 1) * P))
                        nc.vector.tensor_tensor(s_lo[at], ps[:, 2 + n % 2, 0:(qt + 1) * P].rearrange("p (b n) -> p b n", b=qt + 1),
                                                s_hi[at].bitcast(F32), ALU.subtract).then_inc(low.sem, 1)

                    def cmp_shift(hd):
                        pair, g = hd // 2, hd % 2
                        wc = bias_of(pair, g)
                        e.wait_ge(c_scored.sem, c_scored.base + i * 4 + hd + 1)
                        e.wait_ge(c_turned.sem, c_turned.base + i * 4 + hd)
                        dve_own.link(e, nc.vector.tensor_tensor(cmp_s[:, :, :], ps[:, 4, 0:P].rearrange("p (r c) -> p r c", r=4), wc, ALU.add))
                        dve_own.link(e, nc.vector.tensor_reduce(cmp_n[:, 0, :], cmp_s[:, :, :], AX_X, ALU.max))
                        nc.vector.tensor_tensor(cmp_s[:, :, :], cmp_s[:, :, :], bc(cmp_n[:, 0, :]), ALU.subtract).then_inc(c_shifted.sem, 1)

                    def cmp_scale(hd):
                        pair, g = hd // 2, hd % 2
                        e.wait_ge(c_exp.sem, c_exp.base + i * 4 + hd + 1)
                        dve_own.link(e, nc.vector.tensor_reduce(cmp_n[:, 1, :], cmp_s[:, :, :], AX_X, ALU.add))
                        dve_own.link(e, nc.vector.reciprocal(cmp_n[:, 2, :], cmp_n[:, 1, :]))
                        dve_own.link(e, nc.vector.tensor_tensor(
                            cmp_n[:, 3, :], cmp_n[:, 2, :],
                            br_cols[:, :, bass.ds(i * 2 + (4 * g + pair), 1)].rearrange("p r a -> p (r a)"), ALU.mult))
                        dve_own.link(e, nc.vector.scalar_tensor_tensor(cmp_s[:, :, :], bias_of(pair, g), NEG / 2, cmp_s[:, :, :],
                                                                       ALU.is_gt, ALU.mult))
                        nc.vector.tensor_tensor(cmp_s[:, :, :], cmp_s[:, :, :], bc(cmp_n[:, 3, :]), ALU.mult).then_inc(c_scaled.sem, 1)

                    def cmp_take(hd):
                        e.wait_ge(c_high.sem, c_high.base + i * 4 + hd + 1)
                        nc.vector.tensor_tensor(sc_lo[0:32, hd % 2, :], ps[0:32, 5, :], sc_hi[0:32, hd % 2, :].bitcast(F32),
                                                ALU.subtract).then_inc(c_low.sem, 1)

                    def y(pair):
                        e.wait_ge(summed.sem, summed.base + i * VH + 4 * pair + 4)
                        e.wait_ge(y_low.sem, y_low.base + i * 2 + pair)
                        nc.vector.tensor_tensor(yf[:, :], ps[:, 6, :], gn[:, pair, :], ALU.mult).then_inc(y_ready.sem, 1)
                        e.wait_ge(y_high.sem, y_high.base + i * 2 + pair + 1)
                        nc.vector.tensor_tensor(ql[:, pair, :], yf[:, :], qh[:, pair, :].bitcast(F32), ALU.subtract).then_inc(y_low.sem, 1)

                    cmp_shift(0)
                    shift(0)
                    shift(1)
                    for n in range(M):
                        scale(n)
                        if n % 8 == 7 and n + 1 < M:
                            cmp_shift((n + 1) // 8)
                        if n + 2 < M:
                            shift(n + 2)
                        if n:
                            take(n - 1)
                        if n % 8 == 1:
                            cmp_scale(n // 8)
                        if n % 8 == 3:
                            cmp_take(n // 8)
                        if n == 18:
                            y(0)
                    take(M - 1)
                    y(1)
                    dve_own.leave(2)

            def bias_of(pair, g):
                at = (pair * 2 + g) * W_LEN + 31
                return bass.AP(bias, at, [[4 * W_LEN, P], [P, 4], [16, 32]])

            def pool(e):
                def store(p):
                    e.wait_ge(y_low.sem, y_low.base + p + 1)
                    for dst, src in ((q_hi, qh), (q_lo, ql)):
                        e.dma_start(dst[:, p, 0:SEQ], src[:, p % 2, :]).then_inc(stored.sem, 16)

                for p in range(PAIRS):
                    s = p % 2
                    if p >= 2:
                        store(p - 2)
                        e.wait_ge(stored.sem, stored.base + 32 * (p - 1))
                    for dst, src in ((qh, q_hi), (ql, q_lo)):
                        e.dma_start(dst[:, s, :], src[:, p, 0:SEQ]).then_inc(here[s].sem, 16)
                    for g in range(2):
                        rows = bias_mem[4 * g + p].rearrange("p l -> (p l)")[P - 1:P - 1 + P * RV_LEN].rearrange("(p l) -> p l", p=P)
                        e.dma_start(bias[:, s, g, :], rows[:, 0:W_LEN]).then_inc(here[s].sem, 16)
                    e.dma_start(gn[:, s, :], gates[16 + p, :, 0:SEQ]).then_inc(here[s].sem, 16)
                store(2)
                store(3)

            phase([(stored, 128), (y_low, 4), (y_high, 4), (summed, 16), (low, 2 * M), (c_low, 8), (here[0], 160), (here[1], 160)],
                  pe=pe, act=act, dve=dve, pool=pool)

        def recurrence():
            nonlocal u0
            base = u0
            u, gl, uc, uc_hi, uc_lo, sp = (r_kv[n] for n in ("u", "gl", "uc", "uc_hi", "uc_lo", "sp"))
            rg, ig, a, th, aa, hh = (r_h[n] for n in ("rg", "ig", "a", "th", "aa", "hh"))
            here, = signals("lru", by_dma=True, here=32)
            abs_exp, sp_done, conv, split, split2, blocks, gated, powers, tanhs, driven, one_less, root, scanned, y_, yh, yl = signals(
                "lru", exp=1, softplus=1, conv=16, split=4, split2=4, blocks=3, gates=8, powers=8, tanh=4, driven=4, one_less=4,
                root=4, scanned=4, y=4, yh=4, yl=4)

            def pool(e):
                e.dma_start(u[:, :, :], gates[20:24, :, 0:SEQ].rearrange("c p n -> p c n")).then_inc(here.sem, 16)
                e.dma_start(gl[:, :, :], gates[24:28, :, 0:SEQ].rearrange("c p n -> p c n")).then_inc(here.sem, 16)

            def pe(e):
                e.wait_ge(lo_ready, base + 1)
                s = base % 2
                for c in range(4):
                    e.wait_ge(split2.sem, split2.base + c + 1)
                    for k in range(2):
                        w = slice((4 * k + c) * P, (4 * k + c + 1) * P)
                        mm = three(ps[:, 2 * c + k, :], w_hi[:, s, w], w_lo[:, s, w], uc_hi[:, c, :], uc_lo[:, c, :], True, True)
                    mm.then_inc(blocks.sem if c < 3 else unit_done, 1)

            def act(e):
                az, ex, lam = sp[:, 0, :], sp[:, 1, :], col("lam", 0, 4)
                act_own.link(e, nc.scalar.activation(az, lam, ACT.Abs))
                nc.scalar.activation(ex, az, ACT.Exp, scale=-1.0).then_inc(abs_exp.sem, 1)
                split_hi(e, base + 1)
                for c in range(4):
                    e.wait_ge(conv.sem, conv.base + 4 * (c + 1))
                    nc.scalar.activation(uc_hi[:, c, :], uc[:, c, :], ACT.Copy).then_inc(split.sem, 1)
                for c in range(4):
                    if c < 3:
                        e.wait_ge(blocks.sem, blocks.base + c + 1)
                    else:
                        e.wait_ge(unit_done, 1 + base + 1)
                    nc.scalar.activation(ig[:, c, :], ps[:, 2 * c + 1, :], ACT.Sigmoid, bias=col("bx", c)).then_inc(gated.sem, 1)
                    nc.scalar.activation(rg[:, c, :], ps[:, 2 * c, :], ACT.Sigmoid, bias=col("ba", c)).then_inc(gated.sem, 1)
                e.wait_ge(sp_done.sem, sp_done.base + 1)
                for c in range(4):
                    if c == 0:
                        e.wait_ge(gated.sem, gated.base + 8)
                    nc.scalar.activation(aa[:, c, :], rg[:, c, :], ACT.Exp, scale=sp[:, 6, c:c + 1]).then_inc(powers.sem, 1)
                    nc.scalar.activation(a[:, c, :], rg[:, c, :], ACT.Exp, scale=sp[:, 5, c:c + 1]).then_inc(powers.sem, 1)
                for c in range(4):
                    nc.scalar.activation(th[:, c, :], rg[:, c, :], ACT.Tanh, scale=sp[:, 7, c:c + 1]).then_inc(tanhs.sem, 1)
                for c in range(4):
                    e.wait_ge(one_less.sem, one_less.base + c + 1)
                    nc.scalar.activation(aa[:, c, :], aa[:, c, :], ACT.Sqrt).then_inc(root.sem, 1)
                for c in range(4):
                    e.wait_ge(y_.sem, y_.base + c + 1)
                    nc.scalar.activation(q_hi[:, 4 + c, 0:SEQ], hh[:, c, :], ACT.Copy).then_inc(yh.sem, 1)

            def dve(e):
                T = nc.vector
                own = lambda ins: dve_own.link(e, ins)
                lam, ex, s1, s2, po = col("lam", 0, 4), sp[:, 1, :], sp[:, 2, :], sp[:, 3, :], sp[:, 4, :]
                split_lo(e, base + 1)
                e.wait_ge(here.sem, here.base + 32)
                cw = lambda c, k: col("convw", 4 * c + k)
                for c in range(4):
                    T.tensor_scalar(uc[:, c, :], u[:, c, :], cw(c, 3), col("convb", c), ALU.mult, ALU.add).then_inc(conv.sem, 1)
                    for k in range(3):
                        d = 3 - k
                        e.wait_ge(conv.sem, conv.base + 4 * c + k + 1)
                        T.scalar_tensor_tensor(uc[:, c, d:], u[:, c, 0:SEQ - d], cw(c, k), uc[:, c, d:], ALU.mult,
                                               ALU.add).then_inc(conv.sem, 1)
                    if c:
                        lower(e, c - 1)
                lower(e, 3)
                e.wait_ge(abs_exp.sem, abs_exp.base + 1)
                own(T.tensor_scalar(s2, ex, 2.0, None, ALU.add))
                own(T.reciprocal(s2, s2))
                own(T.tensor_tensor(s1, ex, s2, ALU.mult))
                own(T.tensor_tensor(s2, s1, s1, ALU.mult))
                own(T.tensor_scalar(po, s2, 1.0 / 15, 1.0 / 13, ALU.mult, ALU.add))
                for k in (11, 9, 7, 5, 3, 1):
                    own(T.tensor_tensor(po, po, s2, ALU.mult))
                    own(T.tensor_scalar(po, po, 1.0 / k, None, ALU.add))
                own(T.scalar_tensor_tensor(po, po, 2.0, s1, ALU.mult, ALU.mult))
                own(T.tensor_scalar(s1, lam, -1.0, 0.0, ALU.mult, ALU.max))
                own(T.tensor_tensor(po, po, s1, ALU.add))
                own(T.tensor_scalar(sp[:, 5, :], po, -LRU_C, None, ALU.mult))
                own(T.tensor_scalar(sp[:, 6, :], po, -2 * LRU_C, None, ALU.mult))
                T.tensor_scalar(sp[:, 7, :], po, LRU_C, None, ALU.mult).then_inc(sp_done.sem, 1)
                for c in range(4):
                    e.wait_ge(gated.sem, gated.base + 2 * c + 1)
                    T.tensor_tensor(ig[:, c, :], ig[:, c, :], uc[:, c, :], ALU.mult).then_inc(driven.sem, 1)
                for c in range(4):
                    e.wait_ge(powers.sem, powers.base + 2 * c + 1)
                    e.wait_ge(tanhs.sem, tanhs.base + c + 1)
                    T.scalar_tensor_tensor(aa[:, c, :], aa[:, c, :], 1.0, th[:, c, :], ALU.add, ALU.mult).then_inc(one_less.sem, 1)
                for c in range(4):
                    e.wait_ge(driven.sem, driven.base + c + 1)
                    e.wait_ge(root.sem, root.base + c + 1)
                    own(T.tensor_tensor(ig[:, c, :], ig[:, c, :], aa[:, c, :], ALU.mult))
                    e.wait_ge(powers.sem, powers.base + 2 * c + 2)
                    T.tensor_tensor_scan(hh[:, c, :], a[:, c, :], ig[:, c, :], 0.0, ALU.mult, ALU.add).then_inc(scanned.sem, 1)
                    e.wait_ge(scanned.sem, scanned.base + c + 1)
                    T.tensor_tensor(hh[:, c, :], hh[:, c, :], gl[:, c, :], ALU.mult).then_inc(y_.sem, 1)
                    if c:
                        out_low(e, c - 1)
                out_low(e, 3)

            def lower(e, c):
                e.wait_ge(split.sem, split.base + c + 1)
                nc.vector.tensor_tensor(uc_lo[:, c, :], uc[:, c, :], uc_hi[:, c, :].bitcast(F32), ALU.subtract).then_inc(split2.sem, 1)

            def out_low(e, c):
                e.wait_ge(yh.sem, yh.base + c + 1)
                nc.vector.tensor_tensor(q_lo[:, 4 + c, 0:SEQ], hh[:, c, :], q_hi[:, 4 + c, 0:SEQ].bitcast(F32),
                                        ALU.subtract).then_inc(yl.sem, 1)

            u0 += 1
            phase([(yl, 4), (yh, 4), (unit_done, 1 + u0), (lo_ready, u0 + 1), (here, 32)], pe=pe, act=act, dve=dve, pool=pool)

        def second_block():
            lat = [LAT]
            sc = HD ** -0.5
            steps = [
                lambda: norm(lat, lambda c, v: col_at("gf", c), None, out_f32=True),
                lambda: norm(lat, lambda c, v: col_at("ng2", c), lambda c, v: 0.0),
                lambda: project([("raw", cmp_raw[:, 0, :], SEQ, None, False, ACT.Copy), ("raw", cmp_raw[:, 1, :], SEQ, None, False, ACT.Copy),
                                 ("k", 0, SEQ, col("kg2", 1), False, 1.0), ("v", 0, SEQ, None, False, 1.0),
                                 ("k", 1, SEQ, col("kg2", 2), False, 1.0), ("v", 1, SEQ, None, False, 1.0)]
                                + [("q", j, SEQ, col("qg2"), False, sc) for j in range(4)]
                                + [("raw", br[:, :], SEQ, None, False, ACT.Sigmoid)], 0.0),
                lambda: gate_tiles("gates_2", lat, [(ACT.Sigmoid, 4), (ACT.Silu, 1), (ACT.Copy, 1), (ACT.Silu, 1)]),
                compress, sparse_attention, recurrence,
                lambda: merge("merge_2", lat),
                lambda: add_to_x("out_2", lat, h_hi, h_lo, 0, reload_x=True, plain=True, last=True)]
            for step in steps:
                step()

        for layer in range(DEPTH):
            both = [LAT, CON]
            mine = both if layer == 0 else [LAT]
            steps = [
                lambda: ada(layer, relative_bias() if layer == 0 else ({}, [])),
                lambda: norm(both, lambda c, v: aff[:, 0, bass.ds(c, 1), v], lambda c, v: mod[:, bass.ds(c, 1), v]),
                lambda: project(layer_tiles(layer, layer == 0), 1.0),
                lambda: gate_tiles(f"gates{layer}", mine, [(ACT.Sigmoid, N_GATE // 4)]),
                lambda: attention(layer, 0, layer == 0),
                lambda: attention(layer, 1, layer == 0),
                lambda: merge(f"merge{layer}", mine),
                lambda: add_to_x(f"out{layer}", mine, h_hi, h_lo, 2, reload_x=True),
                lambda: norm(mine, lambda c, v: aff[:, 1, bass.ds(c, 1), v],
                             lambda c, v: mod[:, bass.ds(c + 3 * CH, 1), v])]
            for part, nf in enumerate(FF_PARTS):
                steps += [lambda part=part, nf=nf: hidden(f"hidden{layer}_{part}", mine, nf),
                          lambda part=part, nf=nf: add_to_x(f"down{layer}_{part}", mine, q_hi, q_lo, 5, chunks=nf)]
            for step in steps:
                step()
        second_block()
        assert u0 == N_UNITS

        out_done = sem("out_done")
        block = ctx.enter_context(nc.Block())

        def run(e, name):
            for k, (engines, _, follows_on) in enumerate(phases):
                if name in engines and follows_on:
                    engines[name](e)
                elif name in engines:
                    for s, v in (phases[k - 1][1] if k else []):
                        if v:
                            e.wait_ge(s, v)
                    engines[name](e)

        @block.sync
        def _(e):
            for s in range(2):
                e.dma_start(raw[:, s, :], stream[s]).then_inc(raw_loaded[s], 16)
            with e.Fori(1, N_UNITS // 2) as i:
                for s in range(2):
                    e.wait_ge(lo_ready, i * 2 + (s - 1))
                    e.dma_start(raw[:, s, :], stream[bass.ds(i * 2 + s, 1)].rearrange("a p n -> p (a n)")).then_inc(raw_loaded[s], 16)
            for s in range(2):
                e.wait_ge(raw_loaded[s], 8 * N_UNITS)

        @block.gpsimd
        def _(e):
            for counter in [unit_done] + from_one:
                e.sem_inc(counter, 1)
            run(e, "pool")
            for s, v in phases[-1][1]:
                e.wait_ge(s, v)
            e.dma_start(out, x[:, :, 0:SEQ]).then_inc(out_done, 16)
            e.wait_ge(out_done, 16)

        @block.scalar
        def _(e):
            run(e, "act")

        @block.vector
        def _(e):
            run(e, "dve")

        @block.tensor
        def _(e):
            run(e, "pe")


PAIR = [[64 * j + r for r in range(64)] + [256 + 64 * j + r for r in range(64)] for j in range(PAIRS)]


def unit_of(w):
    c = w.shape[0] // P
    t = w.reshape(c, P, w.shape[1]).transpose(1, 0, 2).reshape(P, -1)
    if t.shape[1] < UNIT:
        t = np.concatenate([t, np.zeros((P, UNIT - t.shape[1]), np.float32)], axis=1)
    return t


def layer_units(a, l):
    w = a["w_in"][l]
    for at in (512, 640, 1280, 1408):
        yield unit_of(w[:, at:at + P])
    for at in (0, 768):
        for j in range(PAIRS):
            yield unit_of(w[:, [at + r for r in PAIR[j]]])
    for n in range(16):
        yield unit_of(w[:, 1536 + P * n:1536 + P * n + P])
    rows = sum(PAIR, [])
    for n in range(8):
        c = slice(P * n, P * n + P)
        yield np.concatenate([unit_of(a["w_proj_a"][l][rows][:, c])[:, :512], unit_of(a["w_proj_b"][l][rows][:, c])[:, :512]], axis=1)
    for n in range(8):
        yield unit_of(a["w_out"][l][:, P * n:P * n + P])
    f0 = 0
    for nf in FF_PARTS:
        for f in range(f0, f0 + nf):
            yield unit_of(a["w_ffn_gate"][l][:, P * f:P * f + P])
            yield unit_of(a["w_ffn_up"][l][:, P * f:P * f + P])
        for n in range(8):
            yield unit_of(a["w_ffn_down"][l][P * f0:P * (f0 + nf), P * n:P * n + P])
        f0 += nf


def second_units(a):
    w = a["w_in_2"]
    for at in range(512, 1280, P):
        yield unit_of(w[:, at:at + P])
    for j in range(PAIRS):
        yield unit_of(w[:, PAIR[j]])
    yield unit_of(np.concatenate([w[:, 1792:1816], np.zeros((D, P - 24), np.float32)], axis=1))
    for n in range(16):
        yield unit_of(w[:, 2840 + P * n:2840 + P * n + P])
    for j in range(PAIRS):
        yield unit_of(w[:, [1280 + r for r in PAIR[j]]])
    for at in (1816, 2328):
        for n in range(4):
            yield unit_of(w[:, at + P * n:at + P * n + P])
    for kind in range(2):
        for m in range(4):
            yield unit_of(a["cmp_w1_2"][kind][512 * m:512 * m + 512])
    blocks = np.zeros((8, P, P), np.float32)
    for n in range(8):
        at = slice(64 * (n % 2), 64 * (n % 2) + 64)
        blocks[n // 2, at, at] = a["lru_wa_2"][n]
        blocks[4 + n // 2, at, at] = a["lru_wx_2"][n]
    yield unit_of(blocks.reshape(8 * P, P))
    rows = sum(PAIR, [])
    for n in range(8):
        c = slice(P * n, P * n + P)
        yield np.concatenate([unit_of(a["w_proj_a_2"][rows][:, c])[:, :512], unit_of(a["w_proj_b_2"][:, c])[:, :512]], axis=1)
    for n in range(8):
        yield unit_of(a["w_out_2"][:, P * n:P * n + P])


def columns(v):
    return v.reshape(-1, P).T


def twice(m):
    return np.stack([m, m], axis=2).reshape(P, -1)


def every(v):
    return np.broadcast_to(v.reshape(1, -1), (P, v.size))


def table(a):
    t = np.zeros((P, COLS["all"][1]), np.float32)

    def put(name, v, at=0):
        v = np.asarray(v)
        t[:, COLS[name][0] + at:COLS[name][0] + at + v.shape[1]] = v

    put("ident", np.eye(P, dtype=np.float32))
    put("ones", np.ones((P, P), np.float32))
    b = np.zeros((P, P), np.float32)
    b[:64, :64] = b[64:, 64:] = 1
    put("bones", b)
    s = np.zeros((P, 2), np.float32)
    s[0, 0] = s[1, 1] = s[2, 0] = s[3, 1] = 1
    put("sel", s)
    put("eps", np.full((P, 1), EPS, np.float32))
    put("c", np.stack([columns(a["c"][0]), columns(a["c_ctx"])], axis=2).reshape(P, 16))
    for l in range(DEPTH):
        put("b_ada", twice(columns(a["b_ada"][l])), 96 * l)
        put("g1", twice(columns(a["norm1_g"][l])), 16 * l)
        put("g2", twice(columns(a["norm2_g"][l])), 16 * l)
        put("qg", np.concatenate([a["q_norm_g"][l]] * 2)[:, None], l)
        put("kg", np.concatenate([a["k_norm_g"][l]] * 2)[:, None], l)
        put("sink", every(a["sink_a"][l]), 8 * l)
    put("gf", columns(a["final_norm_g"]))
    put("ng2", columns(a["norm_gain_2"]))
    put("qg2", np.concatenate([a["q_norm_gain_2"]] * 2)[:, None])
    put("kg2", np.concatenate([a["k_norm_gain_2"]] * 2, axis=1).T)
    put("pe", a["cmp_pe_2"].reshape(2, 16, P).transpose(2, 0, 1).reshape(P, 32))
    put("convw", a["conv_w_2"].reshape(4, 4, P).transpose(2, 1, 0).reshape(P, 16))
    put("convb", columns(a["conv_b_2"]))
    put("ba", columns(a["lru_ba_2"]))
    put("bx", columns(a["lru_bx_2"]))
    put("lam", columns(a["lru_lambda_2"]))
    return t


def bucket(n):
    if n < 16:
        return n
    f = np.float32
    return min(16 + int(np.log(f(n) / f(16)) / f(np.log(8.0)) * f(16)), 31)


def constants(a):
    t = np.zeros((P, B_ALL), np.float32)
    tok = np.arange(SEQ)
    pos = np.stack([tok // 64, tok % 64]).astype(np.float32)
    inv = (np.float32(10000.0) ** (-np.arange(0, 32, 2, dtype=np.float32) / np.float32(32))).astype(np.float32)
    for p in range(P):
        d = p % 64
        ang = pos[d // 32] * inv[d % 16]
        t[p, 0:SEQ] = np.cos(ang)
        t[p, SEQ:2 * SEQ] = np.sin(ang) * (-1 if d % 32 < 16 else 1)
    q, k = np.arange(P)[:, None], np.arange(P)[None, :]
    t[:, 2 * SEQ:2 * SEQ + P] = np.where(k < q, NEG, 0)
    t[:, 2 * SEQ + 2 * P:2 * SEQ + 3 * P] = np.where(k > q, NEG, 0)
    t[0:32, B_REL:B_REL + 8 * P] = np.repeat(a["rel_bias_2"], P, axis=1)
    t[32, B_REL:B_REL + 8 * P] = NEG
    for n in range(RV_LEN):
        t[bucket(SEQ - 1 - n) if n < SEQ else 32, B_HOT + n] = 1
    w2 = t[:, B_W2:B_W2 + 8 * P].reshape(P, 2, 2, 2, P)
    for g in range(2):
        w2[:, :, :, g, 64 * g:64 * g + 64] = a["cmp_w2_2"].reshape(2, 2, P, HD).transpose(2, 0, 1, 3)
    t[:, B_W2:B_W2 + 8 * P] = w2.reshape(P, -1)
    t[:, B_B1:] = every(a["cmp_b1_2"])
    return t


def pack(a):
    x = np.concatenate([a["x"][0], a["ctx"][0]], axis=0)
    return {
        "stream": np.stack([u for l in range(DEPTH) for u in layer_units(a, l)] + list(second_units(a))),
        "ada": a["w_ada"].reshape(DEPTH, CH, P, 12, 512).transpose(0, 3, 2, 1, 4).reshape(DEPTH * 12, P, 4 * UNIT),
        "x": np.ascontiguousarray(x.T.reshape(CH, P, TOK).transpose(1, 0, 2)),
        "cst": table(a),
        "big": constants(a),
    }


def kernel(**inputs):
    import concourse.bacc as bacc
    from concourse.bass_utils import run_bass_kernel_spmd

    nc = bacc.Bacc("TRN2", target_bir_lowering=False, num_devices=1)
    packed = pack({name: np.asarray(v) for name, v in inputs.items()})
    arrays, ins = {}, {}
    for name, v in packed.items():
        v = np.ascontiguousarray(v)
        arrays["in_" + name] = v
        ins[name] = nc.dram_tensor("in_" + name, v.shape, mybir.dt.from_np(v.dtype), kind="ExternalInput").ap()
    out = nc.dram_tensor("out_0", (P, CH, SEQ), F32, kind="ExternalOutput").ap()
    build_program(nc, ins, out)
    result = run_bass_kernel_spmd(nc, [arrays], core_ids=[0])
    got = result.results[0]["out_0"]
    return np.ascontiguousarray(got.transpose(2, 1, 0).reshape(1, SEQ, D))
```
